# Optimizing a Trainium2 kernel written in Bass

```python
import jax
import jax.numpy as jnp
from jax import lax
import numpy as np
import jax, jax.numpy as jnp

D_MODEL = 1024
BATCH = 1
SEQ = 512
DEPTH = 2

N_GROUPS = 4
GROUP = D_MODEL // N_GROUPS
CHUNK = 64

HGRN_HEADS = 4
GLA_HEADS = 4
GLA_KEY = GROUP // (2 * GLA_HEADS)
GLA_GATE_RANK = 16
GLA_GATE_NORM = 16.0
RWKV_HEADS = 4
RWKV_HEAD = GROUP // RWKV_HEADS
RWKV_DECAY_RANK = 64
RWKV_A_RANK = 64
RWKV_V_RANK = 32
RWKV_GATE_RANK = 160
RWKV_LNX_EPS = 64e-5
RET_HEADS = 4
RET_KEY = GROUP // RET_HEADS
ROPE_BASE = 10000.0

HGRN_COLS = (GROUP, GROUP, GROUP, GROUP)
GLA_COLS = (GLA_HEADS * GLA_KEY, GLA_HEADS * GLA_KEY, GROUP, GLA_GATE_RANK, GROUP)
RWKV_COLS = (GROUP, GROUP, GROUP, RWKV_DECAY_RANK, RWKV_A_RANK, RWKV_GATE_RANK)
RET_COLS = (GROUP, GROUP, GROUP, GROUP)
MIXER_COLS = (sum(HGRN_COLS), sum(GLA_COLS), sum(RWKV_COLS), sum(RET_COLS))
IN_COLS = sum(MIXER_COLS)

FFN_DENSE = 2816
N_EXPERTS = 8
TOP_K = 2
FFN_EXPERT = 1408
N_DENSE = (DEPTH + 1) // 2
N_MOE = DEPTH // 2

DN_ALPHA = (2.0 * DEPTH) ** 0.25
DN_BETA = (8.0 * DEPTH) ** -0.25
LN_EPS = 1e-5
F32 = jnp.float32


def _split(p, sizes):
    return jnp.split(p, np.cumsum(sizes)[:-1].tolist(), axis=-1)

def _heads(t, n):
    return t.reshape(t.shape[:-1] + (n, t.shape[-1] // n))

def _merge(t):
    return t.reshape(t.shape[:-2] + (t.shape[-2] * t.shape[-1],))

def _layer_norm(x, g, b):
    x = x.astype(F32)
    mu = jnp.mean(x, -1, keepdims=True)
    var = jnp.mean(jnp.square(x - mu), -1, keepdims=True)
    return (x - mu) * lax.rsqrt(var + LN_EPS) * g + b

def _rms_norm(x, g, eps=1e-6):
    return x * lax.rsqrt(jnp.mean(jnp.square(x), -1, keepdims=True) + eps) * g

def _group_norm(x, eps):
    mu = jnp.mean(x, -1, keepdims=True)
    var = jnp.mean(jnp.square(x - mu), -1, keepdims=True)
    return (x - mu) * lax.rsqrt(var + eps)

def _to_chunks(t):
    b, s, h, d = t.shape
    return t.reshape(b, s // CHUNK, CHUNK, h, d).transpose(1, 0, 3, 2, 4)

def _from_chunks(t):
    n, b, h, c, d = t.shape
    return t.transpose(1, 0, 3, 2, 4).reshape(b, n * c, h, d)

def _chunked_gated_linear(q, k, v, log_f):
    b, _, h, kd = q.shape
    vd = v.shape[-1]
    qc, kc, vc, gc = (_to_chunks(t.astype(F32)) for t in (q, k, v, log_f))
    causal = jnp.tril(jnp.ones((CHUNK, CHUNK), dtype=bool))

    def step(state, inp):
        qi, ki, vi, gi = inp
        cum = jnp.cumsum(gi, axis=2)
        diff = cum[:, :, :, None, :] - cum[:, :, None, :, :]
        decay = jnp.exp(jnp.where(causal[:, :, None], diff, -jnp.inf))
        scores = jnp.einsum('bhik,bhjk,bhijk->bhij', qi, ki, decay)
        out = (jnp.einsum('bhij,bhjv->bhiv', scores, vi)
               + jnp.einsum('bhik,bhkv->bhiv', qi * jnp.exp(cum), state))
        cum_end = cum[:, :, -1:, :]
        state = (jnp.exp(cum_end[:, :, 0, :])[..., None] * state
                 + jnp.einsum('bhjk,bhjv->bhkv', ki * jnp.exp(cum_end - cum), vi))
        return state, out

    _, o = lax.scan(step, jnp.zeros((b, h, kd, vd), F32), (qc, kc, vc, gc))
    return _from_chunks(o)

def _retention_chunkwise(q, k, v, log_gamma):
    b, _, h, kd = q.shape
    vd = v.shape[-1]
    qc, kc, vc = (_to_chunks(t.astype(F32)) for t in (q, k, v))
    idx = jnp.arange(CHUNK, dtype=F32)
    rel = idx[:, None] - idx[None, :]
    intra = jnp.exp(jnp.where(rel >= 0, rel * log_gamma[:, None, None], -jnp.inf))
    q_dec = jnp.exp((idx + 1.0)[None, :] * log_gamma[:, None])
    k_dec = jnp.exp((CHUNK - 1.0 - idx)[None, :] * log_gamma[:, None])
    c_dec = jnp.exp(CHUNK * log_gamma)

    def step(state, inp):
        qi, ki, vi = inp
        scores = jnp.einsum('bhik,bhjk->bhij', qi, ki) * intra
        out = (jnp.einsum('bhij,bhjv->bhiv', scores, vi)
               + jnp.einsum('bhik,bhkv->bhiv', qi * q_dec[..., None], state))
        state = (c_dec[:, None, None] * state
                 + jnp.einsum('bhjk,bhjv->bhkv', ki * k_dec[..., None], vi))
        return state, out

    _, o = lax.scan(step, jnp.zeros((b, h, kd, vd), F32), (qc, kc, vc))
    return _from_chunks(o)

def _rotary(t, positions):
    half = t.shape[-1] // 2
    inv_freq = ROPE_BASE ** (-jnp.arange(half, dtype=F32) / half)
    ang = positions.astype(F32)[:, :, None, None] * inv_freq
    cos, sin = jnp.cos(ang), jnp.sin(ang)
    t1, t2 = t[..., :half], t[..., half:]
    return jnp.concatenate([t1 * cos - t2 * sin, t1 * sin + t2 * cos], axis=-1)

def _rwkv7_scan(r, w, k, v, kk, a):
    b, _, h, n = r.shape
    xs = tuple(jnp.moveaxis(t, 1, 0) for t in (r, w, k, v, kk, a))

    def step(state, inp):
        rt, wt, kt, vt, kkt, at = inp
        sa = jnp.einsum('bhvk,bhk->bhv', state, -kkt)
        state = (state * wt[:, :, None, :]
                 + sa[..., None] * (kkt * at)[:, :, None, :]
                 + vt[..., None] * kt[:, :, None, :])
        return state, jnp.einsum('bhvk,bhk->bhv', state, rt)

    _, o = lax.scan(step, jnp.zeros((b, h, n, n), F32), xs)
    return jnp.moveaxis(o, 0, 1)

def _hgrn2_mixer(p, lb, norm_g):
    q_raw, f_raw, i_raw, g_raw = _split(p, HGRN_COLS)
    f = lb + (1.0 - lb) * jax.nn.sigmoid(f_raw)
    hd = lambda t: _heads(t, HGRN_HEADS)
    o = _chunked_gated_linear(hd(jax.nn.silu(q_raw)), hd(1.0 - f), hd(i_raw), hd(jnp.log(f)))
    o = _rms_norm(o, norm_g) * jax.nn.silu(hd(g_raw))
    return _merge(o)

def _gla_mixer(p, gate_w2, gate_b, norm_g):
    q, k, v, g_lr, r = _split(p, GLA_COLS)
    log_f = jax.nn.log_sigmoid(g_lr @ gate_w2 + gate_b) / GLA_GATE_NORM
    hd = lambda t: _heads(t, GLA_HEADS)
    o = _chunked_gated_linear(hd(q) * GLA_KEY ** -0.5, hd(k), hd(v), hd(log_f))
    o = _rms_norm(o, norm_g) * jax.nn.silu(hd(r))
    return _merge(o)

def _rwkv7_mixer(p, v_first, v_mix, mu, w0, w2, a0, a2, g2, k_k, k_a, r_k, lnx_g, lnx_b):
    p_prev = jnp.pad(p, ((0, 0), (1, 0), (0, 0)))[:, :-1]
    p = p + (p_prev - p) * mu
    r, k, v, w_lr, a_lr, g_lr = _split(p, RWKV_COLS)
    w = -jax.nn.softplus(-(w0 + jnp.tanh(w_lr) @ w2)) - 0.5
    decay = jnp.exp(-jnp.exp(w))
    a = jax.nn.sigmoid(a0 + a_lr @ a2)
    g = jax.nn.sigmoid(g_lr) @ g2
    if v_mix is None:
        v_first = v
    else:
        v0, v1, v2 = v_mix
        v = v + (v_first - v) * jax.nn.sigmoid(v0 + (v @ v1) @ v2)
    hd = lambda t: _heads(t, RWKV_HEADS)
    kk = hd(k * k_k)
    kk = kk / jnp.maximum(jnp.sqrt(jnp.sum(jnp.square(kk), -1, keepdims=True)), 1e-12)
    k = k * (1.0 + (a - 1.0) * k_a)
    rh, kh, vh = hd(r), hd(k), hd(v)
    o = _rwkv7_scan(rh, hd(decay), kh, vh, kk, hd(a))
    o = _group_norm(o, RWKV_LNX_EPS) * hd(lnx_g) + hd(lnx_b)
    o = o + jnp.sum(rh * kh * r_k, -1, keepdims=True) * vh
    return _merge(o) * g, v_first

def _retnet_mixer(p, positions, log_gamma):
    q, k, v, g = _split(p, RET_COLS)
    hd = lambda t: _heads(t, RET_HEADS)
    qh = _rotary(hd(q), positions)
    kh = _rotary(hd(k), positions) * RET_KEY ** -0.5
    o = _group_norm(_retention_chunkwise(qh, kh, hd(v), log_gamma), LN_EPS)
    return jax.nn.silu(g) * _merge(o)

def _swiglu(h, wg, wu, wd):
    return (jax.nn.silu(h @ wg) * (h @ wu)) @ wd

def _moe(h, router, wg, wu, wd):
    b, s, d = h.shape
    hf = h.reshape(b * s, d)
    probs = jax.nn.softmax((hf @ router).astype(F32), axis=-1)
    top_p, top_i = lax.top_k(probs, TOP_K)
    top_p = top_p / jnp.sum(top_p, -1, keepdims=True)
    gates = jnp.sum(jax.nn.one_hot(top_i, N_EXPERTS, dtype=F32) * top_p[..., None], axis=1)
    out = jnp.zeros_like(hf)
    for e in range(N_EXPERTS):
        out = out + gates[:, e:e + 1] * _swiglu(hf, wg[e], wu[e], wd[e])
    return out.reshape(b, s, d)

def first_inputs(seed: int = 0) -> dict:
    key = jax.random.key(seed)
    ks = iter(jax.random.split(key, 48))

    def nrm(shape, scale):
        return scale * jax.random.normal(next(ks), shape, F32)

    D = D_MODEL
    decay_base = -6.0 + 5.0 * (jnp.arange(GROUP, dtype=F32) / (GROUP - 1)) ** 0.9
    return {
        'x': nrm((BATCH, SEQ, D), 1.0),
        'positions': jnp.broadcast_to(jnp.arange(SEQ, dtype=jnp.int32)[None, :], (BATCH, SEQ)),
        'w_in': nrm((DEPTH, D, IN_COLS), D ** -0.5),
        'w_out': nrm((DEPTH, D, D), DN_BETA * D ** -0.5),
        'ln1_g': 1.0 + nrm((DEPTH, D), 0.01),
        'ln1_b': nrm((DEPTH, D), 0.01),
        'ln2_g': 1.0 + nrm((DEPTH, D), 0.01),
        'ln2_b': nrm((DEPTH, D), 0.01),
        'hgrn_lb_logits': nrm((DEPTH, GROUP), 0.5),
        'hgrn_norm_g': 1.0 + nrm((DEPTH, GROUP // HGRN_HEADS), 0.01),
        'gla_gate_w2': nrm((DEPTH, GLA_GATE_RANK, GLA_HEADS * GLA_KEY), GLA_GATE_RANK ** -0.5),
        'gla_gate_b': nrm((DEPTH, GLA_HEADS * GLA_KEY), 0.1),
        'gla_norm_g': 1.0 + nrm((DEPTH, GROUP // GLA_HEADS), 0.01),
        'rwkv_mu': jax.random.uniform(next(ks), (DEPTH, sum(RWKV_COLS)), F32),
        'rwkv_w0': decay_base[None, :] + nrm((DEPTH, GROUP), 0.1),
        'rwkv_w2': nrm((DEPTH, RWKV_DECAY_RANK, GROUP), 0.5 * RWKV_DECAY_RANK ** -0.5),
        'rwkv_a0': nrm((DEPTH, GROUP), 0.1),
        'rwkv_a2': nrm((DEPTH, RWKV_A_RANK, GROUP), 0.5 * RWKV_A_RANK ** -0.5),
        'rwkv_g2': nrm((DEPTH, RWKV_GATE_RANK, GROUP), RWKV_GATE_RANK ** -0.5),
        'rwkv_k_k': 0.85 + nrm((DEPTH, GROUP), 0.02),
        'rwkv_k_a': 1.0 + nrm((DEPTH, GROUP), 0.02),
        'rwkv_r_k': -0.04 + nrm((DEPTH, RWKV_HEADS, RWKV_HEAD), 0.02),
        'rwkv_lnx_g': 1.0 + nrm((DEPTH, GROUP), 0.01),
        'rwkv_lnx_b': nrm((DEPTH, GROUP), 0.01),
        'rwkv_v0': 1.0 + nrm((DEPTH - 1, GROUP), 0.1),
        'rwkv_v1': nrm((DEPTH - 1, GROUP, RWKV_V_RANK), GROUP ** -0.5),
        'rwkv_v2': nrm((DEPTH - 1, RWKV_V_RANK, GROUP), 0.5 * RWKV_V_RANK ** -0.5),
        'ffn_w_gate': nrm((N_DENSE, D, FFN_DENSE), D ** -0.5),
        'ffn_w_up': nrm((N_DENSE, D, FFN_DENSE), D ** -0.5),
        'ffn_w_down': nrm((N_DENSE, FFN_DENSE, D), DN_BETA * FFN_DENSE ** -0.5),
        'moe_router': nrm((N_MOE, D, N_EXPERTS), D ** -0.5),
        'moe_w_gate': nrm((N_MOE, N_EXPERTS, D, FFN_EXPERT), D ** -0.5),
        'moe_w_up': nrm((N_MOE, N_EXPERTS, D, FFN_EXPERT), D ** -0.5),
        'moe_w_down': nrm((N_MOE, N_EXPERTS, FFN_EXPERT, D), DN_BETA * FFN_EXPERT ** -0.5),
    }

def first_block(x, positions, w_in, w_out, ln1_g, ln1_b, ln2_g, ln2_b, hgrn_lb_logits, hgrn_norm_g,
              gla_gate_w2, gla_gate_b, gla_norm_g, rwkv_mu, rwkv_w0, rwkv_w2, rwkv_a0, rwkv_a2,
              rwkv_g2, rwkv_k_k, rwkv_k_a, rwkv_r_k, rwkv_lnx_g, rwkv_lnx_b, rwkv_v0, rwkv_v1,
              rwkv_v2, ffn_w_gate, ffn_w_up, ffn_w_down, moe_router, moe_w_gate, moe_w_up,
              moe_w_down):
    out_dtype = x.dtype
    h = x.astype(F32)
    lb_all = jnp.cumsum(jax.nn.softmax(hgrn_lb_logits.astype(F32), axis=0), axis=0)
    lb_all = lb_all - lb_all[:1]
    log_gamma = jnp.log(1.0 - 2.0 ** (-5.0 - jnp.arange(RET_HEADS, dtype=F32)))
    v_first = None
    for l in range(DEPTH):
        p = jnp.einsum('btd,dc->btc', h, w_in[l]).astype(F32)
        pa, pb, pc, pd = _split(p, MIXER_COLS)
        ya = _hgrn2_mixer(pa, lb_all[l], hgrn_norm_g[l])
        yb = _gla_mixer(pb, gla_gate_w2[l], gla_gate_b[l], gla_norm_g[l])
        v_mix = None if l == 0 else (rwkv_v0[l - 1], rwkv_v1[l - 1], rwkv_v2[l - 1])
        yc, v_first = _rwkv7_mixer(pc, v_first, v_mix, rwkv_mu[l], rwkv_w0[l], rwkv_w2[l],
                                   rwkv_a0[l], rwkv_a2[l], rwkv_g2[l], rwkv_k_k[l], rwkv_k_a[l],
                                   rwkv_r_k[l], rwkv_lnx_g[l], rwkv_lnx_b[l])
        yd = _retnet_mixer(pd, positions, log_gamma)
        mix = jnp.einsum('btc,cd->btd', jnp.concatenate([ya, yb, yc, yd], axis=-1), w_out[l])
        h = _layer_norm(DN_ALPHA * h + mix, ln1_g[l], ln1_b[l])
        if l % 2 == 0:
            i = l // 2
            f = _swiglu(h, ffn_w_gate[i], ffn_w_up[i], ffn_w_down[i])
        else:
            i = l // 2
            f = _moe(h, moe_router[i], moe_w_gate[i], moe_w_up[i], moe_w_down[i])
        h = _layer_norm(DN_ALPHA * h + f, ln2_g[l], ln2_b[l])
    return h.astype(out_dtype)


DEPTH_2 = 1

D_MIX = D_MODEL
D_LRU = D_MIX // 2
LRU_BLOCKS = 8
LRU_BLOCK = D_LRU // LRU_BLOCKS
CONV_WIDTH = 4
LRU_C = 8.0
N_HEADS = 8
N_KV_HEADS = 2
GQA_GROUP = N_HEADS // N_KV_HEADS
HEAD_DIM = (D_MIX - D_LRU) // N_HEADS
D_ATTN = N_HEADS * HEAD_DIM
WINDOW = 128
BLOCK_Q = 128
D_FF = 2816
RMS_EPS = 1e-6
D_IN = 2 * D_LRU + (N_HEADS + 2 * N_KV_HEADS) * HEAD_DIM
MASK_VALUE = -1e30


def rms_norm(x, g):
    xf = x.astype(jnp.float32)
    y = xf * lax.rsqrt(jnp.mean(xf * xf, axis=-1, keepdims=True) + RMS_EPS)
    return (y * g.astype(jnp.float32)).astype(x.dtype)

def swiglu(x, w_gu, w_down):
    gate, up = jnp.split(x @ w_gu, 2, axis=-1)
    return (jax.nn.silu(gate) * up) @ w_down

def causal_depthwise_conv(x, w, b):
    c = x.shape[-1]
    rhs = w.astype(x.dtype)[:, None, :]
    y = lax.conv_general_dilated(x, rhs, window_strides=(1,), padding=[(CONV_WIDTH - 1, 0)],
                                 dimension_numbers=("NWC", "WIO", "NWC"), feature_group_count=c)
    return y + b.astype(x.dtype)

def block_diag(x, w, b):
    bsz, s, _ = x.shape
    xh = x.reshape(bsz, s, LRU_BLOCKS, LRU_BLOCK)
    y = jnp.einsum("bshi,hij->bshj", xh, w).reshape(bsz, s, D_LRU)
    return y + b

def rg_lru(x_in, conv_w, conv_b, w_rg, b_rg, w_ig, b_ig, lam):
    xc = causal_depthwise_conv(x_in, conv_w, conv_b)
    r = jax.nn.sigmoid(block_diag(xc, w_rg, b_rg).astype(jnp.float32))
    i = jax.nn.sigmoid(block_diag(xc, w_ig, b_ig).astype(jnp.float32))
    log_a = LRU_C * r * jax.nn.log_sigmoid(lam.astype(jnp.float32))
    a = jnp.exp(log_a)
    mult = jnp.sqrt(-jnp.expm1(2.0 * log_a))
    u = mult * (i * xc.astype(jnp.float32))

    def combine(left, right):
        a_l, u_l = left
        a_r, u_r = right
        return a_l * a_r, a_r * u_l + u_r

    _, h = lax.associative_scan(combine, (a, u), axis=1)
    return h.astype(x_in.dtype)

def sliding_window_sink_attention(q, k, v, sinks):
    bsz, s = q.shape[0], q.shape[1]
    nb = s // BLOCK_Q
    qb = q.reshape(bsz, nb, BLOCK_Q, N_KV_HEADS, GQA_GROUP, HEAD_DIM)
    kb = k.reshape(bsz, nb, BLOCK_Q, N_KV_HEADS, HEAD_DIM)
    vb = v.reshape(bsz, nb, BLOCK_Q, N_KV_HEADS, HEAD_DIM)
    k_band = jnp.concatenate([jnp.concatenate([jnp.zeros_like(kb[:, :1]), kb[:, :-1]], axis=1), kb], axis=2)
    v_band = jnp.concatenate([jnp.concatenate([jnp.zeros_like(vb[:, :1]), vb[:, :-1]], axis=1), vb], axis=2)
    scale = HEAD_DIM ** -0.5
    scores = jnp.einsum("bnqkgd,bnjkd->bnkgqj", qb, k_band).astype(jnp.float32) * scale
    qi = jnp.arange(BLOCK_Q)[:, None]
    kj = jnp.arange(2 * BLOCK_Q)[None, :]
    rel = qi + BLOCK_Q - kj
    band = (rel >= 0) & (rel < WINDOW)
    blk = jnp.arange(nb)[:, None, None]
    mask = band[None] & ((blk > 0) | (kj >= BLOCK_Q)[None])
    scores = jnp.where(mask[None, :, None, None], scores, MASK_VALUE)
    sink = sinks.astype(jnp.float32).reshape(1, 1, N_KV_HEADS, GQA_GROUP, 1, 1)
    m = jnp.maximum(jnp.max(scores, axis=-1, keepdims=True), sink)
    p = jnp.exp(scores - m)
    denom = jnp.sum(p, axis=-1, keepdims=True) + jnp.exp(sink - m)
    p = (p / denom).astype(v.dtype)
    out = jnp.einsum("bnkgqj,bnjkd->bnqkgd", p, v_band)
    return out.reshape(bsz, s, D_ATTN)

def hybrid_mixer(h, w_in, conv_w, conv_b, w_rg, b_rg, w_ig, b_ig, lam, sinks, g_lru_out, g_attn_out, w_o):
    bsz, s, _ = h.shape
    proj = h @ w_in
    o1 = D_LRU
    o2 = o1 + D_LRU
    o3 = o2 + D_ATTN
    o4 = o3 + N_KV_HEADS * HEAD_DIM
    x_lru = proj[..., :o1]
    gate_lru = proj[..., o1:o2]
    q = proj[..., o2:o3].reshape(bsz, s, N_HEADS, HEAD_DIM)
    k = proj[..., o3:o4].reshape(bsz, s, N_KV_HEADS, HEAD_DIM)
    v = proj[..., o4:].reshape(bsz, s, N_KV_HEADS, HEAD_DIM)
    y_lru = rg_lru(x_lru, conv_w, conv_b, w_rg, b_rg, w_ig, b_ig, lam) * jax.nn.gelu(gate_lru)
    y_attn = sliding_window_sink_attention(q, k, v, sinks)
    y = jnp.concatenate([rms_norm(y_lru, g_lru_out), rms_norm(y_attn, g_attn_out)], axis=-1)
    return y @ w_o

def second_inputs(seed: int = 0) -> dict:
    key = jax.random.key(seed)
    ks = jax.random.split(key, 32)
    f32 = jnp.float32

    def nrm(k, shape, scale):
        return jax.random.normal(k, shape, f32) * scale

    def gain(k, n):
        return 1.0 + 0.05 * jax.random.normal(k, (DEPTH_2, n), f32)

    u = jax.random.uniform(ks[13], (DEPTH_2, D_LRU), f32, 0.9, 0.999)
    return {
        "x": jax.random.normal(ks[0], (BATCH, SEQ, D_MODEL), f32),
        "ffn1_pre_g": gain(ks[1], D_MODEL),
        "ffn1_w_gu": nrm(ks[2], (DEPTH_2, D_MODEL, 2 * D_FF), D_MODEL ** -0.5),
        "ffn1_w_down": nrm(ks[3], (DEPTH_2, D_FF, D_MODEL), D_FF ** -0.5),
        "ffn1_post_g": gain(ks[4], D_MODEL),
        "mix_pre_g": gain(ks[5], D_MODEL),
        "w_in": nrm(ks[6], (DEPTH_2, D_MODEL, D_IN), D_MODEL ** -0.5),
        "conv_w": nrm(ks[7], (DEPTH_2, CONV_WIDTH, D_LRU), CONV_WIDTH ** -0.5),
        "conv_b": nrm(ks[8], (DEPTH_2, D_LRU), 0.01),
        "w_rg": nrm(ks[9], (DEPTH_2, LRU_BLOCKS, LRU_BLOCK, LRU_BLOCK), LRU_BLOCK ** -0.5),
        "b_rg": nrm(ks[10], (DEPTH_2, D_LRU), 0.01),
        "w_ig": nrm(ks[11], (DEPTH_2, LRU_BLOCKS, LRU_BLOCK, LRU_BLOCK), LRU_BLOCK ** -0.5),
        "b_ig": nrm(ks[12], (DEPTH_2, D_LRU), 0.01),
        "lru_lambda": jnp.log(u) - jnp.log1p(-u),
        "sinks": nrm(ks[14], (DEPTH_2, N_HEADS), 1.0),
        "g_lru_out": gain(ks[15], D_LRU),
        "g_attn_out": gain(ks[16], D_ATTN),
        "w_o": nrm(ks[17], (DEPTH_2, D_MIX, D_MODEL), D_MIX ** -0.5),
        "mix_post_g": gain(ks[18], D_MODEL),
        "ffn2_pre_g": gain(ks[19], D_MODEL),
        "ffn2_w_gu": nrm(ks[20], (DEPTH_2, D_MODEL, 2 * D_FF), D_MODEL ** -0.5),
        "ffn2_w_down": nrm(ks[21], (DEPTH_2, D_FF, D_MODEL), D_FF ** -0.5),
        "ffn2_post_g": gain(ks[22], D_MODEL),
    }

def second_block(x, ffn1_pre_g, ffn1_w_gu, ffn1_w_down, ffn1_post_g, mix_pre_g, w_in, conv_w, conv_b,
              w_rg, b_rg, w_ig, b_ig, lru_lambda, sinks, g_lru_out, g_attn_out, w_o, mix_post_g,
              ffn2_pre_g, ffn2_w_gu, ffn2_w_down, ffn2_post_g):
    for l in range(DEPTH_2):
        x = x + 0.5 * rms_norm(swiglu(rms_norm(x, ffn1_pre_g[l]), ffn1_w_gu[l], ffn1_w_down[l]), ffn1_post_g[l])
        y = hybrid_mixer(rms_norm(x, mix_pre_g[l]), w_in[l], conv_w[l], conv_b[l], w_rg[l], b_rg[l],
                         w_ig[l], b_ig[l], lru_lambda[l], sinks[l], g_lru_out[l], g_attn_out[l], w_o[l])
        x = x + rms_norm(y, mix_post_g[l])
        x = x + 0.5 * rms_norm(swiglu(rms_norm(x, ffn2_pre_g[l]), ffn2_w_gu[l], ffn2_w_down[l]), ffn2_post_g[l])
    return x


def setup_inputs(seed=0):
    out = dict(first_inputs(seed))
    for name, value in second_inputs(seed + 1).items():
        if name != "x":
            out[name + "_2"] = value
    return out


def reference(
    x, positions, w_in, w_out, ln1_g, ln1_b, ln2_g, ln2_b, hgrn_lb_logits, hgrn_norm_g,
    gla_gate_w2, gla_gate_b, gla_norm_g, rwkv_mu, rwkv_w0, rwkv_w2, rwkv_a0, rwkv_a2, rwkv_g2,
    rwkv_k_k, rwkv_k_a, rwkv_r_k, rwkv_lnx_g, rwkv_lnx_b, rwkv_v0, rwkv_v1, rwkv_v2, ffn_w_gate,
    ffn_w_up, ffn_w_down, moe_router, moe_w_gate, moe_w_up, moe_w_down, ffn1_pre_g_2,
    ffn1_w_gu_2, ffn1_w_down_2, ffn1_post_g_2, mix_pre_g_2, w_in_2, conv_w_2, conv_b_2, w_rg_2,
    b_rg_2, w_ig_2, b_ig_2, lru_lambda_2, sinks_2, g_lru_out_2, g_attn_out_2, w_o_2,
    mix_post_g_2, ffn2_pre_g_2, ffn2_w_gu_2, ffn2_w_down_2, ffn2_post_g_2,
):
    x = first_block(
        x, positions, w_in, w_out, ln1_g, ln1_b, ln2_g, ln2_b, hgrn_lb_logits, hgrn_norm_g,
        gla_gate_w2, gla_gate_b, gla_norm_g, rwkv_mu, rwkv_w0, rwkv_w2, rwkv_a0, rwkv_a2,
        rwkv_g2, rwkv_k_k, rwkv_k_a, rwkv_r_k, rwkv_lnx_g, rwkv_lnx_b, rwkv_v0, rwkv_v1,
        rwkv_v2, ffn_w_gate, ffn_w_up, ffn_w_down, moe_router, moe_w_gate, moe_w_up, moe_w_down,
    )
    return second_block(
        x, ffn1_pre_g_2, ffn1_w_gu_2, ffn1_w_down_2, ffn1_post_g_2, mix_pre_g_2, w_in_2,
        conv_w_2, conv_b_2, w_rg_2, b_rg_2, w_ig_2, b_ig_2, lru_lambda_2, sinks_2, g_lru_out_2,
        g_attn_out_2, w_o_2, mix_post_g_2, ffn2_pre_g_2, ffn2_w_gu_2, ffn2_w_down_2,
        ffn2_post_g_2,
    )


_drawn_inputs = setup_inputs


def setup_inputs(seed=0):
    import zlib

    import numpy as np

    out = dict(_drawn_inputs(seed))
    spreads = {}
    factors = {'hgrn_lb_logits': 2.89,
     'hgrn_norm_g': 21.505,
     'gla_gate_b': 3.937,
     'gla_norm_g': 18.705,
     'rwkv_w2': 3.565,
     'rwkv_a0': 3.14,
     'rwkv_k_k': 8.0,
     'rwkv_k_a': 5.276,
     'rwkv_r_k': 4.347,
     'rwkv_lnx_g': 28.781,
     'rwkv_lnx_b': 8.0,
     'rwkv_v0': 61.192,
     'conv_b_2': 2.984,
     'b_rg_2': 40.306,
     'b_ig_2': 22.272,
     'sinks_2': 4.179,
     'ffn2_post_g_2': 3.734,
     'rwkv_v1': 8.0,
     'rwkv_v2': 8.0}
    for name, (base, spread) in spreads.items():
        noise = np.random.default_rng([zlib.crc32(name.encode()), seed]).standard_normal(out[name].shape)
        drawn = base * np.exp(spread * noise) if base else spread * noise
        out[name] = jnp.asarray(drawn.astype(out[name].dtype))
    for name, factor in factors.items():
        out[name] = (out[name] * factor).astype(out[name].dtype)
    return out
```

```python
import numpy as np
import concourse.bass as bass
from concourse import mybir

F32 = mybir.dt.float32
I32 = mybir.dt.int32
U32 = mybir.dt.uint32
ACT = mybir.ActivationFunctionType
ALU = mybir.AluOpType
AX = mybir.AxisListType

P = 128
SEQ = 512
D = 1024
TT = SEQ // P
DT = D // P
HALF = 512
GROUP = 256
NHEAD = 4
HD = 64
LEVELS = 7
FU = 11
FPASS = FU * P
N_EXPERTS = 8
ALPHA = 4.0 ** 0.25
LN_EPS = 1e-5
RMS_EPS = 1e-6
LNX_EPS = 64e-5
EXP_NEG_HALF = float(np.exp(-0.5))

IN_COLS = 3888
HQ, HF, GQ, GK, GLR, RR, RK, RV, RWA, RG, RQ, RKK = 0, 2, 4, 5, 6, 7, 9, 11, 13, 14, 16, 18
two_tiles = lambda tile: [("F", tile, 0, 128), ("F", tile + 1, 128, 128)]
IN_PIECES = [[(0, 256)], [(256, 256)], [(512, 256)], [(768, 256)], [(1024, 256)], [(1280, 272)], [(1552, 256)],
             [(1808, 256)], [(2064, 256)], [(2320, 256)], [(2576, 288)], [(2864, 256)], [(3120, 256)], [(3376, 256)], [(3632, 256)]]
IN_UNITS = [two_tiles(HQ), two_tiles(HF), [("T", 0, 0, 256)], [("T", 256, 0, 256)], two_tiles(GQ),
            [("T", 512, 0, 256), ("F", GLR, 256, 16)], [("T", 768, 0, 256)], two_tiles(RR), two_tiles(RK), two_tiles(RV),
            two_tiles(RWA) + [("F", RG + 1, 256, 32)], two_tiles(RQ), two_tiles(RKK), [("T", 1024, 0, 256)], [("T", 1280, 0, 256)]]
PW = 288
PRAW, PSPL = 2, 3
NFT = 20
L2X, L2G, L2Q, L2K = 0, 4, 8, 12
IN2_PIECES = [[(256 * i, 256)] for i in range(6)] + [[(1536, 64), (1536, 64), (1600, 64), (1600, 64)], [(1664, 128)]]
IN2_UNITS = [two_tiles(2 * i) for i in range(7)] + [[("T", 0, 0, 128)]]
OUT_PIECES = [[(256 * i, 256)] for i in range(4)]
OUT_UNITS = [[("T", 256 * i, 0, 256)] for i in range(4)]
QH = 8
PRE1, PRE_MIX, PRE2, G_OUT, CONV_W, CONV_B, B_RG, B_IG, LAM = 0, 8, 16, 24, 32, 48, 52, 56, 60
TOKW = 1536

PAR = {}
for _name, _n in (("lb0", 2), ("lb1", 2), ("gate_b", 1), ("mu", 9), ("w0", 2), ("a0", 2), ("k_k", 2), ("k_a", 2), ("r_k", 2), ("v0", 2)):
    PAR[_name] = (sum(n for _, n in PAR.values()), _n)
NPAR = sum(n for _, n in PAR.values())

SCR = 39424
FT0 = 23040
TOK0 = FT0 + NFT * SEQ
HT0 = TOK0 + TT * TOKW
ARENA = 44672
WSP0 = 2 * DT * SEQ
assert TOK0 + TT * TOKW == SCR and WSP0 + PSPL * 2 * DT * PW <= FT0 - D and HT0 + PRAW * DT * PW <= ARENA
FRING = 3
XR0 = 0
HID0 = XR0 + 2 * DT * SEQ
GRAW0 = HID0 + 2 * FU * SEQ
GSPL0 = GRAW0 + FRING * 2 * D
DRAW0 = GSPL0 + FRING * 4 * D
DSPL0 = DRAW0 + FRING * HALF
TMP0 = DSPL0 + FRING * 2 * HALF
assert TMP0 + 2 * SEQ <= ARENA
F32R = mybir.dt.float32r
CAP = 160
NBLK = -(-SEQ // CAP)
HIDS0 = HID0
XE0 = HIDS0 + 2 * FU * CAP
PSEL0 = XE0 + 2 * DT * CAP
PT0 = PSEL0 + TT * CAP
SVW0 = PT0 + 2 * SEQ
SVN = NBLK * N_EXPERTS + 8
IOTA0 = SVW0 + TT * SVN
NBI0 = IOTA0 + CAP
SLOT_TMP = NBI0 + 8
assert SLOT_TMP + 336 <= GRAW0

CF = {}
for _name, _n in (("ident", 128), ("headcol", 8), ("invf", 1), ("iota8", 8), ("tail", 1)):
    CF[_name] = (sum(n for _, n in CF.values()), _n)
NCF = sum(n for _, n in CF.values())
LVT = 0
DIAG = LEVELS
LV = LEVELS + 1
INCL = 2 * LEVELS + 1
STRICT = INCL + 1
NCI = STRICT + 1
RET_D, RET_Q, RET_K, RET_C = 0, 512, 512 + 2 * P, 512 + 4 * P
NRET = RET_C + 2


class Signal:

    def __init__(self, nc, name):
        self.sem, self.base, self.sent = nc.alloc_semaphore(name), 0, 0

    def up(self, n=1, times=1):
        self.sent += n * times
        return self.sem, n

    def at(self, n):
        return self.sem, self.base + n


class Steps:

    def __init__(self, eng, count):
        self.eng, self.count = eng, count

    def __call__(self, ins):
        ins.then_inc(*self.count.up())

    def wait(self):
        self.eng.wait_ge(*self.count.at(self.count.sent))

    def link(self, ins):
        self(ins)
        self.wait()


class Kernel:
    def __init__(self, nc, ap):
        self.nc, self.ap, self.counts = nc, ap, {}
        base = (nc.sbuf_base + 31) // 32 * 32
        self.placed = 0

        def place(name, n, at=None, dt=F32):
            off = self.placed if at is None else at + self.arena_at
            if at is None:
                self.placed += (n + 7) // 8 * 8
            return nc.alloc_sbuf_tensor_at(name, [P, n], dt, offset=base + 4 * off)[:, :]

        self.H = place("h_tok", TT * D).rearrange("p (t d) -> p t d", d=D)
        self.B = place("keep", 4096)
        self.CF = place("const_sb", NCF)
        self.PAR = place("par_sb", 2 * NPAR + 12)
        self.SM = place("small", P)
        self.arena_at = self.placed
        self.A = place("arena", ARENA)
        self.HT = self.A[:, HT0:HT0 + DT * SEQ].rearrange("p (k t) -> p k t", t=SEQ)
        self.XR = place("x_split", 2 * DT * SEQ, XR0, F32R).rearrange("p (s k t) -> p s k t", s=2, t=SEQ)
        self.HID = place("hidden_split", 2 * FU * SEQ, HID0, F32R).rearrange("p (s f t) -> p s f t", s=2, t=SEQ)
        self.GSPL = place("gate_up_split", FRING * 4 * D, GSPL0, F32R).rearrange("p (r s u k f) -> p r s (u k f)", r=FRING, s=2, u=2, f=P)
        self.DSPL = place("down_split", FRING * 2 * HALF, DSPL0, F32R).rearrange("p (r s n) -> p r s n", r=FRING, s=2)
        self.WSPL = [place(f"w_split{r}", 2 * DT * PW, WSP0 + r * 2 * DT * PW, F32R).rearrange("p (s n) -> p s n", s=2) for r in range(PSPL)]
        self.HR = place("x_tok_split", 2 * TT * D, XR0, F32R).rearrange("p (s t d) -> p s t d", s=2, t=TT)
        self.HIDS = place("hidden_slots_split", 2 * FU * CAP, HIDS0, F32R).rearrange("p (s f t) -> p s f t", s=2, t=CAP)
        self.XE = place("x_slots_split", 2 * DT * CAP, XE0, F32R).rearrange("p (k s t) -> p k s t", s=2, t=CAP)
        self.PSEL = place("pick", TT * CAP, PSEL0, F32R).rearrange("p (t n) -> p t n", n=CAP)
        self.PT = place("scatter", 2 * SEQ, PT0, F32R).rearrange("p (j t) -> p j t", t=SEQ)
        self.YE = place("y_slots_split", 4 * D, TT * D - self.arena_at, F32R).rearrange("p (s j d) -> p s j d", s=2, j=2)
        self.SVW = self.A[:, SVW0:IOTA0].rearrange("p (t n) -> p t n", n=SVN)
        self.IOTA = self.A[:, IOTA0:NBI0]
        self.NBI = self.A[:, NBI0:NBI0 + 1].bitcast(I32)
        self.GRAW = self.A[:, GRAW0:GSPL0].rearrange("p (r n) -> p r n", r=FRING)
        self.DRAW = self.A[:, DRAW0:DSPL0].rearrange("p (r n) -> p r n", r=FRING)
        self.TMP = self.A[:, TMP0:TMP0 + 2 * SEQ].rearrange("p (r t) -> p r t", t=SEQ)
        self.PS = nc.alloc_psum_tensor("psum", [P, 8 * HALF], F32)
        self.MASK = self.B[:, 0:NCI * P].bitcast(I32)
        self.VF = self.B[:, NCI * P:NCI * P + 1024]
        self.SWAP = self.B[:, NCI * P + 1024:NCI * P + 1152]
        self.HSUM = self.B[:, NCI * P + 1152:NCI * P + 1280]
        self.GMASK = self.B[:, NCI * P + 1280:NCI * P + 1536]

    def sig(self, name):
        if name not in self.counts:
            self.counts[name] = Signal(self.nc, name)
        return self.counts[name]

    def close(self):
        for s in self.counts.values():
            s.base, s.sent = s.base + s.sent, 0

    def cf(self, name):
        a, n = CF[name]
        return self.CF[:, a:a + n]

    def par(self, l, name, i=0):
        a = PAR[name][0] + l * NPAR + i
        return self.PAR[:, a:a + 1]

    def bank(self, b, n=HALF):
        return self.PS[:, b * HALF:b * HALF + n]

    def stage_ffn(self, passes, gate_w, up_w, down_w):
        nc, H, XR, HID, TMP = self.nc, self.H, self.XR, self.HID, self.TMP
        GSPL, DSPL, GRAW, DRAW = self.GSPL, self.DSPL, self.GRAW, self.DRAW
        g_loaded = [self.sig(f"ffn_gate_up_loaded{r}") for r in range(FRING)]
        d_loaded = [self.sig(f"ffn_down_loaded{r}") for r in range(FRING)]
        g_hi, g_lo, d_hi, d_lo, g_mm, d_mm, silu_done, prod_done, hid_hi, hid_lo, sum_mm, acc_done = (self.sig(n) for n in (
            "ffn_gate_up_hi_ready", "ffn_gate_up_lo_ready", "ffn_down_hi_ready", "ffn_down_lo_ready", "ffn_gate_up_products", "ffn_down_products",
            "ffn_silu_done", "ffn_hidden_product_done", "ffn_hidden_hi_ready", "ffn_hidden_lo_ready", "ffn_half_summed", "ffn_sum_done"))
        G, N = passes * FU, passes * 2 * FU

        def g_waits(eng, g, *counts):
            if g >= FRING:
                for c in counts:
                    eng.wait_ge(*c.at(g - FRING + 1))

        with nc.Block() as block:
            @block.sync
            def _(sp):
                def load_g(g):
                    i, f = divmod(g, FU)
                    g_waits(sp, g, g_hi, g_lo)
                    for u, w in enumerate((gate_w, up_w)):
                        sp.dma_start(GRAW[:, g % FRING, u * D:(u + 1) * D].rearrange("p (k f) -> p k f", k=DT),
                                     w(i)[:, f * P:(f + 1) * P].rearrange("(k p) f -> p k f", p=P)).then_inc(*g_loaded[g % FRING].up(16))

                def load_d(n):
                    i, r = divmod(n, 2 * FU)
                    half, f = divmod(r, FU)
                    g_waits(sp, n, d_hi, d_lo)
                    sp.dma_start(DRAW[:, n % FRING, :], down_w(i)[f * P:(f + 1) * P, half * HALF:(half + 1) * HALF]).then_inc(*d_loaded[n % FRING].up(16))

                load_g(0)
                load_g(1)
                for i in range(passes):
                    for f in range(FU):
                        if f + 2 < FU:
                            load_g(i * FU + f + 2)
                        load_d(i * 2 * FU + f)
                    for f in range(FU):
                        load_d(i * 2 * FU + FU + f)
                        if f in (2, 5) and i + 1 < passes:
                            load_g((i + 1) * FU + (f == 5))

            @block.tensor
            def _(pe):
                def gate_up(g):
                    f, r = g % FU, g % FRING
                    pe.wait_ge(*g_hi.at(g + 1))
                    pe.wait_ge(*g_lo.at(g + 1))
                    if f >= 2:
                        pe.wait_ge(*prod_done.at(g - 1))
                    elif g >= FU:
                        pe.wait_ge(*acc_done.at((g // FU) * 2 * TT))
                    for u in range(2):
                        out = self.bank(2 * (f % 2) + u)
                        for k in range(DT):
                            w = [GSPL[:, r, s, (u * DT + k) * P:(u * DT + k + 1) * P] for s in range(2)]
                            nc.tensor.matmul(out, w[0], XR[:, 0, k, :], start=k == 0, stop=False)
                            nc.tensor.matmul(out, w[0], XR[:, 1, k, :], start=False, stop=False)
                            mm = nc.tensor.matmul(out, w[1], XR[:, 0, k, :], start=False, stop=k == DT - 1)
                    mm.then_inc(*g_mm.up())

                def down(n):
                    i, r = divmod(n, 2 * FU)
                    half, f = divmod(r, FU)
                    g = i * FU + f
                    pe.wait_ge(*d_hi.at(n + 1))
                    pe.wait_ge(*d_lo.at(n + 1))
                    if half == 0:
                        pe.wait_ge(*hid_lo.at(g + 1))
                        if f == 0 and i > 0:
                            pe.wait_ge(*acc_done.at(i * 2 * TT - TT))
                    for t in range(TT):
                        x = [HID[:, s, f, t * P:(t + 1) * P] for s in range(2)]
                        w = [DSPL[:, n % FRING, s, :] for s in range(2)]
                        out = self.bank(4 - 4 * half + t)
                        nc.tensor.matmul(out, x[0], w[0], start=f == 0, stop=False)
                        nc.tensor.matmul(out, x[0], w[1], start=False, stop=False)
                        mm = nc.tensor.matmul(out, x[1], w[0], start=False, stop=f == FU - 1)
                    mm.then_inc(*d_mm.up())

                for i in range(passes):
                    for f in range(FU):
                        gate_up(i * FU + f)
                        if f:
                            down(i * 2 * FU + f - 1)
                    for f in range(FU - 1, 2 * FU):
                        down(i * 2 * FU + f)

            @block.scalar
            def _(act):
                def split_g(g):
                    r = g % FRING
                    act.wait_ge(*g_loaded[r].at(32 * (g // FRING + 1)))
                    g_waits(act, g, g_mm)
                    nc.scalar.activation(GSPL[:, r, 0, :], GRAW[:, r, :], ACT.Copy).then_inc(*g_hi.up())

                def split_d(n):
                    r = n % FRING
                    act.wait_ge(*d_loaded[r].at(16 * (n // FRING + 1)))
                    g_waits(act, n, d_mm)
                    nc.scalar.activation(DSPL[:, r, 0, :], DRAW[:, r, :], ACT.Copy).then_inc(*d_hi.up())

                split_g(0)
                split_g(1)
                for i in range(passes):
                    for f in range(FU):
                        g = i * FU + f
                        if f + 2 < FU:
                            split_g(g + 2)
                        split_d(i * 2 * FU + f)
                        act.wait_ge(*g_mm.at(g + 1))
                        if g >= 2:
                            act.wait_ge(*hid_lo.at(g - 1))
                        nc.scalar.activation(TMP[:, f % 2, :], self.bank(2 * (f % 2)), ACT.Silu).then_inc(*silu_done.up())
                        act.wait_ge(*prod_done.at(g + 1))
                        if i > 0:
                            act.wait_ge(*d_mm.at(i * 2 * FU))
                        nc.scalar.activation(HID[:, 0, f, :], TMP[:, f % 2, :], ACT.Copy).then_inc(*hid_hi.up())
                    for f in range(FU):
                        split_d(i * 2 * FU + FU + f)
                    if i + 1 < passes:
                        split_g((i + 1) * FU)
                        split_g((i + 1) * FU + 1)

            @block.vector
            def _(dve):
                def split_g(g):
                    r = g % FRING
                    dve.wait_ge(*g_hi.at(g + 1))
                    nc.vector.tensor_tensor(GSPL[:, r, 1, :], GRAW[:, r, :], GSPL[:, r, 0, :].bitcast(F32), ALU.subtract).then_inc(*g_lo.up())

                def split_d(n):
                    r = n % FRING
                    dve.wait_ge(*d_hi.at(n + 1))
                    nc.vector.tensor_tensor(DSPL[:, r, 1, :], DRAW[:, r, :], DSPL[:, r, 0, :].bitcast(F32), ALU.subtract).then_inc(*d_lo.up())

                def add(i, half):
                    dve.wait_ge(*d_mm.at(i * 2 * FU + (half + 1) * FU))
                    for t in range(TT):
                        y = H[:, t, half * HALF:(half + 1) * HALF]
                        nc.vector.tensor_tensor(y, y, self.bank(4 - 4 * half + t), ALU.add).then_inc(*acc_done.up())

                split_g(0)
                split_g(1)
                for i in range(passes):
                    for f in range(FU):
                        g = i * FU + f
                        if f + 2 < FU:
                            split_g(g + 2)
                        split_d(i * 2 * FU + f)
                        dve.wait_ge(*silu_done.at(g + 1))
                        nc.vector.tensor_tensor(TMP[:, f % 2, :], TMP[:, f % 2, :], self.bank(2 * (f % 2) + 1), ALU.mult).then_inc(*prod_done.up())
                        dve.wait_ge(*hid_hi.at(g + 1))
                        nc.vector.tensor_tensor(HID[:, 1, f, :], TMP[:, f % 2, :], HID[:, 0, f, :].bitcast(F32), ALU.subtract).then_inc(*hid_lo.up())
                    if i > 0:
                        dve.wait_ge(*acc_done.at(i * 2 * TT))
                    for f in range(FU):
                        split_d(i * 2 * FU + FU + f)
                        if f == 1:
                            add(i, 0)
                    if i + 1 < passes:
                        split_g((i + 1) * FU)
                        split_g((i + 1) * FU + 1)
                    add(i, 1)
        self.close()

    def area(self, off, *dims):
        n = int(np.prod(dims))
        a = self.A[:, off:off + n]
        if len(dims) == 2:
            a = a.rearrange("p (a b) -> p a b", b=dims[1])
        elif len(dims) == 3:
            a = a.rearrange("p (a b c) -> p a b c", b=dims[1], c=dims[2])
        return a

    def ft(self, i, n=1):
        return self.A[:, FT0 + i * SEQ:FT0 + (i + n) * SEQ]

    def tok(self, col, n=GROUP):
        return self.area(TOK0, TT, TOKW)[:, :, col:col + n]

    def stage_load(self):
        nc, ap = self.nc, self.ap
        loaded = self.sig("inputs_loaded")
        with nc.Block() as block:
            @block.sync
            def _(sp):
                sp.dma_start(self.H, ap["x"][0].rearrange("(t p) d -> p t d", p=P)).then_inc(*loaded.up(16))
                sp.dma_start(self.CF[:, :], ap["const_f"]).then_inc(*loaded.up(16))
                sp.dma_start(self.PAR[:, 0:2 * NPAR], ap["par"]).then_inc(*loaded.up(16))
                sp.dma_start(self.MASK, ap["const_i"]).then_inc(*loaded.up(16))
                sp.dma_start(self.B[:, NCI * P + 1024:NCI * P + 1536], ap["const_g"]).then_inc(*loaded.up(16))
                sp.wait_ge(*loaded.at(80))

            @block.scalar
            def _(act):
                for n in ("gate_up_hi_ready", "down_hi_ready", "silu_done", "hidden_hi_ready", "scatter_matrix_ready", "tokens_hi_ready", "outputs_hi_ready"):
                    act.sem_inc(*self.sig("moe_" + n).up(8))

            @block.vector
            def _(dve):
                for n in ("gate_up_lo_ready", "down_lo_ready", "hidden_product_done", "hidden_lo_ready", "sum_done", "pick_ready", "part_sums_ready", "tokens_lo_ready", "outputs_lo_ready"):
                    dve.sem_inc(*self.sig("moe_" + n).up(8))

            @block.tensor
            def _(pe):
                for n in ("gate_up_products", "down_products", "pick_turned", "gathered", "scattered"):
                    pe.sem_inc(*self.sig("moe_" + n).up(8))
        self.close()

    def stage_to_feature(self, src, dst, scale=None, src_factor=None, split=None):
        nc, PS = self.nc, self.PS
        turned, moved, parts, read = self.sig("turned_to_feature"), self.sig("feature_tile_copied"), self.sig("feature_tile_split"), self.sig("source_scaled")
        ident = self.cf("ident")
        with nc.Block() as block:
            @block.tensor
            def _(pe):
                for k in range(DT):
                    for t in range(TT):
                        mm = nc.tensor.transpose(PS[:, k * HALF + t * P:k * HALF + (t + 1) * P], src[:, t, k * P:(k + 1) * P], ident)
                    mm.then_inc(*turned.up())

            @block.scalar
            def _(act):
                for k in range(DT):
                    act.wait_ge(*turned.at(k + 1))
                    if split is not None:
                        nc.scalar.activation(split[:, 0, k, :], self.bank(k), ACT.Copy, scale=1.0 if scale is None else scale(k)).then_inc(*parts.up())
                    elif k % 2 == 0:
                        nc.scalar.activation(dst[:, k, :], self.bank(k), ACT.Copy, scale=1.0 if scale is None else scale(k)).then_inc(*moved.up())

            @block.vector
            def _(dve):
                for k in range(DT):
                    if split is not None:
                        dve.wait_ge(*parts.at(k + 1))
                        nc.vector.scalar_tensor_tensor(split[:, 1, k, :], self.bank(k), 1.0 if scale is None else scale(k), split[:, 0, k, :].bitcast(F32),
                                                       ALU.mult, ALU.subtract).then_inc(*moved.up())
                    elif k % 2 == 1:
                        dve.wait_ge(*turned.at(k + 1))
                        if scale is None:
                            nc.vector.tensor_copy(dst[:, k, :], self.bank(k)).then_inc(*moved.up())
                        else:
                            nc.vector.tensor_scalar(dst[:, k, :], self.bank(k), scale(k), None, ALU.mult).then_inc(*moved.up())
                if src_factor == 0.0:
                    nc.vector.memset(src, 0.0).then_inc(*read.up())
                elif src_factor is not None:
                    nc.vector.tensor_scalar(src, src, src_factor, None, ALU.mult).then_inc(*read.up())
        self.close()

    def stage_stream(self, w, pieces, units, raw_at, copy_out, parts=1, engines=2, row=None):
        nc, XR, WSPL = self.nc, self.XR, self.WSPL
        loaded = [self.sig(f"w_piece_loaded{r}") for r in range(PRAW)]
        hi, lo, used, done, row_loaded = (self.sig(n) for n in ("w_piece_hi_ready", "w_piece_lo_ready", "w_piece_used", "projection_products", "gain_rows_loaded"))
        copied = [self.sig("projection_copied_act"), self.sig("projection_copied_dve")]
        raw = self.area(raw_at, PRAW, DT * PW)
        width = [sum(n for _, n in p) for p in pieces]
        flat = [(p, u, t) for p, us in enumerate(units) for u in us for t in (range(TT) if u[0] == "T" else [0])]
        turn = lambda j: j % 2 if engines == 2 else 1
        nth = lambda j: j // 2 + 1 if engines == 2 else j + 1
        dmas = lambda p: 16 * sum(len(x) for x in pieces[p % PRAW:p + 1:PRAW])

        with nc.Block() as block:
            @block.sync
            def _(sp):
                for p, part in enumerate(pieces):
                    if p >= PRAW:
                        sp.wait_ge(*hi.at(p - PRAW + 1))
                        sp.wait_ge(*lo.at(p - PRAW + 1))
                    at = 0
                    for c, n in part:
                        sp.dma_start(raw[:, p % PRAW, 0:DT * width[p]].rearrange("p (k c) -> p k c", k=DT)[:, :, at:at + n],
                                     w[:, c:c + n].rearrange("(k p) c -> p k c", p=P)).then_inc(*loaded[p % PRAW].up(16))
                        at += n
                    if p == 1 and row is not None:
                        sp.dma_start(self.area(FT0 - D, D), row.partition_broadcast(P)).then_inc(*row_loaded.up(16))
                if row is not None:
                    sp.wait_ge(*row_loaded.at(16))

            @block.tensor
            def _(pe):
                for j, (p, u, t) in enumerate(flat):
                    kind, _, c, n = u
                    if j == 0 or flat[j - 1][0] != p:
                        pe.wait_ge(*hi.at(p + 1))
                        pe.wait_ge(*lo.at(p + 1))
                    if j >= 8:
                        pe.wait_ge(*copied[turn(j)].at(nth(j - 8)))
                    ws = [WSPL[p % PSPL][:, s, 0:DT * width[p]].rearrange("p (k c) -> p k c", k=DT)[:, :, c:c + n] for s in range(2)]
                    for part in range(parts):
                        per = DT // parts
                        for k in range(part * per, (part + 1) * per):
                            first, last = k == part * per, k == (part + 1) * per - 1
                            if kind == "F":
                                out = self.bank(j % 8)[0:n, :]
                                trio = [(ws[0][:, k, :], XR[:, 0, k, :]), (ws[0][:, k, :], XR[:, 1, k, :]), (ws[1][:, k, :], XR[:, 0, k, :])]
                            else:
                                out = self.bank(j % 8)[:, part * n:(part + 1) * n]
                                xs = [XR[:, s, k, t * P:(t + 1) * P] for s in range(2)]
                                trio = [(xs[0], ws[0][:, k, :]), (xs[0], ws[1][:, k, :]), (xs[1], ws[0][:, k, :])]
                            if kind == "F" and n < P:
                                trio = [(a.bitcast(F32), b.bitcast(F32)) for a, b in trio]
                            for i, (a, b) in enumerate(trio):
                                mm = nc.tensor.matmul(out, a, b, start=first and i == 0, stop=last and i == 2)
                    mm.then_inc(*done.up())
                    if j + 1 == len(flat) or flat[j + 1][0] != p:
                        pe.wait_ge(*done.at(j + 1))
                        pe.sem_inc(*used.up())

            @block.scalar
            def _(act):
                j = 0
                for p in range(len(pieces) + 1):
                    if p < len(pieces):
                        act.wait_ge(*loaded[p % PRAW].at(dmas(p)))
                        if p >= PSPL:
                            act.wait_ge(*used.at(p - PSPL + 1))
                        nc.scalar.activation(WSPL[p % PSPL][:, 0, 0:DT * width[p]], raw[:, p % PRAW, 0:DT * width[p]], ACT.Copy).then_inc(*hi.up())
                    while j < len(flat) and flat[j][0] < p:
                        if turn(j) == 0:
                            act.wait_ge(*done.at(j + 1))
                            copy_out(0, flat[j][1], flat[j][2], j % 8).then_inc(*copied[0].up())
                        j += 1

            @block.vector
            def _(dve):
                j = 0
                for p in range(len(pieces) + 1):
                    if p < len(pieces):
                        dve.wait_ge(*hi.at(p + 1))
                        nc.vector.tensor_tensor(WSPL[p % PSPL][:, 1, 0:DT * width[p]], raw[:, p % PRAW, 0:DT * width[p]],
                                                WSPL[p % PSPL][:, 0, 0:DT * width[p]].bitcast(F32), ALU.subtract).then_inc(*lo.up())
                    while j < len(flat) and flat[j][0] < p:
                        if turn(j) == 1:
                            dve.wait_ge(*done.at(j + 1))
                            copy_out(1, flat[j][1], flat[j][2], j % 8).then_inc(*copied[1].up())
                        j += 1
        self.close()

    def project(self, w, pieces, units, row, ft, tok):
        nc = self.nc

        def copy_out(engine, u, t, b):
            kind, where, _, n = u
            out, src = (tok(where, n)[:, t, :], self.bank(b, n)) if kind == "T" else (ft(where)[0:n, :], self.bank(b)[0:n, :])
            return nc.vector.tensor_copy(out, src) if engine else nc.scalar.activation(out, src, ACT.Copy)
        self.stage_stream(w, pieces, units, HT0, copy_out, row=row)

    def stage_hgrn_gates(self, l, k):
        nc, SM = self.nc, self.SM
        sig_done, f_done, lb_ready, act_done = self.sig("hgrn_sigmoid_done"), self.sig("hgrn_f_done"), self.sig("hgrn_lb_step"), self.sig("hgrn_log_done")
        step = self.sig("dve_steps")
        q, f = self.ft(HQ, 2), self.ft(HF, 2)
        lb, om = SM[:, 64:66], SM[:, 66:68]
        a0, a1 = PAR["lb0"][0] + l * NPAR, PAR["lb1"][0] + l * NPAR
        with nc.Block() as block:
            @block.scalar
            def _(act):
                nc.scalar.activation(f, f, ACT.Sigmoid).then_inc(*sig_done.up())
                if l > 0:
                    act.wait_ge(*lb_ready.at(1))
                    nc.scalar.activation(lb, om, ACT.Sigmoid).then_inc(*sig_done.up())
                nc.scalar.activation(q, q, ACT.Silu).then_inc(*act_done.up())
                act.wait_ge(*f_done.at(2))
                nc.scalar.activation(f, f, ACT.Ln).then_inc(*act_done.up())

            @block.vector
            def _(dve):
                s = Steps(dve, step)
                if l > 0:
                    nc.vector.tensor_tensor(om, self.PAR[:, a1:a1 + 2], self.PAR[:, a0:a0 + 2], ALU.subtract).then_inc(*lb_ready.up())
                    dve.wait_ge(*sig_done.at(2))
                    s.link(nc.vector.tensor_scalar(om, lb, -1.0, 1.0, ALU.mult, ALU.add))
                    for i in range(2):
                        fi = f[:, i * SEQ:(i + 1) * SEQ]
                        s(nc.vector.tensor_scalar(fi, fi, om[:, i:i + 1], lb[:, i:i + 1], ALU.mult, ALU.add))
                    s.wait()
                else:
                    dve.wait_ge(*sig_done.at(1))
                nc.vector.tensor_scalar(k, f, -1.0, 1.0, ALU.mult, ALU.add).then_inc(*f_done.up(2))
        self.close()

    def stage_gla_gates(self, l, g, x):
        nc, ap = self.nc, self.ap
        loaded, mm_done, x_ready, log_done, step = (self.sig(n) for n in (
            "gla_w2_loaded", "gla_gate_product", "gla_gate_biased", "gla_softplus_done", "dve_steps"))
        w2 = self.A[0:16, 0:P]
        q = self.ft(GQ)
        astep = self.sig("act_steps")
        with nc.Block() as block:
            @block.sync
            def _(sp):
                sp.dma_start(w2, ap["gla_gate_w2"][l]).then_inc(*loaded.up(16))

            @block.tensor
            def _(pe):
                pe.wait_ge(*loaded.at(16))
                nc.tensor.matmul(self.bank(0), w2, self.ft(GLR)[0:16, :], start=True, stop=True).then_inc(*mm_done.up())

            @block.vector
            def _(dve):
                s = Steps(dve, step)
                dve.wait_ge(*mm_done.at(1))
                nc.vector.tensor_scalar(x, self.bank(0), self.par(l, "gate_b"), None, ALU.add).then_inc(*x_ready.up())
                dve.wait_ge(*x_ready.at(1))
                s(nc.vector.tensor_scalar(q, q, 32.0 ** -0.5, None, ALU.mult))
                s.link(nc.vector.tensor_scalar(self.bank(1), x, 0.0, None, ALU.min))
                dve.wait_ge(*log_done.at(1))
                s.link(nc.vector.tensor_tensor(g, self.bank(1), g, ALU.subtract))
                s.link(nc.vector.tensor_scalar(g, g, 1.0 / 16.0, None, ALU.mult))

            @block.scalar
            def _(act):
                s = Steps(act, astep)
                act.wait_ge(*x_ready.at(1))
                s.link(nc.scalar.activation(g, x, ACT.Abs))
                s.link(nc.scalar.activation(g, g, ACT.Exp, scale=-1.0))
                nc.scalar.activation(g, g, ACT.Ln, bias=1.0).then_inc(*log_done.up())
        self.close()

    def stage_decay_scores(self, q, k, g, T, kd, S, Qc, KD, DEC, base):
        nc, PS = self.nc, self.PS
        W = T * SEQ
        cum, rst = self.area(base, W), self.area(base + 1024, W)
        E = [self.area(base + 2048 + 1024 * i, W) for i in range(2)]
        Q = [self.area(base + 4096 + 1024 * i, W) for i in range(2)]
        K = [self.area(base + 6144 + 1024 * i, W) for i in range(2)]
        step, astep, diff, exps, qk, mms, taken = (self.sig(n) for n in (
            "dve_steps", "act_steps", "decay_difference", "decay_factor", "decayed_qk_ready", "score_products", "scores_taken"))
        hpt = P // kd
        chunks = cum.rearrange("p (n s) -> p n s", s=P)
        LAST = LEVELS + 1
        with nc.Block() as block:
            @block.vector
            def _(dve):
                s = Steps(dve, step)
                s(nc.vector.memset(S, 0.0))
                s.link(nc.vector.memset(rst, 1.0))
                s.link(nc.vector.memset(rst.rearrange("p (n s) -> p n s", s=P)[:, :, 0:1], 0.0))
                s.link(nc.vector.tensor_tensor_scan(cum, rst, g, 0.0, ALU.mult, ALU.add))

                def subtract(l):
                    if l < LEVELS:
                        h = 1 << l
                        v = "p (n s) -> p n s"
                        c = cum.rearrange(v, s=2 * h)
                        nc.vector.tensor_tensor(E[l % 2].rearrange(v, s=2 * h), c, c[:, :, h - 1:h].broadcast_to([P, W // (2 * h), 2 * h]),
                                                ALU.subtract).then_inc(*diff.up())
                    elif l == LEVELS:
                        nc.vector.tensor_tensor(E[l % 2].rearrange("p (n s) -> p n s", s=P), chunks, chunks[:, :, P - 1:P].broadcast_to([P, W // P, P]),
                                                ALU.subtract).then_inc(*diff.up())

                def take(l):
                    dve.wait_ge(*mms.at(l + 1))
                    if l >= 1:
                        dve.wait_ge(*taken.at(l))
                    m = self.MASK[:, (LVT + l) * P:(LVT + l + 1) * P] if l < LEVELS else self.MASK[:, DIAG * P:(DIAG + 1) * P]
                    nc.vector.copy_predicated(S.rearrange("p (n i) -> p n i", i=P), m.unsqueeze(1).broadcast_to([P, 16, P]),
                                              PS[:, (l % 2) * 2048:(l % 2) * 2048 + 2048].rearrange("p (n i) -> p n i", i=P)).then_inc(*taken.up())

                subtract(0)
                for l in range(LEVELS):
                    if l >= 1:
                        dve.wait_ge(*qk.at(l))
                    subtract(l + 1)
                    dve.wait_ge(*exps.at(l + 1))
                    if l >= 2:
                        dve.wait_ge(*mms.at(l - 1))
                    s(nc.vector.tensor_tensor(Q[l % 2], q, E[l % 2], ALU.mult))
                    nc.vector.tensor_tensor(K[l % 2], k, E[l % 2], ALU.mult).then_inc(*qk.up())
                    if l >= 1:
                        take(l - 1)
                take(LEVELS - 1)
                dve.wait_ge(*exps.at(LEVELS + 1))
                s(nc.vector.tensor_tensor(KD, k, E[LEVELS % 2], ALU.mult))
                dve.wait_ge(*exps.at(LEVELS + 2))
                s(nc.vector.tensor_tensor(Qc, q, rst, ALU.mult))
                take(LEVELS)

            @block.scalar
            def _(act):
                s = Steps(act, astep)
                for l in range(LEVELS + 1):
                    act.wait_ge(*diff.at(l + 1))
                    s.link(nc.scalar.activation(E[l % 2], E[l % 2], ACT.Abs))
                    nc.scalar.activation(E[l % 2], E[l % 2], ACT.Exp, scale=-1.0).then_inc(*exps.up())
                nc.scalar.activation(DEC.rearrange("p (n s) -> p n s", s=1), chunks[:, :, P - 1:P], ACT.Exp).then_inc(*astep.up())
                nc.scalar.activation(rst, cum, ACT.Exp).then_inc(*exps.up())

            @block.tensor
            def _(pe):
                for l in range(LEVELS + 1):
                    a, b = (Q[l % 2], K[l % 2]) if l < LEVELS else (q, k)
                    if l < LEVELS:
                        pe.wait_ge(*qk.at(l + 1))
                    if l >= 2:
                        pe.wait_ge(*taken.at(l - 1))
                    for c in range(TT):
                        for h in range(NHEAD):
                            r, col = (h % hpt) * kd, (h // hpt) * SEQ + c * P
                            o = (l % 2) * 2048 + (h * TT + c) * P
                            mm = nc.tensor.matmul(PS[:, o:o + P], b[r:r + kd, col:col + P], a[r:r + kd, col:col + P], start=True, stop=True)
                    mm.then_inc(*mms.up())
        self.close()

    def stage_state(self, S, Qc, KD, DEC, V, T, kd, O, KT, Z):
        nc, PS = self.nc, self.PS
        turned, kt_ready, out_mm, z_mm, z_ready, o_ready, step = (self.sig(n) for n in (
            "key_turned", "key_token_major_ready", "chunk_output_products", "state_products", "state_ready", "chunk_output_ready", "dve_steps"))
        hpt = P // kd
        N = hpt * HD
        s_v = S.rearrange("p (n i) -> p n i", i=P)
        with nc.Block() as block:
            @block.tensor
            def _(pe):
                for c in range(TT - 1):
                    for j in range(T):
                        mm = nc.tensor.transpose(PS[:, c * HALF + j * P:c * HALF + (j + 1) * P], KD[:, j * SEQ + c * P:j * SEQ + (c + 1) * P], self.cf("ident"))
                mm.then_inc(*turned.up())
                for c in range(TT):
                    for h in range(NHEAD):
                        mm = nc.tensor.matmul(self.bank(4 + c)[:, h * HD:(h + 1) * HD], s_v[:, h * TT + c, :], V[:, c, h * HD:(h + 1) * HD], start=True, stop=c == 0)
                        if c > 0:
                            if h == 0:
                                pe.wait_ge(*z_ready.at(c))
                            j = h // hpt
                            mm = nc.tensor.matmul(self.bank(4 + c)[:, h * HD:(h + 1) * HD], Qc[:, j * SEQ + c * P:j * SEQ + (c + 1) * P],
                                                  Z[:, c - 1, h * HD:(h + 1) * HD], start=False, stop=True)
                    mm.then_inc(*out_mm.up())
                    if c == 0:
                        pe.wait_ge(*kt_ready.at(1))
                    if c < TT - 1:
                        for j in range(T):
                            mm = nc.tensor.matmul(self.bank(c)[:, j * N:(j + 1) * N], KT[:, c, j * P:(j + 1) * P], V[:, c, j * N:(j + 1) * N], start=True, stop=True)
                        mm.then_inc(*z_mm.up())

            @block.vector
            def _(dve):
                s = Steps(dve, step)
                dve.wait_ge(*turned.at(1))
                nc.vector.tensor_copy(KT[:, 0:TT - 1, :], PS[:, 0:(TT - 1) * HALF].rearrange("p (c n) -> p c n", n=HALF)[:, :, 0:T * P]).then_inc(*kt_ready.up())
                for c in range(TT - 1):
                    dve.wait_ge(*z_mm.at(c + 1))
                    z = Z[:, c, :].rearrange("p (j n) -> p j n", n=N)
                    own = (self.HSUM if kd == HD else self.GMASK).unsqueeze(1).broadcast_to([P, T, N])
                    if c == 0:
                        nc.vector.tensor_tensor(z, self.bank(0, GROUP).rearrange("p (j n) -> p j n", n=N), own, ALU.mult).then_inc(*z_ready.up())
                    else:
                        dve.wait_ge(*z_ready.at(c))
                        for j in range(T):
                            a = slice(j * N, (j + 1) * N)
                            s(nc.vector.scalar_tensor_tensor(Z[:, c, a], Z[:, c - 1, a], DEC[:, j * TT + c:j * TT + c + 1], self.bank(c)[:, a], ALU.mult, ALU.add))
                        s.wait()
                        nc.vector.tensor_tensor(z, z, own, ALU.mult).then_inc(*z_ready.up())

            @block.scalar
            def _(act):
                for c in range(TT):
                    act.wait_ge(*out_mm.at(c + 1))
                    nc.scalar.activation(O[:, c, :], self.bank(4 + c, GROUP), ACT.Copy).then_inc(*o_ready.up())
        self.close()

    def stage_head_norm(self, O, SQ, gate, out, eps, center=False, gain=None, bias=None, bonus=None, silu_gate=True):
        nc, SM = self.nc, self.SM
        step, var_ready, root_ready, gate_ready = self.sig("dve_steps"), self.sig("head_variance_ready"), self.sig("head_root_ready"), self.sig("head_gate_ready")
        N = TT * NHEAD
        mean, var = SM[:, 64:64 + N], SM[:, 80:80 + N]
        fh = "p t (h e) -> p (t h) e"
        o3, sq3, v3 = O.rearrange("p t n -> p (t n)").rearrange("p (n e) -> p n e", e=HD), SQ.rearrange("p t n -> p (t n)").rearrange("p (n e) -> p n e", e=HD), None
        bc = lambda x: x.unsqueeze(2).broadcast_to([P, N, HD])
        rowbc = lambda x: x.unsqueeze(1).broadcast_to([P, TT, GROUP])
        with nc.Block() as block:
            @block.vector
            def _(dve):
                s = Steps(dve, step)
                if center:
                    s.link(nc.vector.tensor_reduce(mean, o3, AX.X, ALU.add))
                    s.link(nc.vector.tensor_scalar(mean, mean, 1.0 / HD, None, ALU.mult))
                    s.link(nc.vector.tensor_tensor(o3, o3, bc(mean), ALU.subtract))
                s.link(nc.vector.tensor_tensor(SQ, O, O, ALU.mult))
                s.link(nc.vector.tensor_reduce(var, sq3, AX.X, ALU.add))
                nc.vector.tensor_scalar(var, var, 1.0 / HD, eps, ALU.mult, ALU.add).then_inc(*var_ready.up())
                dve.wait_ge(*root_ready.at(1))
                s.link(nc.vector.reciprocal(var, var))
                s.link(nc.vector.tensor_tensor(o3, o3, bc(var), ALU.mult))
                if gain is not None:
                    s.link(nc.vector.tensor_tensor(O, O, rowbc(gain), ALU.mult))
                if bias is not None:
                    s.link(nc.vector.tensor_tensor(O, O, rowbc(bias), ALU.add))
                if bonus is not None:
                    s.link(nc.vector.tensor_tensor(sq3, bonus[0].rearrange("p t n -> p (t n)").rearrange("p (n e) -> p n e", e=HD), bc(bonus[1]), ALU.mult))
                    s.link(nc.vector.tensor_tensor(O, O, SQ, ALU.add))
                if silu_gate:
                    dve.wait_ge(*gate_ready.at(1))
                s.link(nc.vector.tensor_tensor(out, O, gate, ALU.mult))

            @block.scalar
            def _(act):
                if silu_gate:
                    nc.scalar.activation(gate, gate, ACT.Silu).then_inc(*gate_ready.up())
                act.wait_ge(*var_ready.at(1))
                nc.scalar.activation(var, var, ACT.Sqrt).then_inc(*root_ready.up())
        self.close()

    def stage_retention_scores(self, S, Qc, KD, DEC, base):
        nc, ap, PS = self.nc, self.ap, self.PS
        loaded, step, asteps, swapped, rotated, mms, angles, trig = (self.sig(n) for n in (
            "retention_tables_loaded", "dve_steps", "act_steps", "rotary_swapped", "rotary_ready", "score_products", "angles_ready", "sines_ready"))
        q, k = self.ft(RQ, 2), self.ft(RKK, 2)
        pos = self.area(base, SEQ).bitcast(I32)
        ang, n1, sn, cs = (self.area(base + SEQ * i, SEQ) for i in (1, 2, 3, 4))
        tab = self.area(base + SEQ * 5, NRET)
        tmp = self.area(base + SEQ * 5 + 1088, 2 * SEQ)
        MAGIC = 12582912.0
        C1, C2 = 6.28125, 0.0019350051879882812
        C3 = float(2.0 * np.pi - C1 - C2)
        LIM = 3.1415925
        t3 = lambda x: x.rearrange("p (a t) -> p a t", t=SEQ)
        bc = lambda x: x.unsqueeze(1).broadcast_to([P, 2, SEQ])
        with nc.Block() as block:
            @block.sync
            def _(sp):
                sp.dma_start(pos, ap["positions"][0].partition_broadcast(P)).then_inc(*loaded.up(16))
                sp.dma_start(tab, ap["ret_c"]).then_inc(*loaded.up(16))

            @block.tensor
            def _(pe):
                for i, x in enumerate((q, k)):
                    for j in range(2):
                        mm = nc.tensor.matmul(self.bank(2 * i + j), self.SWAP, x[:, j * SEQ:(j + 1) * SEQ], start=True, stop=True)
                mm.then_inc(*swapped.up())
                pe.wait_ge(*rotated.at(1))
                for c in range(TT):
                    for h in range(NHEAD):
                        r, col = (h % 2) * HD, (h // 2) * SEQ + c * P
                        mm = nc.tensor.matmul(self.bank(4 + h)[:, c * P:(c + 1) * P], k[r:r + HD, col:col + P], q[r:r + HD, col:col + P], start=True, stop=True)
                mm.then_inc(*mms.up())

            @block.scalar
            def _(act):
                for i, x in enumerate((sn, cs)):
                    act.wait_ge(*angles.at(i + 1))
                    nc.scalar.activation(x, x, ACT.Sin).then_inc(*trig.up())

            @block.vector
            def _(dve):
                s = Steps(dve, step)
                dve.wait_ge(*loaded.at(32))
                s.link(nc.vector.tensor_copy(ang, pos))
                s.link(nc.vector.tensor_scalar(ang, ang, self.cf("invf"), None, ALU.mult))
                for i, (x, turn) in enumerate(((sn, 0.0), (cs, 0.25))):
                    s.link(nc.vector.tensor_scalar(n1, ang, 1.0 / (2.0 * np.pi), turn, ALU.mult, ALU.add))
                    s.link(nc.vector.tensor_scalar(n1, n1, MAGIC, None, ALU.add))
                    s.link(nc.vector.tensor_scalar(n1, n1, MAGIC, None, ALU.subtract))
                    s.link(nc.vector.scalar_tensor_tensor(x, n1, -C1, ang, ALU.mult, ALU.add))
                    s.link(nc.vector.scalar_tensor_tensor(x, n1, -C2, x, ALU.mult, ALU.add))
                    s.link(nc.vector.scalar_tensor_tensor(x, n1, -C3, x, ALU.mult, ALU.add))
                    s.link(nc.vector.tensor_scalar(x, x, turn * 2.0 * np.pi, None, ALU.add))
                    nc.vector.tensor_scalar(x, x, LIM, -LIM, ALU.min, ALU.max).then_inc(*angles.up())
                dve.wait_ge(*trig.at(2))
                dve.wait_ge(*swapped.at(1))
                for i, x in enumerate((q, k)):
                    s.link(nc.vector.tensor_tensor(t3(tmp), t3(PS[:, 2 * i * HALF:(2 * i + 2) * HALF]), bc(sn), ALU.mult))
                    s.link(nc.vector.tensor_tensor(t3(x), t3(x), bc(cs), ALU.mult))
                    if i == 0:
                        s.link(nc.vector.tensor_tensor(x, x, tmp, ALU.add))
                s.link(nc.vector.tensor_tensor(k, k, tmp, ALU.add))
                nc.vector.tensor_scalar(k, k, HD ** -0.5, None, ALU.mult).then_inc(*rotated.up())
                dve.wait_ge(*rotated.at(1))
                for j in range(2):
                    c3 = lambda x: x[:, j * SEQ:(j + 1) * SEQ].rearrange("p (c t) -> p c t", t=P)
                    tbl = lambda o: tab[:, o + j * P:o + (j + 1) * P].unsqueeze(1).broadcast_to([P, TT, P])
                    s(nc.vector.tensor_tensor(c3(Qc), c3(q), tbl(RET_Q), ALU.mult))
                    s(nc.vector.tensor_tensor(c3(KD), c3(k), tbl(RET_K), ALU.mult))
                    s(nc.vector.tensor_copy(DEC[:, j * TT:(j + 1) * TT], tab[:, RET_C + j:RET_C + j + 1].broadcast_to([P, TT])))
                dve.wait_ge(*mms.at(1))
                h3 = lambda x: x.rearrange("p (h c i) -> p h c i", c=TT, i=P)
                s(nc.vector.tensor_tensor(h3(S), h3(PS[:, 4 * HALF:8 * HALF]),
                                          tab[:, RET_D:RET_D + HALF].rearrange("p (h i) -> p h i", i=P).unsqueeze(2).broadcast_to([P, NHEAD, TT, P]), ALU.mult))
        self.close()

    RW_A, RW_B, RW_R, RW_K = 0, 1024, 2048, 3072
    RW_AT, RW_BT, RW_KT, RW_VT = 4096, 5120, 6144, 7168
    RW_M, RW_MAK, RW_MRB, RW_MRK = 8192, 10240, 12288, 14336
    RW_T, RW_U, RW_X, RW_PT = 16384, 18432, FT0, FT0 + 2048
    RW_SMALL = FT0 + 3072
    RW_Z = 20480
    RW_C, RW_LR, RW_KK, RW_G, RW_T1, RW_T2 = (TOK0 + 1024 * i for i in range(6))
    RW_O, RW_U0 = FT0 + 16 * SEQ, FT0 + 18 * SEQ

    def stage_rwkv_gates(self, l):
        nc, ap, PS = self.nc, self.ap, self.PS
        loaded, step, astep, shifted, lowrank, mms, gates, v_mm, v_cp, kk_sq, kk_sum, kk_root, root, cum_ready, exps = (self.sig(n) for n in (
            "rwkv_weights_loaded", "dve_steps", "act_steps", "rwkv_shifted", "rwkv_low_rank_ready", "rwkv_gate_products", "rwkv_gates_ready",
            "rwkv_value_products", "rwkv_value_step", "rwkv_kk_squares", "rwkv_kk_sums", "rwkv_kk_clamped", "rwkv_kk_norm", "rwkv_decay_sums", "rwkv_decay_factors"))
        X = self.ft(RR, 9).rearrange("p (n t) -> p n t", t=SEQ)
        Dd = self.area(8192, 9, SEQ)
        r, k, v = self.ft(RR, 2), self.ft(RK, 2), self.ft(RV, 2)
        wa, g0, g1 = self.ft(RWA), self.ft(RG), self.ft(RG + 1)[0:32, :]
        w2a2 = self.area(self.RW_T, 256)
        g2a, g2b = self.area(self.RW_T + 256, 256), self.area(self.RW_T + 512, 256)
        v1 = self.area(self.RW_T + 768, 2, 32)
        v2 = self.area(self.RW_T + 832, 256)[0:32, :]
        t32 = self.area(self.RW_T + 1088, SEQ)[0:32, :]
        rst = self.area(self.RW_U, 1024)
        c, a, kk, gt, t1, t2 = (self.area(o, 1024) for o in (self.RW_C, self.RW_LR, self.RW_KK, self.RW_G, self.RW_T1, self.RW_T2))
        At, Bt, Rt, Kt = (self.area(o, 1024) for o in (self.RW_A, self.RW_B, self.RW_R, self.RW_K))
        DEC, MID = self.area(self.RW_SMALL, 8), self.area(self.RW_SMALL + 8, 8)
        two = lambda x: [x[:, j * SEQ:(j + 1) * SEQ] for j in range(2)]
        chunk = lambda x: x.rearrange("p (n s) -> p n s", s=P)
        with nc.Block() as block:
            @block.sync
            def _(sp):
                sp.dma_start(w2a2[0:64, :], ap["rwkv_w2"][l]).then_inc(*loaded.up(16))
                sp.dma_start(w2a2[64:128, :], ap["rwkv_a2"][l]).then_inc(*loaded.up(16))
                sp.dma_start(g2a, ap["rwkv_g2"][l][0:P, :]).then_inc(*loaded.up(16))
                sp.dma_start(g2b[0:32, :], ap["rwkv_g2"][l][P:160, :]).then_inc(*loaded.up(16))
                if l > 0:
                    sp.dma_start(v1, ap["rwkv_v1"][l - 1].rearrange("(a p) n -> p a n", p=P)).then_inc(*loaded.up(16))
                    sp.dma_start(v2, ap["rwkv_v2"][l - 1]).then_inc(*loaded.up(16))

            @block.vector
            def _(dve):
                s = Steps(dve, step)
                s(nc.vector.tensor_tensor(Dd[:, 0:8, 1:SEQ], X[:, 0:8, 0:SEQ - 1], X[:, 0:8, 1:SEQ], ALU.subtract))
                s(nc.vector.tensor_tensor(Dd[0:32, 8, 1:SEQ], X[0:32, 8, 0:SEQ - 1], X[0:32, 8, 1:SEQ], ALU.subtract))
                s(nc.vector.tensor_scalar(Dd[:, 0:8, 0:1], X[:, 0:8, 0:1], -1.0, None, ALU.mult))
                s.link(nc.vector.tensor_scalar(Dd[0:32, 8, 0:1], X[0:32, 8, 0:1], -1.0, None, ALU.mult))
                for j in range(9):
                    n = 32 if j == 8 else P
                    nc.vector.scalar_tensor_tensor(X[0:n, j, :], Dd[0:n, j, :], self.par(l, "mu", j)[0:n, :], X[0:n, j, :], ALU.mult, ALU.add).then_inc(*shifted.up())
                dve.wait_ge(*shifted.at(9))
                for j in range(2):
                    s(nc.vector.tensor_scalar(two(kk)[j], two(k)[j], self.par(l, "k_k", j), None, ALU.mult))
                s.wait()
                nc.vector.tensor_tensor(t1, kk, kk, ALU.mult).then_inc(*kk_sq.up())
                s.link(nc.vector.memset(rst, 1.0))
                s.link(nc.vector.memset(chunk(rst)[:, :, 0:1], 0.0))
                dve.wait_ge(*gates.at(4))
                s.link(nc.vector.tensor_scalar(t2, t2, -EXP_NEG_HALF, None, ALU.mult))
                s.link(nc.vector.tensor_tensor_scan(c, rst, t2, 0.0, ALU.mult, ALU.add))
                s.link(nc.vector.tensor_copy(MID, chunk(c)[:, :, P // 2 - 1:P // 2].rearrange("p n s -> p (n s)")))
                s.link(nc.vector.tensor_tensor(chunk(c), chunk(c), MID.unsqueeze(2).broadcast_to([P, 8, P]), ALU.subtract))
                nc.vector.tensor_tensor(t2, c, t2, ALU.subtract).then_inc(*cum_ready.up())
                s.link(nc.vector.tensor_copy(DEC, chunk(c)[:, :, P - 1:P].rearrange("p n s -> p (n s)")))
                for j in range(2):
                    s(nc.vector.tensor_tensor(DEC[:, j * TT:j * TT + 3], DEC[:, j * TT:j * TT + 3], MID[:, j * TT + 1:j * TT + 4], ALU.add))
                s.wait()
                nc.vector.tensor_copy(DEC, DEC).then_inc(*cum_ready.up())
                if l == 0:
                    s(nc.vector.tensor_copy(self.VF, v))
                else:
                    dve.wait_ge(*v_mm.at(1))
                    nc.vector.tensor_copy(t32, self.bank(0)[0:32, :]).then_inc(*v_cp.up())
                    s.link(nc.vector.tensor_tensor(self.VF, self.VF, v, ALU.subtract))
                    dve.wait_ge(*v_cp.at(3))
                    s.link(nc.vector.tensor_tensor(self.VF, self.VF, At, ALU.mult))
                    s.link(nc.vector.tensor_tensor(v, v, self.VF, ALU.add))
                dve.wait_ge(*kk_sum.at(1))
                nc.vector.tensor_scalar(t1, PS[:, 6 * HALF:8 * HALF], 1e-24, None, ALU.max).then_inc(*kk_root.up())
                dve.wait_ge(*root.at(1))
                s.link(nc.vector.reciprocal(t1, t1))
                s.link(nc.vector.tensor_tensor(kk, kk, t1, ALU.mult))
                for j in range(2):
                    s(nc.vector.tensor_scalar(two(t1)[j], two(a)[j], 1.0, self.par(l, "k_a", j), ALU.subtract, ALU.mult))
                s.wait()
                s.link(nc.vector.scalar_tensor_tensor(k, t1, 1.0, k, ALU.add, ALU.mult))
                dve.wait_ge(*exps.at(3))
                s.link(nc.vector.scalar_tensor_tensor(At, kk, -1.0, t2, ALU.mult, ALU.mult))
                s.link(nc.vector.tensor_tensor(Rt, r, Rt, ALU.mult))
                s.link(nc.vector.tensor_tensor(Kt, k, Bt, ALU.mult))
                s.link(nc.vector.tensor_tensor(kk, kk, a, ALU.mult))
                s.link(nc.vector.tensor_tensor(Bt, kk, Bt, ALU.mult))
                for j in range(2):
                    s(nc.vector.scalar_tensor_tensor(two(r)[j], two(r)[j], self.par(l, "r_k", j), two(k)[j], ALU.mult, ALU.mult))

            @block.scalar
            def _(act):
                s = Steps(act, astep)
                act.wait_ge(*shifted.at(9))
                nc.scalar.activation(wa[0:64, :], wa[0:64, :], ACT.Tanh).then_inc(*lowrank.up())
                nc.scalar.activation(g0, g0, ACT.Sigmoid).then_inc(*lowrank.up())
                nc.scalar.activation(g1, g1, ACT.Sigmoid).then_inc(*lowrank.up())
                act.wait_ge(*mms.at(1))
                for j in range(2):
                    nc.scalar.activation(two(t2)[j], self.bank(j), ACT.Sigmoid, bias=self.par(l, "w0", j)).then_inc(*gates.up())
                for j in range(2):
                    nc.scalar.activation(two(a)[j], self.bank(2 + j), ACT.Sigmoid, bias=self.par(l, "a0", j)).then_inc(*gates.up())
                s(nc.scalar.activation(gt, PS[:, 4 * HALF:6 * HALF], ACT.Copy))
                if l > 0:
                    act.wait_ge(*v_mm.at(2))
                    for j in range(2):
                        nc.scalar.activation(two(At)[j], self.bank(2 + j), ACT.Sigmoid, bias=self.par(l, "v0", j)).then_inc(*v_cp.up())
                act.wait_ge(*kk_root.at(1))
                nc.scalar.activation(t1, t1, ACT.Sqrt).then_inc(*root.up())
                act.wait_ge(*cum_ready.at(2))
                nc.scalar.activation(Rt, c, ACT.Exp).then_inc(*exps.up())
                nc.scalar.activation(Bt, c, ACT.Exp, scale=-1.0).then_inc(*exps.up())
                s(nc.scalar.activation(DEC, DEC, ACT.Exp))
                nc.scalar.activation(t2, t2, ACT.Exp).then_inc(*exps.up())

            @block.tensor
            def _(pe):
                pe.wait_ge(*loaded.at(64 if l == 0 else 96))
                pe.wait_ge(*lowrank.at(3))
                for j in range(2):
                    nc.tensor.matmul(self.bank(j), w2a2[0:64, j * P:(j + 1) * P], wa[0:64, :], start=True, stop=True)
                    nc.tensor.matmul(self.bank(2 + j), w2a2[64:128, j * P:(j + 1) * P], wa[64:128, :], start=True, stop=True)
                for t in range(TT):
                    o = PS[:, 4 * HALF + t * GROUP:4 * HALF + (t + 1) * GROUP]
                    nc.tensor.matmul(o, g0[:, t * P:(t + 1) * P], g2a, start=True, stop=False)
                    mm = nc.tensor.matmul(o, g1[:, t * P:(t + 1) * P], g2b[0:32, :], start=False, stop=True)
                mm.then_inc(*mms.up())
                pe.wait_ge(*kk_sq.at(1))
                for j in range(2):
                    mm = nc.tensor.matmul(self.bank(6 + j), self.HSUM, two(t1)[j], start=True, stop=True)
                mm.then_inc(*kk_sum.up())
                if l > 0:
                    pe.wait_ge(*gates.at(4))
                    for j in range(2):
                        mm = nc.tensor.matmul(self.bank(0)[0:32, :], v1[:, j, :], two(v)[j], start=j == 0, stop=j == 1)
                    mm.then_inc(*v_mm.up())
                    pe.wait_ge(*v_cp.at(1))
                    for j in range(2):
                        mm = nc.tensor.matmul(self.bank(2 + j), v2[:, j * P:(j + 1) * P], t32, start=True, stop=True)
                    mm.then_inc(*v_mm.up())
        self.close()

    def stage_rwkv_scores(self, l):
        nc, PS = self.nc, self.PS
        mms, taken, turned, copied, step, cleared = (self.sig(n) for n in (
            "score_products", "scores_taken", "rwkv_turned", "rwkv_token_major_ready", "dve_steps", "rwkv_scores_cleared"))
        At, Bt, Rt, Kt = (self.area(o, 1024) for o in (self.RW_A, self.RW_B, self.RW_R, self.RW_K))
        v, r = self.ft(RV, 2), self.ft(RR, 2)
        pairs = [(Bt, At, self.RW_M, STRICT), (Kt, At, self.RW_MAK, STRICT), (Bt, Rt, self.RW_MRB, INCL), (Kt, Rt, self.RW_MRK, INCL)]
        turns = [(At, self.RW_AT), (Bt, self.RW_BT), (Kt, self.RW_KT), (v, self.RW_VT)]
        n3 = lambda x: x.rearrange("p (n i) -> p n i", i=P)
        bonus = self.area(self.RW_SMALL + 16, 16)
        with nc.Block() as block:
            @block.gpsimd
            def _(pool):
                for _, _, o, _ in pairs:
                    nc.gpsimd.memset(self.area(o, 2048), 0.0).then_inc(*cleared.up())

            @block.tensor
            def _(pe):
                def scores(i):
                    a, b, _, _ = pairs[i]
                    for c in range(TT):
                        for h in range(NHEAD):
                            rr, col = (h % 2) * HD, (h // 2) * SEQ + c * P
                            o = (h * TT + c) * P
                            mm = nc.tensor.matmul(PS[:, o:o + P], a[rr:rr + HD, col:col + P], b[rr:rr + HD, col:col + P], start=True, stop=True)
                    mm.then_inc(*mms.up())

                def turn(i):
                    for c in range(TT):
                        for j in range(2):
                            o = 2048 + i % 2 * 1024 + c * GROUP + j * P
                            mm = nc.tensor.transpose(PS[:, o:o + P], turns[i][0][:, j * SEQ + c * P:j * SEQ + (c + 1) * P], self.cf("ident"))
                    mm.then_inc(*turned.up())

                for i in range(4):
                    if i >= 1:
                        pe.wait_ge(*taken.at(i))
                    scores(i)
                    if i >= 2:
                        pe.wait_ge(*copied.at(i - 1))
                    turn(i)
                pe.wait_ge(*copied.at(3))
                for c in range(TT):
                    for j in range(2):
                        mm = nc.tensor.matmul(PS[:, 2048 + c * NHEAD:2048 + (c + 1) * NHEAD], r[:, j * SEQ + c * P:j * SEQ + (c + 1) * P],
                                              self.cf("headcol")[:, j * 4:j * 4 + 4], start=j == 0, stop=j == 1)
                mm.then_inc(*turned.up())

            @block.vector
            def _(dve):
                dve.wait_ge(*cleared.at(4))
                for i, (_, _, o, m) in enumerate(pairs):
                    dve.wait_ge(*mms.at(i + 1))
                    nc.vector.copy_predicated(n3(self.area(o, 2048)), self.MASK[:, m * P:(m + 1) * P].unsqueeze(1).broadcast_to([P, 16, P]),
                                              n3(PS[:, 0:2048])).then_inc(*taken.up())
                for o in (self.RW_T, self.RW_U):
                    nc.vector.tensor_copy(n3(self.area(o, 2048)), self.cf("ident").unsqueeze(1).broadcast_to([P, 16, P])).then_inc(*step.up())

            @block.scalar
            def _(act):
                for i, (_, o) in enumerate(turns):
                    act.wait_ge(*turned.at(i + 1))
                    nc.scalar.activation(self.area(o, 1024), PS[:, 2048 + i % 2 * 1024:3072 + i % 2 * 1024], ACT.Copy).then_inc(*copied.up())
                act.wait_ge(*turned.at(5))
                nc.scalar.activation(bonus, PS[:, 2048:2064], ACT.Copy).then_inc(*copied.up())
        self.close()

    def stage_rwkv_solve(self):
        nc, PS = self.nc, self.PS
        x_mm, x_ready, t_mm, u_mm, t_ready, u_ready = (self.sig(n) for n in (
            "solve_nt_products", "solve_nt_ready", "solve_tnt_products", "solve_u_products", "solve_t_ready", "solve_u_ready"))
        M, T, U, X = (self.area(o, NHEAD, TT, P) for o in (self.RW_M, self.RW_T, self.RW_U, self.RW_X))
        b3 = lambda b: self.bank(b).rearrange("p (c i) -> p c i", i=P)
        with nc.Block() as block:
            @block.tensor
            def _(pe):
                for l in range(LEVELS):
                    for h in range(NHEAD):
                        if l > 0:
                            pe.wait_ge(*t_ready.at((l - 1) * NHEAD + h + 1))
                            pe.wait_ge(*u_ready.at((l - 1) * NHEAD + h + 1))
                        for c in range(TT):
                            mm = nc.tensor.matmul(self.bank(h)[:, c * P:(c + 1) * P], M[:, h, c, :], T[:, h, c, :], start=True, stop=True)
                        mm.then_inc(*x_mm.up())
                    for h in range(NHEAD):
                        pe.wait_ge(*x_ready.at(l * NHEAD + h + 1))
                        if l < LEVELS - 1:
                            for c in range(TT):
                                mm = nc.tensor.matmul(self.bank(4 + h)[:, c * P:(c + 1) * P], U[:, h, c, :], X[:, h, c, :], start=True, stop=True)
                            mm.then_inc(*t_mm.up())
                        for c in range(TT):
                            mm = nc.tensor.matmul(self.bank(h)[:, c * P:(c + 1) * P], X[:, h, c, :], U[:, h, c, :], start=True, stop=True)
                        mm.then_inc(*u_mm.up())

            @block.scalar
            def _(act):
                for l in range(LEVELS):
                    for h in range(NHEAD):
                        act.wait_ge(*x_mm.at(l * NHEAD + h + 1))
                        nc.scalar.activation(X[:, h, :, :], b3(h), ACT.Copy).then_inc(*x_ready.up())

            @block.vector
            def _(dve):
                mask = lambda m: self.MASK[:, m * P:(m + 1) * P].unsqueeze(1).broadcast_to([P, TT, P])
                for l in range(LEVELS):
                    for h in range(NHEAD):
                        dve.wait_ge(*u_mm.at(l * NHEAD + h + 1))
                        if l < LEVELS - 1:
                            nc.vector.copy_predicated(T[:, h, :, :], mask(LV + l), b3(4 + h)).then_inc(*t_ready.up())
                        nc.vector.copy_predicated(U[:, h, :, :], mask(LVT + l), b3(h)).then_inc(*u_ready.up())
        self.close()

    def stage_rwkv_scan(self):
        nc, PS = self.nc, self.PS
        pre_mm, y_ready, p_ready, u0_mm, u0_ready, sa_mm, sa_ready, z_mm, z_ready, o_mm, o_ready, step = (self.sig(n) for n in (
            "rwkv_precomputed", "rwkv_y_ready", "rwkv_p_ready", "rwkv_u0_products", "rwkv_u0_ready", "rwkv_sa_products", "rwkv_sa_ready",
            "state_products", "state_ready", "chunk_output_products", "chunk_output_ready", "dve_steps"))
        U = self.area(self.RW_U, NHEAD, TT, P)
        MAK, MRB, MRK = (self.area(o, NHEAD, TT, P) for o in (self.RW_MAK, self.RW_MRB, self.RW_MRK))
        AT, BT, KT, VT, Y, U0, O = (self.area(o, TT, GROUP) for o in (self.RW_AT, self.RW_BT, self.RW_KT, self.RW_VT, self.RW_T1, self.RW_U0, self.RW_O))
        PT, Rt = self.area(self.RW_PT, 1024), self.area(self.RW_R, 1024)
        DEC = self.area(self.RW_SMALL, 8)
        Z = self.area(self.RW_Z, 3, GROUP)
        hs = lambda h: slice(h * HD, (h + 1) * HD)
        rows = lambda h: slice((h % 2) * HD, (h % 2) * HD + HD)
        js = lambda j: slice(j * P, (j + 1) * P)
        cols = lambda j, c: slice(j * SEQ + c * P, j * SEQ + (c + 1) * P)
        with nc.Block() as block:
            @block.tensor
            def _(pe):
                for c in range(TT):
                    for h in range(NHEAD):
                        nc.tensor.matmul(PS[:, c * GROUP + h * HD:c * GROUP + (h + 1) * HD], MAK[:, h, c, :], VT[:, c, hs(h)], start=True, stop=True)
                for c in range(TT):
                    for h in range(NHEAD):
                        o = 1024 + (h // 2) * SEQ + c * P
                        mm = nc.tensor.matmul(PS[rows(h), o:o + P], AT[:, c, hs(h)], U[:, h, c, :], start=True, stop=True)
                mm.then_inc(*pre_mm.up())
                pe.wait_ge(*y_ready.at(1))
                for c in range(TT):
                    for h in range(NHEAD):
                        o = 2048 + c * GROUP + h * HD
                        mm = nc.tensor.matmul(PS[:, o:o + HD], U[:, h, c, :], Y[:, c, hs(h)], start=True, stop=True)
                mm.then_inc(*u0_mm.up())
                pe.wait_ge(*p_ready.at(1))
                pe.wait_ge(*u0_ready.at(1))
                for c in range(TT):
                    if c > 0:
                        pe.wait_ge(*z_ready.at(c))
                        for j in range(2):
                            mm = nc.tensor.matmul(self.bank(6)[:, js(j)], PT[:, cols(j, c)], Z[:, c - 1, js(j)], start=True, stop=True)
                        mm.then_inc(*sa_mm.up())
                        pe.wait_ge(*sa_ready.at(c))
                    if c < TT - 1:
                        for j in range(2):
                            nc.tensor.matmul(self.bank(7)[:, js(j)], BT[:, c, js(j)], U0[:, c, js(j)], start=True, stop=False)
                            mm = nc.tensor.matmul(self.bank(7)[:, js(j)], KT[:, c, js(j)], VT[:, c, js(j)], start=False, stop=True)
                        mm.then_inc(*z_mm.up())
                    for h in range(NHEAD):
                        o = self.bank(c)[:, hs(h)]
                        nc.tensor.matmul(o, MRB[:, h, c, :], U0[:, c, hs(h)], start=True, stop=False)
                        mm = nc.tensor.matmul(o, MRK[:, h, c, :], VT[:, c, hs(h)], start=False, stop=c == 0)
                        if c > 0:
                            mm = nc.tensor.matmul(o, Rt[:, cols(h // 2, c)], Z[:, c - 1, hs(h)], start=False, stop=True)
                    mm.then_inc(*o_mm.up())

            @block.vector
            def _(dve):
                dve.wait_ge(*pre_mm.at(1))
                nc.vector.tensor_copy(Y.rearrange("p c n -> p (c n)"), PS[:, 0:1024]).then_inc(*y_ready.up())
                dve.wait_ge(*u0_mm.at(1))
                nc.vector.tensor_copy(U0.rearrange("p c n -> p (c n)"), PS[:, 2048:3072]).then_inc(*u0_ready.up())
                dve.wait_ge(*u0_ready.at(1))
                s = Steps(dve, step)
                for c in range(TT - 1):
                    if c > 0:
                        dve.wait_ge(*sa_mm.at(c))
                        nc.vector.tensor_tensor(U0[:, c, :], U0[:, c, :], self.bank(6, GROUP), ALU.add).then_inc(*sa_ready.up())
                    dve.wait_ge(*z_mm.at(c + 1))
                    if c == 0:
                        s.link(nc.vector.tensor_copy(Z[:, 0, :], self.bank(7, GROUP)))
                    else:
                        s.link(nc.vector.tensor_tensor(Z[:, c, :], Z[:, c - 1, :], self.bank(7, GROUP), ALU.add))
                    for j in range(2):
                        ins = nc.vector.scalar_tensor_tensor(Z[:, c, js(j)], Z[:, c, js(j)], DEC[:, j * TT + c:j * TT + c + 1], self.HSUM, ALU.mult, ALU.mult)
                        if j == 0:
                            s(ins)
                        else:
                            ins.then_inc(*z_ready.up())
                    dve.wait_ge(*z_ready.at(c + 1))
                    s.wait()
                dve.wait_ge(*sa_mm.at(TT - 1))
                nc.vector.tensor_tensor(U0[:, TT - 1, :], U0[:, TT - 1, :], self.bank(6, GROUP), ALU.add).then_inc(*sa_ready.up())

            @block.scalar
            def _(act):
                act.wait_ge(*pre_mm.at(1))
                nc.scalar.activation(PT, PS[:, 1024:2048], ACT.Copy).then_inc(*p_ready.up())
                for c in range(TT):
                    act.wait_ge(*o_mm.at(c + 1))
                    nc.scalar.activation(O[:, c, :], self.bank(c, GROUP), ACT.Copy).then_inc(*o_ready.up())
        self.close()

    def out_project(self, w):
        def copy_out(engine, u, t, b):
            y = self.H[:, t, u[1]:u[1] + u[3]]
            return self.nc.vector.scalar_tensor_tensor(y, y, ALPHA, self.bank(b, u[3]), ALU.mult, ALU.add)
        self.stage_stream(w, OUT_PIECES, OUT_UNITS, FT0, copy_out, engines=1)

    def stage_layer_norm(self, row_g, row_b, out=None):
        nc, H = self.nc, self.H
        G, Bb = self.area(0, D), self.area(D, D)
        st, mv, rs = self.area(2 * D, TT, 12), self.area(2 * D + 48, TT, 2), self.area(2 * D + 64, TT)
        loaded, var_ready, root_ready, step, normed = (self.sig(n) for n in ("gain_rows_loaded", "variance_ready", "root_ready", "dve_steps", "layer_normed"))
        with nc.Block() as block:
            @block.sync
            def _(sp):
                sp.dma_start(G, row_g.partition_broadcast(P)).then_inc(*loaded.up(16))
                sp.dma_start(Bb, row_b.partition_broadcast(P)).then_inc(*loaded.up(16))

            @block.vector
            def _(dve):
                s = Steps(dve, step)
                for t in range(TT):
                    for i in range(2):
                        s(nc.vector.bn_stats(st[:, t, 6 * i:6 * i + 6], H[:, t, i * HALF:(i + 1) * HALF]))
                s.wait()
                for t in range(TT):
                    s(nc.vector.bn_aggr(mv[:, t, :], st[:, t, :]))
                s.wait()
                nc.vector.tensor_scalar(rs, mv[:, :, 1:2].rearrange("p t n -> p (t n)"), LN_EPS, None, ALU.add).then_inc(*var_ready.up())
                dve.wait_ge(*root_ready.at(1))
                s.link(nc.vector.reciprocal(rs, rs))
                for t in range(TT):
                    s(nc.vector.tensor_scalar(H[:, t, :], H[:, t, :], mv[:, t, 0:1], rs[:, t:t + 1], ALU.subtract, ALU.mult))
                dve.wait_ge(*loaded.at(32))
                s.wait()
                for x, op in ((G, ALU.mult), (Bb, ALU.add)):
                    s.link(nc.vector.tensor_tensor(H, H, x.unsqueeze(1).broadcast_to([P, TT, D]), op))

            @block.scalar
            def _(act):
                act.wait_ge(*var_ready.at(1))
                nc.scalar.activation(rs, rs, ACT.Sqrt).then_inc(*root_ready.up())
        self.close()

    def stage_router(self, router):
        nc, SM = self.nc, self.SM
        rw = self.area(0, DT, N_EXPERTS)
        lg, pr, top, idx, idf = self.area(64, TT, 8), self.area(96, TT, 8), self.area(128, TT, 8), self.area(160, TT, 8), self.area(192, TT, 8)
        hot, hot2, mx, sm = self.area(224, TT, 8), self.area(256, TT, 8), self.area(288, TT, 1), self.area(292, TT, 1)
        gates = SM[:, 0:32].rearrange("p (t e) -> p t e", e=8)
        loaded, mms, centred, exped, step = (self.sig(n) for n in ("router_loaded", "router_products", "router_centred", "router_exped", "dve_steps"))
        bc = lambda x: x.broadcast_to([P, TT, 8])
        with nc.Block() as block:
            @block.sync
            def _(sp):
                sp.dma_start(rw, router.rearrange("(k p) e -> p k e", p=P)).then_inc(*loaded.up(16))

            @block.tensor
            def _(pe):
                pe.wait_ge(*loaded.at(16))
                for t in range(TT):
                    for k in range(DT):
                        mm = nc.tensor.matmul(self.PS[:, t * 8:(t + 1) * 8], self.HT[:, k, t * P:(t + 1) * P], rw[:, k, :], start=k == 0, stop=k == DT - 1)
                mm.then_inc(*mms.up())

            @block.vector
            def _(dve):
                s = Steps(dve, step)
                dve.wait_ge(*mms.at(1))
                s.link(nc.vector.tensor_copy(lg, self.PS[:, 0:32].rearrange("p (t e) -> p t e", e=8)))
                s.link(nc.vector.tensor_reduce(mx, lg, AX.X, ALU.max))
                nc.vector.tensor_tensor(lg, lg, bc(mx), ALU.subtract).then_inc(*centred.up())
                dve.wait_ge(*exped.at(1))
                s.link(nc.vector.tensor_reduce(sm, pr, AX.X, ALU.add))
                s.link(nc.vector.reciprocal(sm, sm))
                s.link(nc.vector.tensor_tensor(pr, pr, bc(sm), ALU.mult))
                for t in range(TT):
                    s(nc.vector.max(top[:, t, :], pr[:, t, :]))
                s.wait()
                for t in range(TT):
                    s(nc.vector.max_index(idx[:, t, :].bitcast(U32), top[:, t, :], pr[:, t, :]))
                s.wait()
                s.link(nc.vector.tensor_copy(idf, idx.bitcast(U32)))
                s.link(nc.vector.tensor_tensor(sm, top[:, :, 0:1], top[:, :, 1:2], ALU.add))
                s.link(nc.vector.reciprocal(sm, sm))
                iota = self.cf("iota8").unsqueeze(1).broadcast_to([P, TT, 8])
                for i, h in enumerate((hot, hot2)):
                    s.link(nc.vector.tensor_tensor(h, iota, bc(idf[:, :, i:i + 1]), ALU.is_equal))
                    s.link(nc.vector.tensor_tensor(h, h, bc(top[:, :, i:i + 1]), ALU.mult))
                s.link(nc.vector.tensor_tensor(hot, hot, hot2, ALU.add))
                s.link(nc.vector.tensor_tensor(gates, hot, bc(sm), ALU.mult))

            @block.scalar
            def _(act):
                act.wait_ge(*centred.at(1))
                nc.scalar.activation(pr, lg, ACT.Exp).then_inc(*exped.up())
        self.close()

    def block_one(self):
        ap = self.ap
        Y = self.HT.rearrange("p k t -> p (k t)").rearrange("p (t d) -> p t d", d=D)
        S = self.area(8192, 2048)
        Qc, KD, KT = self.area(10240, 1024), self.area(11264, 1024), self.area(12288, 1024)
        DEC, Z, O, kf = self.area(13312, 8), self.area(13320, 3, GROUP), self.area(14336, TT, GROUP), self.area(15360, 1024)
        SQ, g1, x1 = self.area(16384, TT, GROUP), self.area(17408, SEQ), self.area(17920, SEQ)
        ygrp = lambda m: Y[:, :, m * GROUP:(m + 1) * GROUP]
        row = lambda i: self.area(FT0 - 1024 + i * GROUP, GROUP)
        self.stage_to_feature(self.H, None, split=self.XR)
        for l in range(2):
            rows = ap["rows"]
            self.project(ap["w_in"][l], IN_PIECES, IN_UNITS, rows[l * 5 + 4], self.ft, self.tok)
            self.stage_hgrn_gates(l, kf)
            self.stage_decay_scores(self.ft(HQ, 2), kf, self.ft(HF, 2), 2, HD, S, Qc, KD, DEC, 0)
            self.stage_state(S, Qc, KD, DEC, self.tok(0), 2, HD, O, KT.rearrange("p (c n) -> p c n", n=GROUP), Z)
            self.stage_head_norm(O, SQ, self.tok(256), ygrp(0), RMS_EPS, gain=row(0))
            self.stage_gla_gates(l, g1, x1)
            self.stage_decay_scores(self.ft(GQ), self.ft(GK), g1, 1, 32, S, Qc[:, 0:SEQ], KD[:, 0:SEQ], DEC[:, 0:4], 0)
            self.stage_state(S, Qc, KD, DEC, self.tok(512), 1, 32, O, KT[:, 0:SEQ].rearrange("p (c n) -> p c n", n=P), Z)
            self.stage_head_norm(O, SQ, self.tok(768), ygrp(1), RMS_EPS, gain=row(1))
            self.stage_retention_scores(S, Qc, KD, DEC, 0)
            self.stage_state(S, Qc, KD, DEC, self.tok(1024), 2, HD, O, KT.rearrange("p (c n) -> p c n", n=GROUP), Z)
            self.stage_head_norm(O, SQ, self.tok(1280), ygrp(3), LN_EPS, center=True)
            self.stage_rwkv_gates(l)
            self.stage_rwkv_scores(l)
            self.stage_rwkv_solve()
            self.stage_rwkv_scan()
            self.stage_head_norm(self.area(self.RW_O, TT, GROUP), self.area(self.RW_T2, TT, GROUP), self.area(self.RW_G, TT, GROUP), ygrp(2), LNX_EPS,
                                 center=True, gain=row(2), bias=row(3), silu_gate=False,
                                 bonus=(self.area(self.RW_VT, TT, GROUP), self.area(self.RW_SMALL + 16, 16)))
            self.stage_to_feature(Y, None, split=self.XR)
            self.out_project(ap["w_out"][l])
            self.stage_layer_norm(rows[l * 5], rows[l * 5 + 1])
            if l == 0:
                self.stage_to_feature(self.H, None, src_factor=ALPHA, split=self.XR)
                split = lambda w: w.rearrange("d (e f) -> e d f", f=FPASS)
                gw, uw = split(ap["ffn_w_gate"][0]), split(ap["ffn_w_up"][0])
                dw = ap["ffn_w_down"][0].rearrange("(e f) d -> e f d", f=FPASS)
                self.stage_ffn(2, lambda i: gw[i], lambda i: uw[i], lambda i: dw[i])
            else:
                self.stage_to_feature(self.H, self.HT)
                self.stage_router(ap["moe_router"][0])
                self.stage_slots()
                gwm, uwm, dwm = ap["moe_w_gate"][0], ap["moe_w_up"][0], ap["moe_w_down"][0]
                self.stage_moe(lambda i, ahead=0: gwm[ahead:][i], lambda i, ahead=0: uwm[ahead:][i], lambda i: dwm[i])
            self.stage_layer_norm(rows[l * 5 + 2], rows[l * 5 + 3])
            if l == 0:
                self.stage_to_feature(self.H, None, split=self.XR)

    def stage_slots(self):
        nc, H, HR, SM = self.nc, self.H, self.HR, self.SM
        sel, selc, tri, ones = self.area(SLOT_TMP, TT, 8), self.area(SLOT_TMP + 32, TT, 8), self.area(SLOT_TMP + 64, P), self.area(SLOT_TMP + 192, P)
        tot, mx, nb = self.area(SLOT_TMP + 320, 8), self.area(SLOT_TMP + 328, 1), self.area(SLOT_TMP + 329, 1)
        gates = SM[:, 0:32].rearrange("p (t e) -> p t e", e=8)
        SVW = self.SVW
        step, rounded, ready, mms, iota_in = (self.sig(n) for n in ("dve_steps", "tokens_rounded", "slot_inputs_ready", "slot_products", "slot_iota_loaded"))
        FAR = -4096.0
        with nc.Block() as block:
            @block.sync
            def _(sp):
                sp.dma_start(self.IOTA, self.ap["slot_iota"].partition_broadcast(P)).then_inc(*iota_in.up(16))
                sp.wait_ge(*iota_in.at(16))

            @block.scalar
            def _(act):
                nc.scalar.activation(HR[:, 0], H, ACT.Copy).then_inc(*rounded.up())

            @block.vector
            def _(dve):
                s = Steps(dve, step)
                s.link(nc.vector.tensor_scalar(sel, gates, 0.0, None, ALU.is_gt))
                s(nc.vector.tensor_copy(tri, self.MASK[:, STRICT * P:(STRICT + 1) * P]))
                s(nc.vector.memset(ones, 1.0))
                s.link(nc.vector.memset(selc[:, 0, :], 0.0))
                for t in range(1, TT):
                    s.link(nc.vector.tensor_tensor(selc[:, t, :], selc[:, t - 1, :], sel[:, t - 1, :], ALU.add))
                nc.vector.tensor_tensor(tot, selc[:, TT - 1, :], sel[:, TT - 1, :], ALU.add).then_inc(*ready.up())
                dve.wait_ge(*rounded.at(1))
                s.link(nc.vector.tensor_tensor(HR[:, 1], H, HR[:, 0].bitcast(F32), ALU.subtract))
                s.link(nc.vector.tensor_scalar(H, H, ALPHA, None, ALU.mult))
                dve.wait_ge(*mms.at(1))
                s.link(nc.vector.tensor_reduce(mx, self.bank(1, 8), AX.X, ALU.max))
                s.link(nc.vector.memset(nb, 1.0))
                for b in range(1, NBLK):
                    s.link(nc.vector.scalar_tensor_tensor(nb, mx, float(b * CAP), nb, ALU.is_gt, ALU.add))
                s(nc.vector.tensor_copy(self.NBI, nb))
                s(nc.vector.memset(SVW, FAR))
                s.link(nc.vector.tensor_scalar(selc, self.bank(0, 32).rearrange("p (t e) -> p t e", e=8), -FAR, None, ALU.add))
                s.link(nc.vector.tensor_tensor(selc, selc, sel, ALU.mult))
                for b in range(NBLK):
                    s(nc.vector.tensor_scalar(SVW[:, :, b * 8:(b + 1) * 8], selc, FAR - b * CAP, None, ALU.add))

            @block.tensor
            def _(pe):
                pe.wait_ge(*ready.at(1))
                flat = lambda x: x.rearrange("p t e -> p (t e)")
                nc.tensor.matmul(self.bank(0, 32), tri, flat(sel), start=True, stop=False)
                nc.tensor.matmul(self.bank(0, 32), ones, flat(selc), start=False, stop=True)
                nc.tensor.matmul(self.bank(1, 8), ones, tot, start=True, stop=True).then_inc(*mms.up())
        self.close()

    def stage_moe(self, gate_w, up_w, down_w):
        nc, H, HR, HID, TMP, XE, PSEL, PT, YE = self.nc, self.H, self.HR, self.HIDS, self.TMP, self.XE, self.PSEL, self.PT, self.YE
        GSPL, DSPL, GRAW, DRAW, SM = self.GSPL, self.DSPL, self.GRAW, self.DRAW, self.SM
        N, E, DU = CAP, N_EXPERTS, 2 * FU
        gates = SM[:, 0:32].rearrange("p (t e) -> p t e", e=8)
        g_loaded = [self.sig(f"moe_gate_up_loaded{r}") for r in range(FRING)]
        d_loaded = [self.sig(f"moe_down_loaded{r}") for r in range(FRING)]
        g_mm, d_mm, halves = self.sig("moe_gate_up_products"), self.sig("moe_down_products"), self.sig("moe_part_sums_ready")
        (g_hi, g_lo, d_hi, d_lo, silu_done, prod_done, hid_hi, hid_lo, acc_done, pick_ready, pick_turned, pt_ready, gathered,
         x_hi, x_lo, y_hi, y_lo, scattered) = (self.sig("moe_" + n) for n in (
            "gate_up_hi_ready", "gate_up_lo_ready", "down_hi_ready", "down_lo_ready", "silu_done", "hidden_product_done", "hidden_hi_ready", "hidden_lo_ready",
            "sum_done", "pick_ready", "pick_turned", "scatter_matrix_ready", "gathered", "tokens_hi_ready", "tokens_lo_ready", "outputs_hi_ready", "outputs_lo_ready",
            "scattered"))
        uses = lambda L, r: len(range(r, L, FRING))
        TILES = (0, N - P)
        SBANK = (4, 5, 2, 3, 4, 5, 6, 7)
        XB = [(k // 3, (k % 3) * N) for k in range(DT)]

        def before(f, L):
            return f - FRING + 1 if f >= FRING else max(u for u in range(L) if u % FRING == f % FRING) - L + 1

        def wait(eng, w, c, L, k):
            eng.wait_ge(c.sem, c.base + w * L + k)

        def passes(eng, body):
            nb = eng.value_load(self.NBI[0:1, 0:1], min_val=1, max_val=NBLK)
            with eng.Fori(0, nb) as b:
                with eng.Fori(0, E) as e:
                    body(b * E + e, e)

        with nc.Block() as block:
            @block.sync
            def _(sp):
                def load_g(w, e, f, k=0, ahead=0):
                    for c in (g_hi, g_lo):
                        wait(sp, w, c, FU, before(f, FU) + k)
                    fill_g(e, f, ahead)

                def fill_g(e, f, ahead=0):
                    r = f % FRING
                    for u, wt in enumerate((gate_w, up_w)):
                        sp.dma_start(GRAW[:, r, u * D:(u + 1) * D].rearrange("p (k f) -> p k f", k=DT),
                                     wt(e, ahead)[:, f * P:(f + 1) * P].rearrange("(k p) f -> p k f", p=P)).then_inc(g_loaded[r].sem, 16)

                def load_d(w, e, n):
                    half, f = divmod(n, FU)
                    for c in (d_hi, d_lo):
                        wait(sp, w, c, DU, before(n, DU))
                    sp.dma_start(DRAW[:, n % FRING, :], down_w(e)[f * P:(f + 1) * P, half * HALF:(half + 1) * HALF]).then_inc(d_loaded[n % FRING].sem, 16)

                def body(w, e, after, ahead):
                    for f in range(FU):
                        load_d(w, e, f)
                        if f + 3 < FU:
                            load_g(w, e, f + 3)
                    for f in range(FU):
                        load_d(w, e, FU + f)
                        if f in (2, 5, 8):
                            load_g(w, after, f // 3, FU, ahead)

                for r in range(FRING):
                    fill_g(0, r)
                nb = sp.value_load(self.NBI[0:1, 0:1], min_val=1, max_val=NBLK)
                with sp.Fori(0, nb) as b:
                    with sp.Fori(0, E - 1) as e:
                        body(b * E + e, e, e, 1)
                    with sp.Fori(E - 1, E) as e:
                        body(b * E + e, e, 0, 0)

            @block.tensor
            def _(pe):
                def gather():
                    for k, (b, o) in enumerate(XB):
                        for t in range(TT):
                            for s in range(2):
                                mm = nc.tensor.matmul(self.bank(b)[:, o:o + N], HR[:, s, t, k * P:(k + 1) * P], PSEL[:, t, :],
                                                      start=t + s == 0, stop=t == TT - 1 and s == 1)
                    mm.then_inc(gathered.sem, 1)

                def gate_up(w, f, k=0):
                    wait(pe, w, g_hi, FU, f + 1 + k * FU)
                    wait(pe, w, g_lo, FU, f + 1 + k * FU)
                    if f >= 2:
                        wait(pe, w, halves, FU, f - 1)
                    else:
                        wait(pe, w, x_lo, 1, 1 + k)
                        wait(pe, w, acc_done, 2 * TT, -TT + k * 2 * TT)
                    r = f % FRING
                    for u in range(2):
                        out = self.bank(2 * (f % 2) + u, 2 * N)
                        for k8 in range(DT):
                            wt = [GSPL[:, r, s, (u * DT + k8) * P:(u * DT + k8 + 1) * P] for s in range(2)]
                            hi = lambda start, stop: nc.tensor.matmul(out, wt[0], XE[:, k8, :, :].rearrange("p s n -> p (s n)"), start=start, stop=stop)
                            lo = lambda: nc.tensor.matmul(out[:, N:2 * N], wt[1], XE[:, k8, 0, :], start=False, stop=False)
                            if k8 < DT - 1:
                                hi(k8 == 0, False)
                                lo()
                            else:
                                lo()
                                mm = hi(False, True)
                    mm.then_inc(g_mm.sem, 1)

                def down(w, n):
                    half, f = divmod(n, FU)
                    wait(pe, w, d_hi, DU, n + 1)
                    wait(pe, w, d_lo, DU, n + 1)
                    if half == 0:
                        wait(pe, w, hid_lo, FU, f + 1)
                    if f == 0:
                        wait(pe, w, acc_done, 2 * TT, 0)
                        wait(pe, w, pt_ready, 2, 2)
                    for j, s0 in enumerate(TILES):
                        x = [HID[:, s, f, s0:s0 + P] for s in range(2)]
                        wt = [DSPL[:, n % FRING, s, :] for s in range(2)]
                        out = self.bank(4 + 2 * half + j)
                        nc.tensor.matmul(out, x[0], wt[0], start=f == 0, stop=False)
                        nc.tensor.matmul(out, x[0], wt[1], start=False, stop=False)
                        mm = nc.tensor.matmul(out, x[1], wt[0], start=False, stop=f == FU - 1)
                    mm.then_inc(d_mm.sem, 1)

                def turn_pick(w):
                    wait(pe, w, acc_done, 2 * TT, 0)
                    for j, s0 in enumerate(TILES):
                        for t in range(TT):
                            mm = nc.tensor.transpose(self.bank(6 + j)[:, t * P:(t + 1) * P], PSEL[:, t, s0:s0 + P].bitcast(F32), self.cf("ident"))
                        mm.then_inc(pick_turned.sem, 1)

                def scatter(w, half):
                    wait(pe, w, y_lo, 2, half + 1)
                    for t in range(TT):
                        n = half * TT + t
                        if n in (4, 5):
                            wait(pe, w, acc_done, 2 * TT, n - 3)
                        if n in (2, 3):
                            wait(pe, w, x_lo, 1, 2)
                        for j in range(2):
                            for s in range(2):
                                mm = nc.tensor.matmul(self.bank(SBANK[n]), PT[:, j, t * P:(t + 1) * P], YE[:, s, j, half * HALF:(half + 1) * HALF],
                                                      start=j + s == 0, stop=j + s == 2)
                        mm.then_inc(scattered.sem, 1)

                def body(w, e):
                    for f in range(1, FU):
                        gate_up(w, f)
                        if f == 1:
                            turn_pick(w)
                        down(w, f - 1)
                    down(w, FU - 1)
                    wait(pe, w, pick_ready, 1, 2)
                    wait(pe, w, halves, FU, FU)
                    gather()
                    for f in range(FU):
                        down(w, FU + f)
                        if f == 6:
                            scatter(w, 0)
                    gate_up(w, 0, 1)
                    scatter(w, 1)

                pe.wait_ge(pick_ready.sem, pick_ready.base + 1)
                gather()
                gate_up(0, 0)
                passes(pe, body)

            @block.scalar
            def _(act):
                def split_g(w, f, k=0):
                    r = f % FRING
                    act.wait_ge(g_loaded[r].sem, g_loaded[r].base + 32 * (w * uses(FU, r) + f // FRING + 1) + 32 * k * uses(FU, r))
                    wait(act, w, g_mm, FU, before(f, FU) + k * FU)
                    nc.scalar.activation(GSPL[:, r, 0, :], GRAW[:, r, :], ACT.Copy).then_inc(g_hi.sem, 1)

                def split_d(w, n):
                    r = n % FRING
                    act.wait_ge(d_loaded[r].sem, d_loaded[r].base + 16 * (w * uses(DU, r) + n // FRING + 1))
                    wait(act, w, d_mm, DU, before(n, DU))
                    nc.scalar.activation(DSPL[:, r, 0, :], DRAW[:, r, :], ACT.Copy).then_inc(d_hi.sem, 1)

                def tokens_hi(count):
                    act.wait_ge(gathered.sem, count)
                    for b in range(3):
                        n = min(3, DT - 3 * b)
                        ins = nc.scalar.activation(XE[:, 3 * b:3 * b + n, 0, :], self.bank(b, n * N).rearrange("p (k n) -> p k n", n=N), ACT.Copy)
                    ins.then_inc(x_hi.sem, 1)

                def outputs_hi(w, half):
                    wait(act, w, d_mm, DU, (half + 1) * FU)
                    wait(act, w, scattered, 2 * TT, 0)
                    nc.scalar.activation(YE[:, 0, :, half * HALF:(half + 1) * HALF], self.PS[:, (4 + 2 * half) * HALF:(6 + 2 * half) * HALF].rearrange("p (j n) -> p j n", n=HALF),
                                         ACT.Copy).then_inc(y_hi.sem, 1)

                def body(w, e):
                    split_d(w, 0)
                    for f in range(FU):
                        wait(act, w, halves, FU, f + 1)
                        nc.scalar.activation(TMP[:, f % 2, 0:N], TMP[:, f % 2, 0:N], ACT.Silu).then_inc(silu_done.sem, 1)
                        wait(act, w, prod_done, FU, f + 1)
                        wait(act, w, d_mm, DU, 0)
                        nc.scalar.activation(HID[:, 0, f, :], TMP[:, f % 2, 0:N], ACT.Copy).then_inc(hid_hi.sem, 1)
                        if f == 1:
                            wait(act, w, pick_turned, 2, 2)
                            nc.scalar.activation(PT[:, 0, :], self.bank(6), ACT.Copy).then_inc(pt_ready.sem, 1)
                            nc.scalar.activation(PT[:, 1, :], self.bank(7), ACT.Copy, scale=self.cf("tail")).then_inc(pt_ready.sem, 1)
                        if f + 3 < FU:
                            split_g(w, f + 3)
                        split_d(w, f + 1)
                    split_d(w, FU + 1)
                    outputs_hi(w, 0)
                    tokens_hi(gathered.base + w + 2)
                    for f in range(2, FU):
                        split_d(w, FU + f)
                        if f in (4, 6, 8):
                            split_g(w, f // 2 - 2, 1)
                    outputs_hi(w, 1)

                tokens_hi(gathered.base + 1)
                for f in range(FRING):
                    split_g(0, f)
                passes(act, body)

            @block.vector
            def _(dve):
                def split_g(w, f, k=0):
                    r = f % FRING
                    wait(dve, w, g_hi, FU, f + 1 + k * FU)
                    nc.vector.tensor_tensor(GSPL[:, r, 1, :], GRAW[:, r, :], GSPL[:, r, 0, :].bitcast(F32), ALU.subtract).then_inc(g_lo.sem, 1)

                def split_d(w, n):
                    r = n % FRING
                    wait(dve, w, d_hi, DU, n + 1)
                    nc.vector.tensor_tensor(DSPL[:, r, 1, :], DRAW[:, r, :], DSPL[:, r, 0, :].bitcast(F32), ALU.subtract).then_inc(d_lo.sem, 1)

                def tokens_lo(count):
                    dve.wait_ge(x_hi.sem, count)
                    for b in range(3):
                        n = min(3, DT - 3 * b)
                        ins = nc.vector.tensor_tensor(XE[:, 3 * b:3 * b + n, 1, :], self.bank(b, n * N).rearrange("p (k n) -> p k n", n=N),
                                                      XE[:, 3 * b:3 * b + n, 0, :].bitcast(F32), ALU.subtract)
                    ins.then_inc(x_lo.sem, 1)

                def outputs_lo(w, half):
                    wait(dve, w, y_hi, 2, half + 1)
                    cols = slice(half * HALF, (half + 1) * HALF)
                    nc.vector.tensor_tensor(YE[:, 1, :, cols], self.PS[:, (4 + 2 * half) * HALF:(6 + 2 * half) * HALF].rearrange("p (j n) -> p j n", n=HALF),
                                            YE[:, 0, :, cols].bitcast(F32), ALU.subtract).then_inc(y_lo.sem, 1)

                def pick(at):
                    for t in range(TT):
                        ins = nc.vector.tensor_scalar(PSEL[:, t, :], self.IOTA, self.SVW[:, t, bass.ds(at, 1)], None, ALU.is_equal)
                    ins.then_inc(pick_ready.sem, 1)

                def add(w, e, n):
                    half, t = divmod(n, TT)
                    y = H[:, t, half * HALF:(half + 1) * HALF]
                    wait(dve, w, scattered, 2 * TT, n + 1)
                    wait(dve, w, acc_done, 2 * TT, n)
                    nc.vector.scalar_tensor_tensor(y, self.bank(SBANK[n]), gates[:, t, bass.ds(e, 1)], y, ALU.mult, ALU.add).then_inc(acc_done.sem, 1)

                def body(w, e):
                    for f in range(FU):
                        if f + 1 < FU:
                            split_g(w, f + 1)
                        split_d(w, f)
                        wait(dve, w, g_mm, FU, f + 1)
                        wait(dve, w, hid_lo, FU, f - 1)
                        nc.vector.tensor_reduce(TMP[:, f % 2, 0:2 * N].rearrange("p (u n) -> p u n", u=2),
                                                self.PS[:, 2 * (f % 2) * HALF:(2 * (f % 2) + 2) * HALF].rearrange("p (u c) -> p u c", u=2)[:, :, 0:2 * N]
                                                .rearrange("p u (s n) -> p u n s", s=2), AX.X, ALU.add).then_inc(halves.sem, 1)
                        wait(dve, w, silu_done, FU, f + 1)
                        nc.vector.tensor_tensor(TMP[:, f % 2, 0:N], TMP[:, f % 2, 0:N], TMP[:, f % 2, N:2 * N], ALU.mult).then_inc(prod_done.sem, 1)
                        wait(dve, w, hid_hi, FU, f + 1)
                        nc.vector.tensor_tensor(HID[:, 1, f, :], TMP[:, f % 2, 0:N], HID[:, 0, f, :].bitcast(F32), ALU.subtract).then_inc(hid_lo.sem, 1)
                        if f == 3:
                            wait(dve, w, pick_turned, 2, 2)
                            pick(w + 1)
                    split_d(w, FU)
                    split_d(w, FU + 1)
                    outputs_lo(w, 0)
                    tokens_lo(x_hi.base + w + 2)
                    for f in range(2, FU):
                        split_d(w, FU + f)
                        if f == 5:
                            split_g(w, 0, 1)
                        if f >= FU - 2:
                            add(w, e, 2 * (f - FU + 2))
                            add(w, e, 2 * (f - FU + 2) + 1)
                    outputs_lo(w, 1)
                    for n in range(TT, 2 * TT):
                        add(w, e, n)

                pick(0)
                tokens_lo(x_hi.base + 1)
                split_g(0, 0)
                passes(dve, body)
        self.close()

    def stage_begin_two(self):
        nc, ap = self.nc, self.ap
        loaded, copied = self.sig("inputs_loaded"), self.sig("residual_copied")
        with nc.Block() as block:
            @block.sync
            def _(sp):
                sp.dma_start(self.PAR[:, 0:64], ap["par2"]).then_inc(*loaded.up(16))
                sp.wait_ge(*loaded.at(16))

            @block.vector
            def _(dve):
                nc.vector.tensor_copy(self.X2, self.H).then_inc(*copied.up())
        self.close()

    def root_mean_square(self, dve, s, x, junk, ss, n, eps, var_ready, root_ready, factor=1.0):
        nc = self.nc
        s.link(nc.vector.tensor_tensor(junk, x, x, ALU.mult))
        s.link(nc.vector.tensor_reduce(ss, junk, AX.X, ALU.add))
        nc.vector.tensor_scalar(ss, ss, 1.0 / n, eps, ALU.mult, ALU.add).then_inc(*var_ready.up())
        dve.wait_ge(*root_ready.at(1))
        s.link(nc.vector.reciprocal(ss, ss))
        if factor != 1.0:
            s.link(nc.vector.tensor_scalar(ss, ss, factor, None, ALU.mult))

    def stage_pre_norm(self):
        nc, H, X2 = self.nc, self.H, self.X2
        ss = self.SM[:, 64:68]
        step, var_ready, root_ready = (self.sig(n) for n in ("dve_steps", "variance_ready", "root_ready"))
        with nc.Block() as block:
            @block.vector
            def _(dve):
                s = Steps(dve, step)
                self.root_mean_square(dve, s, X2, H, ss.unsqueeze(2), D, RMS_EPS, var_ready, root_ready)
                for t in range(TT):
                    s(nc.vector.tensor_scalar(H[:, t, :], X2[:, t, :], ss[:, t:t + 1], None, ALU.mult))

            @block.scalar
            def _(act):
                act.wait_ge(*var_ready.at(1))
                nc.scalar.activation(ss, ss, ACT.Sqrt).then_inc(*root_ready.up())
        self.close()

    def stage_post_norm(self, row, factor):
        nc, H, X2 = self.nc, self.H, self.X2
        ss, G = self.SM[:, 64:68], self.area(0, D)
        step, var_ready, root_ready, loaded = (self.sig(n) for n in ("dve_steps", "variance_ready", "root_ready", "gain_rows_loaded"))
        with nc.Block() as block:
            @block.sync
            def _(sp):
                sp.dma_start(G, row.partition_broadcast(P)).then_inc(*loaded.up(16))

            @block.vector
            def _(dve):
                s = Steps(dve, step)
                self.root_mean_square(dve, s, H, self.area(4096, TT, D), ss.unsqueeze(2), D, RMS_EPS, var_ready, root_ready, factor)
                dve.wait_ge(*loaded.at(16))
                for t in range(TT):
                    s(nc.vector.scalar_tensor_tensor(H[:, t, :], H[:, t, :], ss[:, t:t + 1], G, ALU.mult, ALU.mult))
                s.wait()
                s(nc.vector.tensor_tensor(X2, X2, H, ALU.add))

            @block.scalar
            def _(act):
                act.wait_ge(*var_ready.at(1))
                nc.scalar.activation(ss, ss, ACT.Sqrt).then_inc(*root_ready.up())
        self.close()

    def stage_lru(self, YT, rl):
        nc, ap, PS = self.nc, self.ap, self.PS
        x, gate = (self.ft(i, 4).rearrange("p (j t) -> p j t", t=SEQ) for i in (L2X, L2G))
        xc, r, ig, th, u, h = (self.area(o, 4, SEQ) for o in (0, 2048, 4096, 6144, 8192, 12288))
        Wr, Wi = self.area(10240, 4, P), self.area(10752, 4, P)
        ls, l1, ones = self.area(11264, 4), self.area(11268, 4), self.area(11272, 1)
        zeroed, loaded, step, astep, conv_ready, mms, gates, lam_ready, logits, th_ready, var_ready, root_ready, gelu_ready, sq_ready, sum_mm = (self.sig(n) for n in (
            "lru_weights_zeroed", "lru_weights_loaded", "dve_steps", "act_steps", "lru_conv_ready", "lru_gate_products", "lru_gates_ready",
            "lru_lambda_ready", "lru_log_a_ready", "lru_tanh_ready", "lru_square_ready", "lru_root_ready", "lru_gelu_ready", "lru_squares_ready", "lru_square_sums"))
        col = lambda base, j: self.PAR[:, base + j:base + j + 1]
        with nc.Block() as block:
            @block.gpsimd
            def _(pool):
                for w in (Wr, Wi):
                    nc.gpsimd.memset(w, 0.0).then_inc(*zeroed.up())

            @block.sync
            def _(sp):
                sp.wait_ge(*zeroed.at(2))
                for w, name in ((Wr, "w_rg_2"), (Wi, "w_ig_2")):
                    src = ap[name][0].rearrange("(j b) i o -> b i j o", b=2)
                    for b in range(2):
                        a = slice(b * HD, (b + 1) * HD)
                        sp.dma_start(w[a, :, a], src[b]).then_inc(*loaded.up(16))

            @block.vector
            def _(dve):
                s = Steps(dve, step)
                for j in range(4):
                    s(nc.vector.tensor_scalar(xc[:, j, :], x[:, j, :], col(CONV_W + 12, j), col(CONV_B, j), ALU.mult, ALU.add))
                for d in range(1, 4):
                    s.wait()
                    for j in range(4):
                        ins = nc.vector.scalar_tensor_tensor(xc[:, j, d:SEQ], x[:, j, 0:SEQ - d], col(CONV_W + 4 * (3 - d), j), xc[:, j, d:SEQ], ALU.mult, ALU.add)
                        if d == 3:
                            ins.then_inc(*conv_ready.up())
                        else:
                            s(ins)
                lam = self.PAR[:, LAM:LAM + 4]
                s.link(nc.vector.tensor_scalar(l1, lam, 0.0, None, ALU.min))
                dve.wait_ge(*lam_ready.at(1))
                s.link(nc.vector.tensor_tensor(ls, l1, ls, ALU.subtract))
                s.link(nc.vector.tensor_scalar(ls, ls, -4.0, None, ALU.mult))
                s.link(nc.vector.memset(ones, 1.0))
                for j in range(4):
                    dve.wait_ge(*gates.at(2 * j + 1))
                    nc.vector.tensor_scalar(th[:, j, :], r[:, j, :], ls[:, j:j + 1], None, ALU.mult).then_inc(*logits.up())
                dve.wait_ge(*gates.at(8))
                s.link(nc.vector.tensor_tensor(u, ig, xc, ALU.mult))
                dve.wait_ge(*th_ready.at(4))
                s.link(nc.vector.tensor_scalar(r, th, 1.0, None, ALU.add))
                s.link(nc.vector.reciprocal(r, r))
                s.link(nc.vector.tensor_tensor(th, th, r, ALU.mult))
                s.link(nc.vector.tensor_scalar(th, th, 2.0, None, ALU.mult))
                s.link(nc.vector.tensor_scalar(r, th, -1.0, 1.0, ALU.mult, ALU.add))
                nc.vector.scalar_tensor_tensor(th, r, 1.0, th, ALU.add, ALU.mult).then_inc(*var_ready.up())
                dve.wait_ge(*root_ready.at(1))
                s.link(nc.vector.tensor_tensor(u, u, th, ALU.mult))
                for j in range(4):
                    s(nc.vector.tensor_tensor_scan(h[:, j, :], r[:, j, :], u[:, j, :], 0.0, ALU.mult, ALU.add))
                s.wait()
                dve.wait_ge(*gelu_ready.at(1))
                s.link(nc.vector.tensor_tensor(h, h, gate, ALU.mult))
                nc.vector.tensor_tensor(th, h, h, ALU.mult).then_inc(*sq_ready.up())
                for j in range(4):
                    s(nc.vector.tensor_scalar(YT[:, j, :], h[:, j, :], col(G_OUT, j), None, ALU.mult))
                dve.wait_ge(*sum_mm.at(1))
                nc.vector.tensor_scalar(rl, PS[:, 0:TT], 1.0 / 512, RMS_EPS, ALU.mult, ALU.add).then_inc(*var_ready.up())
                dve.wait_ge(*root_ready.at(2))
                s(nc.vector.reciprocal(rl, rl))

            @block.scalar
            def _(act):
                s = Steps(act, astep)
                s.link(nc.scalar.activation(ls, self.PAR[:, LAM:LAM + 4], ACT.Abs))
                s.link(nc.scalar.activation(ls, ls, ACT.Exp, scale=-1.0))
                nc.scalar.activation(ls, ls, ACT.Ln, bias=1.0).then_inc(*lam_ready.up())
                for j in range(4):
                    act.wait_ge(*mms.at(j + 1))
                    nc.scalar.activation(r[:, j, :], self.bank(2 * j), ACT.Sigmoid, bias=col(B_RG, j)).then_inc(*gates.up())
                    nc.scalar.activation(ig[:, j, :], self.bank(2 * j + 1), ACT.Sigmoid, bias=col(B_IG, j)).then_inc(*gates.up())
                for j in range(4):
                    act.wait_ge(*logits.at(j + 1))
                    nc.scalar.activation(th[:, j, :], th[:, j, :], ACT.Tanh).then_inc(*th_ready.up())
                nc.scalar.activation(gate, gate, ACT.Gelu_apprx_tanh).then_inc(*gelu_ready.up())
                act.wait_ge(*var_ready.at(1))
                nc.scalar.activation(th, th, ACT.Sqrt).then_inc(*root_ready.up())
                act.wait_ge(*var_ready.at(2))
                nc.scalar.activation(rl, rl, ACT.Sqrt).then_inc(*root_ready.up())

            @block.tensor
            def _(pe):
                pe.wait_ge(*loaded.at(64))
                for j in range(4):
                    pe.wait_ge(*conv_ready.at(j + 1))
                    nc.tensor.matmul(self.bank(2 * j), Wr[:, j, :], xc[:, j, :], start=True, stop=True)
                    nc.tensor.matmul(self.bank(2 * j + 1), Wi[:, j, :], xc[:, j, :], start=True, stop=True).then_inc(*mms.up())
                pe.wait_ge(*sq_ready.at(1))
                for t in range(TT):
                    for j in range(4):
                        mm = nc.tensor.matmul(PS[:, t:t + 1], th[:, j, t * P:(t + 1) * P], ones, start=j == 0, stop=j == 3)
                mm.then_inc(*sum_mm.up())
        self.close()

    def stage_attention(self, YT, ra):
        nc, ap, PS = self.nc, self.ap, self.PS
        q, k = self.ft(L2Q, 4), self.ft(L2K, 2)
        V = self.area(TOK0, TT, P)
        S, PT = self.area(14336, QH, 256), self.area(16384, QH * 256)
        MA, snk, mx, dn = self.area(18432, 256), self.area(18688, QH), self.area(18696, QH), self.area(18704, QH)
        O, SQ = self.area(18944, TT, 512), self.area(12288, TT, 512)
        loaded, step, mms, p_in, p_out, turned, pt_ready, o_mm, o_ready, var_ready, root_ready, y_mm, y_ready = (self.sig(n) for n in (
            "attention_tables_loaded", "dve_steps", "score_products", "softmax_centred", "softmax_exped", "probabilities_turned", "probabilities_ready",
            "chunk_output_products", "chunk_output_ready", "variance_ready", "root_ready", "attention_turned", "attention_feature_ready"))
        slot = lambda h: 2 * (2 * (h // 4) + h % 2) + (h % 4) // 2
        bc = lambda x, n: x.unsqueeze(2).broadcast_to([P, QH, n])
        with nc.Block() as block:
            @block.sync
            def _(sp):
                sp.dma_start(MA, ap["window"]).then_inc(*loaded.up(16))
                sp.dma_start(snk, ap["rows"][13, 0:QH].partition_broadcast(P)).then_inc(*loaded.up(16))

            @block.tensor
            def _(pe):
                for n in range(TT):
                    w0 = P if n == 0 else 0
                    if n > 0:
                        pe.wait_ge(*o_ready.at(n))
                    for h in range(QH):
                        rr = slice((h % 2) * HD, (h % 2) * HD + HD)
                        o = slot(h) * 256
                        mm = nc.tensor.matmul(PS[:, o + w0:o + 256], q[rr, (h // 2) * SEQ + n * P:(h // 2) * SEQ + (n + 1) * P],
                                              k[rr, (h // 4) * SEQ + (n - 1) * P + w0:(h // 4) * SEQ + (n + 1) * P], start=True, stop=True)
                    mm.then_inc(*mms.up())
                    pe.wait_ge(*p_out.at(2 * n + 1))
                    for h in range(QH):
                        for b in range(w0 // P, 2):
                            mm = nc.tensor.transpose(PS[:, 2048 + (2 * h + b) * P:2048 + (2 * h + b + 1) * P], S[:, slot(h), b * P:(b + 1) * P], self.cf("ident"))
                    mm.then_inc(*turned.up())
                    pe.wait_ge(*pt_ready.at(n + 1))
                    for h in range(QH):
                        kv = h // 4
                        for b in range(w0 // P, 2):
                            mm = nc.tensor.matmul(PS[:, slot(h) * HD:(slot(h) + 1) * HD], PT[:, (2 * h + b) * P:(2 * h + b + 1) * P],
                                                  V[:, n - 1 + b, kv * HD:(kv + 1) * HD], start=b == w0 // P, stop=b == 1)
                    mm.then_inc(*o_mm.up())
                pe.wait_ge(*o_ready.at(TT))
                for j in range(4):
                    for t in range(TT):
                        mm = nc.tensor.transpose(PS[:, 2048 + j * HALF + t * P:2048 + j * HALF + (t + 1) * P], O[:, t, j * P:(j + 1) * P], self.cf("ident"))
                    mm.then_inc(*y_mm.up())

            @block.scalar
            def _(act):
                for n in range(TT):
                    w0 = P if n == 0 else 0
                    act.wait_ge(*p_in.at(n + 1))
                    nc.scalar.activation(S[:, :, w0:256], S[:, :, w0:256], ACT.Exp).then_inc(*p_out.up())
                    nc.scalar.activation(mx, mx, ACT.Exp).then_inc(*p_out.up())
                    act.wait_ge(*turned.at(n + 1))
                    v = lambda x: x.rearrange("p (h w) -> p h w", w=256)[:, :, w0:256]
                    nc.scalar.activation(v(PT), v(PS[:, 2048:4096]), ACT.Copy).then_inc(*pt_ready.up())
                for j in range(4):
                    act.wait_ge(*y_mm.at(j + 1))
                    nc.scalar.activation(YT[:, 4 + j, :], self.bank(4 + j), ACT.Copy, scale=self.PAR[:, G_OUT + 4 + j:G_OUT + 5 + j]).then_inc(*y_ready.up())
                act.wait_ge(*var_ready.at(1))
                nc.scalar.activation(ra, ra, ACT.Sqrt).then_inc(*root_ready.up())

            @block.vector
            def _(dve):
                s = Steps(dve, step)
                dve.wait_ge(*loaded.at(32))
                for n in range(TT):
                    w0 = P if n == 0 else 0
                    w = 256 - w0
                    dve.wait_ge(*mms.at(n + 1))
                    s.link(nc.vector.scalar_tensor_tensor(S[:, :, w0:256], PS[:, 0:2048].rearrange("p (h w) -> p h w", w=256)[:, :, w0:256], HD ** -0.5,
                                                          MA[:, w0:256].unsqueeze(1).broadcast_to([P, QH, w]), ALU.mult, ALU.add))
                    s.link(nc.vector.tensor_reduce(mx, S[:, :, w0:256], AX.X, ALU.max))
                    v = lambda x: x.rearrange("p (a r q) -> p a r q", r=2, q=2)
                    sv = snk.rearrange("p (a q r) -> p a r q", r=2, q=2)
                    s.link(nc.vector.tensor_tensor(v(mx), v(mx), sv, ALU.max))
                    s.link(nc.vector.tensor_tensor(S[:, :, w0:256], S[:, :, w0:256], bc(mx, w), ALU.subtract))
                    nc.vector.tensor_tensor(v(mx), sv, v(mx), ALU.subtract).then_inc(*p_in.up())
                    dve.wait_ge(*p_out.at(2 * n + 2))
                    s.link(nc.vector.tensor_reduce(dn, S[:, :, w0:256], AX.X, ALU.add))
                    s.link(nc.vector.tensor_tensor(dn, dn, mx, ALU.add))
                    s.link(nc.vector.reciprocal(dn, dn))
                    dve.wait_ge(*o_mm.at(n + 1))
                    o3 = O[:, n, :].rearrange("p (a q r e) -> p a q r e", q=2, r=2, e=HD)
                    src, dv = PS[:, 0:512].rearrange("p (a r q e) -> p a r q e", r=2, q=2, e=HD), v(dn)
                    for a in range(2):
                        for rr in range(2):
                            ins = nc.vector.tensor_tensor(o3[:, a, :, rr, :], src[:, a, rr, :, :], dv[:, a, rr, :].unsqueeze(2).broadcast_to([P, 2, HD]), ALU.mult)
                            if a + rr < 2:
                                s(ins)
                    ins.then_inc(*o_ready.up())
                    dve.wait_ge(*o_ready.at(n + 1))
                self.root_mean_square(dve, s, O, SQ, ra.unsqueeze(2), 512, RMS_EPS, var_ready, root_ready)
        self.close()

    def out_two(self, w, rl, ra):
        nc = self.nc

        def copy_out(engine, u, t, b):
            y, n = self.H[:, t, u[1]:u[1] + u[3]], u[3]
            step = self.sig("dve_steps")
            nc.vector.tensor_scalar(y, self.bank(b, n), rl[:, t:t + 1], None, ALU.mult).then_inc(*step.up())
            nc.vector.wait_ge(*step.at(step.sent))
            return nc.vector.scalar_tensor_tensor(y, self.bank(b)[:, n:2 * n], ra[:, t:t + 1], y, ALU.mult, ALU.add)
        self.stage_stream(w, OUT_PIECES, OUT_UNITS, FT0, copy_out, parts=2, engines=1)

    def stage_split(self, x):
        nc, XR = self.nc, self.XR
        rounded, rest = self.sig("x_rounded"), self.sig("x_rest_ready")
        with nc.Block() as block:
            @block.scalar
            def _(act):
                for k in range(DT):
                    nc.scalar.activation(XR[:, 0, k, :], x[:, k, :], ACT.Copy).then_inc(*rounded.up())

            @block.vector
            def _(dve):
                for k in range(DT):
                    dve.wait_ge(*rounded.at(k + 1))
                    nc.vector.tensor_tensor(XR[:, 1, k, :], x[:, k, :], XR[:, 0, k, :].bitcast(F32), ALU.subtract).then_inc(*rest.up())
        self.close()

    def stage_store(self):
        nc, stored = self.nc, self.sig("output_stored")
        with nc.Block() as block:
            @block.sync
            def _(sp):
                sp.dma_start(self.ap["out"][0].rearrange("(t p) d -> p t d", p=P), self.X2).then_inc(*stored.up(16))
                sp.wait_ge(*stored.at(16))
        self.close()

    def block_two(self):
        ap, H, HT = self.ap, self.H, self.HT
        self.X2 = self.B[:, 0:TT * D].rearrange("p (t d) -> p t d", d=D)
        col = lambda base: (lambda k: self.PAR[:, base + k:base + k + 1])
        rows = ap["rows"]
        YT = self.area(TOK0 + 512, DT, SEQ)
        rl, ra = self.SM[:, 72:76], self.SM[:, 76:80]

        def feed_forward(pre, w_gu, w_down, row):
            self.stage_pre_norm()
            self.stage_to_feature(H, None, scale=col(pre), src_factor=0.0, split=self.XR)
            gu = w_gu.rearrange("d (u e f) -> u e d f", u=2, f=FPASS)
            dw = w_down.rearrange("(e f) d -> e f d", f=FPASS)
            self.stage_ffn(2, lambda i: gu[0][i], lambda i: gu[1][i], lambda i: dw[i])
            self.stage_post_norm(rows[row], 0.5)

        self.stage_begin_two()
        feed_forward(PRE1, ap["ffn1_w_gu_2"][0], ap["ffn1_w_down_2"][0], 10)
        self.stage_pre_norm()
        self.stage_to_feature(H, None, scale=col(PRE_MIX), split=self.XR)
        self.project(ap["w_in_2"][0], IN2_PIECES, IN2_UNITS, None, self.ft, lambda c, n: self.area(TOK0, TT, P)[:, :, c:c + n])
        self.stage_lru(YT, rl)
        self.stage_attention(YT, ra)
        self.stage_split(YT)
        self.out_two(ap["w_o_2"][0], rl, ra)
        self.stage_post_norm(rows[11], 1.0)
        feed_forward(PRE2, ap["ffn2_w_gu_2"][0], ap["ffn2_w_down_2"][0], 12)
        self.stage_store()


def shape_constants():
    ar = np.arange(P)
    j, i = ar[:, None], ar[None, :]
    cf = np.zeros((P, NCF), np.float32)
    put = lambda name, v: cf.__setitem__((slice(None), slice(CF[name][0], CF[name][0] + CF[name][1])), v)
    put("ident", np.eye(P))
    for t in range(2):
        for h in range(NHEAD):
            cf[:, CF["headcol"][0] + 4 * t + h] = (ar // HD + 2 * t) == h
    cf[:, CF["invf"][0]] = np.float32(10000.0) ** (-(ar % 32).astype(np.float32) / np.float32(32))
    put("iota8", np.broadcast_to(np.arange(8), (P, 8)))
    put("tail", (ar >= 2 * P - CAP)[:, None])
    ci = np.zeros((P, NCI, P), np.int32)
    for l in range(LEVELS):
        s = 1 << l
        m = (j // (2 * s) == i // (2 * s)) & (j % (2 * s) < s) & (i % (2 * s) >= s)
        ci[:, LVT + l], ci[:, LV + l] = m, m.T
    ci[:, DIAG], ci[:, INCL], ci[:, STRICT] = i == j, j <= i, j < i
    cg = np.zeros((P, 512), np.float32)
    for m in range(P):
        if m % HD < 32:
            cg[m + 32, m] = -1.0
        else:
            cg[m - 32, m] = 1.0
    cg[:, P:2 * P] = (j // HD) == (i // HD)
    cg[:, 2 * P:] = (j // 32) == (np.arange(256)[None, :] // HD)
    rc = np.zeros((P, NRET), np.float64)
    lg = np.log(1.0 - 2.0 ** (-5.0 - np.arange(NHEAD)))
    for h in range(NHEAD):
        rc[:, RET_D + h * P:RET_D + (h + 1) * P] = np.where(j <= i, np.exp(np.minimum((i - j), P) * lg[h] * (j <= i)), 0.0)
    for t in range(2):
        g = lg[ar // HD + 2 * t][:, None]
        rc[:, RET_Q + t * P:RET_Q + (t + 1) * P] = np.exp((i + 1) * g)
        rc[:, RET_K + t * P:RET_K + (t + 1) * P] = np.exp((P - 1 - i) * g)
        rc[:, RET_C + t:RET_C + t + 1] = np.exp(P * g)
    kj, qi = np.arange(256)[None, :], j
    window = np.where((qi + P - kj >= 0) & (qi + P - kj < P), 0.0, -1e30).astype(np.float32)
    return {"window": window, "slot_iota": np.arange(CAP, dtype=np.float32), "const_f": cf, "const_i": ci.reshape(P, NCI * P), "const_g": cg, "ret_c": rc.astype(np.float32)}


def columns(v, n):
    v = np.asarray(v, np.float32).reshape(-1)
    out = np.zeros(n * P, np.float32)
    out[:v.size] = v
    return out.reshape(n, P).T


def packed(inputs):
    g = lambda n: np.asarray(inputs[n])
    par = []
    for l in range(2):
        src = {"lb0": g("hgrn_lb_logits")[0], "lb1": g("hgrn_lb_logits")[1], "gate_b": g("gla_gate_b")[l], "mu": g("rwkv_mu")[l],
               "w0": g("rwkv_w0")[l], "a0": g("rwkv_a0")[l], "k_k": g("rwkv_k_k")[l], "k_a": g("rwkv_k_a")[l],
               "r_k": g("rwkv_r_k")[l], "v0": g("rwkv_v0")[0]}
        par += [columns(src[n], PAR[n][1]) for n in PAR]
    rows = []
    for l in range(2):
        rows += [g("ln1_g")[l], g("ln1_b")[l], g("ln2_g")[l], g("ln2_b")[l],
                 np.concatenate([np.tile(g("hgrn_norm_g")[l], NHEAD), np.tile(g("gla_norm_g")[l], NHEAD), g("rwkv_lnx_g")[l], g("rwkv_lnx_b")[l]])]
    rows += [g("ffn1_post_g_2")[0], g("mix_post_g_2")[0], g("ffn2_post_g_2")[0], np.tile(g("sinks_2")[0], P)]
    par2 = [columns(g(n)[0], 8) for n in ("ffn1_pre_g_2", "mix_pre_g_2", "ffn2_pre_g_2")]
    par2.append(columns(np.concatenate([g("g_lru_out_2")[0], g("g_attn_out_2")[0]]), 8))
    par2 += [columns(g("conv_w_2")[0, i], 4) for i in range(4)]
    par2 += [columns(g(n)[0], 4) for n in ("conv_b_2", "b_rg_2", "b_ig_2", "lru_lambda_2")]
    return {"par": np.concatenate(par, 1), "rows": np.stack(rows), "par2": np.concatenate(par2, 1)}


BIG = ["x", "positions", "w_in", "w_out", "gla_gate_w2", "rwkv_w2", "rwkv_a2", "rwkv_g2", "rwkv_v1", "rwkv_v2",
       "ffn_w_gate", "ffn_w_up", "ffn_w_down", "moe_router", "moe_w_gate", "moe_w_up", "moe_w_down",
       "ffn1_w_gu_2", "ffn1_w_down_2", "w_in_2", "w_rg_2", "w_ig_2", "w_o_2", "ffn2_w_gu_2", "ffn2_w_down_2"]


def laid_out(inputs):
    arrays = {n: np.ascontiguousarray(inputs[n]) for n in BIG}
    arrays.update({n: np.ascontiguousarray(a) for n, a in {**shape_constants(), **packed(inputs)}.items()})
    return arrays


def build(nc, ap):
    k = Kernel(nc, ap)
    k.stage_load()
    k.block_one()
    k.block_two()


def kernel(**inputs):
    import concourse.bacc as bacc
    from concourse.bass_utils import run_bass_kernel_spmd

    nc = bacc.Bacc("TRN2", target_bir_lowering=False, num_devices=1)
    arrays, ap = {}, {}
    for name, a in laid_out(inputs).items():
        arrays[f"in_{name}"] = a
        ap[name] = nc.dram_tensor(f"in_{name}", a.shape, mybir.dt.from_np(a.dtype), kind="ExternalInput").ap()
    ap["out"] = nc.dram_tensor("out_0", (1, SEQ, D), F32, kind="ExternalOutput").ap()
    build(nc, ap)
    r = run_bass_kernel_spmd(nc, [arrays], core_ids=[0])
    return r.results[0]["out_0"]
```

```python
import numpy as np
import concourse.bass as bass
from concourse import mybir

F32 = mybir.dt.float32
I32 = mybir.dt.int32
U32 = mybir.dt.uint32
ACT = mybir.ActivationFunctionType
ALU = mybir.AluOpType
AX = mybir.AxisListType

P = 128
SEQ = 512
D = 1024
TT = SEQ // P
DT = D // P
HALF = 512
GROUP = 256
NHEAD = 4
HD = 64
LEVELS = 7
FU = 11
FPASS = FU * P
N_EXPERTS = 8
ALPHA = 4.0 ** 0.25
LN_EPS = 1e-5
RMS_EPS = 1e-6
LNX_EPS = 64e-5
EXP_NEG_HALF = float(np.exp(-0.5))

IN_COLS = 3888
HQ, HF, GQ, GK, GLR, RR, RK, RV, RWA, RG, RQ, RKK = 0, 2, 4, 5, 6, 7, 9, 11, 13, 14, 16, 18
two_tiles = lambda tile: [("F", tile, 0, 128), ("F", tile + 1, 128, 128)]
IN_PIECES = [[(0, 256)], [(256, 256)], [(512, 256)], [(768, 256)], [(1024, 256)], [(1280, 272)], [(1552, 256)],
             [(1808, 256)], [(2064, 256)], [(2320, 256)], [(2576, 288)], [(2864, 256)], [(3120, 256)], [(3376, 256)], [(3632, 256)]]
IN_UNITS = [two_tiles(HQ), two_tiles(HF), [("T", 0, 0, 256)], [("T", 256, 0, 256)], two_tiles(GQ),
            [("T", 512, 0, 256), ("F", GLR, 256, 16)], [("T", 768, 0, 256)], two_tiles(RR), two_tiles(RK), two_tiles(RV),
            two_tiles(RWA) + [("F", RG + 1, 256, 32)], two_tiles(RQ), two_tiles(RKK), [("T", 1024, 0, 256)], [("T", 1280, 0, 256)]]
PW = 288
PRAW, PSPL = 2, 3
NFT = 20
L2X, L2G, L2Q, L2K = 0, 4, 8, 12
IN2_PIECES = [[(256 * i, 256)] for i in range(6)] + [[(1536, 64), (1536, 64), (1600, 64), (1600, 64)], [(1664, 128)]]
IN2_UNITS = [two_tiles(2 * i) for i in range(7)] + [[("T", 0, 0, 128)]]
OUT_PIECES = [[(256 * i, 256)] for i in range(4)]
OUT_UNITS = [[("T", 256 * i, 0, 256)] for i in range(4)]
QH = 8
PRE1, PRE_MIX, PRE2, G_OUT, CONV_W, CONV_B, B_RG, B_IG, LAM = 0, 8, 16, 24, 32, 48, 52, 56, 60
TOKW = 1536

PAR = {}
for _name, _n in (("lb0", 2), ("lb1", 2), ("gate_b", 1), ("mu", 9), ("w0", 2), ("a0", 2), ("k_k", 2), ("k_a", 2), ("r_k", 2), ("v0", 2)):
    PAR[_name] = (sum(n for _, n in PAR.values()), _n)
NPAR = sum(n for _, n in PAR.values())

SCR = 39424
FT0 = 23040
TOK0 = FT0 + NFT * SEQ
HT0 = TOK0 + TT * TOKW
ARENA = 44672
WSP0 = 2 * DT * SEQ
assert TOK0 + TT * TOKW == SCR and WSP0 + PSPL * 2 * DT * PW <= FT0 - D and HT0 + PRAW * DT * PW <= ARENA
FRING = 3
XR0 = 0
HID0 = XR0 + 2 * DT * SEQ
GRAW0 = HID0 + 2 * FU * SEQ
GSPL0 = GRAW0 + FRING * 2 * D
DRAW0 = GSPL0 + FRING * 4 * D
DSPL0 = DRAW0 + FRING * HALF
TMP0 = DSPL0 + FRING * 2 * HALF
assert TMP0 + 2 * SEQ <= ARENA
F32R = mybir.dt.float32r
CAP = 160
NBLK = -(-SEQ // CAP)
HIDS0 = HID0
XE0 = HIDS0 + 2 * FU * CAP
PSEL0 = XE0 + 2 * DT * CAP
PT0 = PSEL0 + TT * CAP
SVW0 = PT0 + 2 * SEQ
SVN = NBLK * N_EXPERTS + 8
IOTA0 = SVW0 + TT * SVN
NBI0 = IOTA0 + CAP
SLOT_TMP = NBI0 + 8
assert SLOT_TMP + 336 <= GRAW0

CF = {}
for _name, _n in (("ident", 128), ("headcol", 8), ("invf", 1), ("iota8", 8), ("tail", 1)):
    CF[_name] = (sum(n for _, n in CF.values()), _n)
NCF = sum(n for _, n in CF.values())
LVT = 0
DIAG = LEVELS
LV = LEVELS + 1
INCL = 2 * LEVELS + 1
STRICT = INCL + 1
NCI = STRICT + 1
RET_D, RET_Q, RET_K, RET_C = 0, 512, 512 + 2 * P, 512 + 4 * P
NRET = RET_C + 2


class Signal:

    def __init__(self, nc, name):
        self.sem, self.base, self.sent = nc.alloc_semaphore(name), 0, 0

    def up(self, n=1, times=1):
        self.sent += n * times
        return self.sem, n

    def at(self, n):
        return self.sem, self.base + n


class Steps:

    def __init__(self, eng, count):
        self.eng, self.count = eng, count

    def __call__(self, ins):
        ins.then_inc(*self.count.up())

    def wait(self):
        self.eng.wait_ge(*self.count.at(self.count.sent))

    def link(self, ins):
        self(ins)
        self.wait()


class Kernel:
    def __init__(self, nc, ap):
        self.nc, self.ap, self.counts = nc, ap, {}
        base = (nc.sbuf_base + 31) // 32 * 32
        self.placed = 0

        def place(name, n, at=None, dt=F32):
            off = self.placed if at is None else at + self.arena_at
            if at is None:
                self.placed += (n + 7) // 8 * 8
            return nc.alloc_sbuf_tensor_at(name, [P, n], dt, offset=base + 4 * off)[:, :]

        self.H = place("h_tok", TT * D).rearrange("p (t d) -> p t d", d=D)
        self.B = place("keep", 4096)
        self.CF = place("const_sb", NCF)
        self.PAR = place("par_sb", 2 * NPAR + 12)
        self.SM = place("small", P)
        self.arena_at = self.placed
        self.A = place("arena", ARENA)
        self.HT = self.A[:, HT0:HT0 + DT * SEQ].rearrange("p (k t) -> p k t", t=SEQ)
        self.XR = place("x_split", 2 * DT * SEQ, XR0, F32R).rearrange("p (s k t) -> p s k t", s=2, t=SEQ)
        self.HID = place("hidden_split", 2 * FU * SEQ, HID0, F32R).rearrange("p (s f t) -> p s f t", s=2, t=SEQ)
        self.GSPL = place("gate_up_split", FRING * 4 * D, GSPL0, F32R).rearrange("p (r s u k f) -> p r s (u k f)", r=FRING, s=2, u=2, f=P)
        self.DSPL = place("down_split", FRING * 2 * HALF, DSPL0, F32R).rearrange("p (r s n) -> p r s n", r=FRING, s=2)
        self.WSPL = [place(f"w_split{r}", 2 * DT * PW, WSP0 + r * 2 * DT * PW, F32R).rearrange("p (s n) -> p s n", s=2) for r in range(PSPL)]
        self.HR = place("x_tok_split", 2 * TT * D, XR0, F32R).rearrange("p (s t d) -> p s t d", s=2, t=TT)
        self.HIDS = place("hidden_slots_split", 2 * FU * CAP, HIDS0, F32R).rearrange("p (s f t) -> p s f t", s=2, t=CAP)
        self.XE = place("x_slots_split", 2 * DT * CAP, XE0, F32R).rearrange("p (k s t) -> p k s t", s=2, t=CAP)
        self.PSEL = place("pick", TT * CAP, PSEL0, F32R).rearrange("p (t n) -> p t n", n=CAP)
        self.PT = place("scatter", 2 * SEQ, PT0, F32R).rearrange("p (j t) -> p j t", t=SEQ)
        self.YE = place("y_slots_split", 4 * D, TT * D - self.arena_at, F32R).rearrange("p (s j d) -> p s j d", s=2, j=2)
        self.SVW = self.A[:, SVW0:IOTA0].rearrange("p (t n) -> p t n", n=SVN)
        self.IOTA = self.A[:, IOTA0:NBI0]
        self.NBI = self.A[:, NBI0:NBI0 + 1].bitcast(I32)
        self.GRAW = self.A[:, GRAW0:GSPL0].rearrange("p (r n) -> p r n", r=FRING)
        self.DRAW = self.A[:, DRAW0:DSPL0].rearrange("p (r n) -> p r n", r=FRING)
        self.TMP = self.A[:, TMP0:TMP0 + 2 * SEQ].rearrange("p (r t) -> p r t", t=SEQ)
        self.PS = nc.alloc_psum_tensor("psum", [P, 8 * HALF], F32)
        self.MASK = self.B[:, 0:NCI * P].bitcast(I32)
        self.VF = self.B[:, NCI * P:NCI * P + 1024]
        self.SWAP = self.B[:, NCI * P + 1024:NCI * P + 1152]
        self.HSUM = self.B[:, NCI * P + 1152:NCI * P + 1280]
        self.GMASK = self.B[:, NCI * P + 1280:NCI * P + 1536]

    def sig(self, name):
        if name not in self.counts:
            self.counts[name] = Signal(self.nc, name)
        return self.counts[name]

    def close(self):
        for s in self.counts.values():
            s.base, s.sent = s.base + s.sent, 0

    def cf(self, name):
        a, n = CF[name]
        return self.CF[:, a:a + n]

    def par(self, l, name, i=0):
        a = PAR[name][0] + l * NPAR + i
        return self.PAR[:, a:a + 1]

    def bank(self, b, n=HALF):
        return self.PS[:, b * HALF:b * HALF + n]

    def first_units(self, gate, up, kind="ffn", n=2):
        def ahead(sp):
            for r in range(n):
                for u, w in enumerate((gate, up)):
                    sp.dma_start(self.GRAW[:, r, u * D:(u + 1) * D].rearrange("p (k f) -> p k f", k=DT),
                                 w[:, r * P:(r + 1) * P].rearrange("(k p) f -> p k f", p=P)).then_inc(*self.sig(f"{kind}_gate_up_loaded{r}").up(16))
        return ahead

    def stage_ffn(self, passes, gate_w, up_w, down_w):
        nc, H, XR, HID, TMP = self.nc, self.H, self.XR, self.HID, self.TMP
        GSPL, DSPL, GRAW, DRAW = self.GSPL, self.DSPL, self.GRAW, self.DRAW
        g_loaded = [self.sig(f"ffn_gate_up_loaded{r}") for r in range(FRING)]
        d_loaded = [self.sig(f"ffn_down_loaded{r}") for r in range(FRING)]
        g_hi, g_lo, d_hi, d_lo, g_mm, d_mm, silu_done, prod_done, hid_hi, hid_lo, sum_mm, acc_done = (self.sig(n) for n in (
            "ffn_gate_up_hi_ready", "ffn_gate_up_lo_ready", "ffn_down_hi_ready", "ffn_down_lo_ready", "ffn_gate_up_products", "ffn_down_products",
            "ffn_silu_done", "ffn_hidden_product_done", "ffn_hidden_hi_ready", "ffn_hidden_lo_ready", "ffn_half_summed", "ffn_sum_done"))
        G, N = passes * FU, passes * 2 * FU

        def g_waits(eng, g, *counts):
            if g >= FRING:
                for c in counts:
                    eng.wait_ge(*c.at(g - FRING + 1))

        with nc.Block() as block:
            @block.sync
            def _(sp):
                def load_g(g):
                    i, f = divmod(g, FU)
                    g_waits(sp, g, g_hi, g_lo)
                    for u, w in enumerate((gate_w, up_w)):
                        sp.dma_start(GRAW[:, g % FRING, u * D:(u + 1) * D].rearrange("p (k f) -> p k f", k=DT),
                                     w(i)[:, f * P:(f + 1) * P].rearrange("(k p) f -> p k f", p=P)).then_inc(*g_loaded[g % FRING].up(16))

                def load_d(n):
                    i, r = divmod(n, 2 * FU)
                    half, f = divmod(r, FU)
                    g_waits(sp, n, d_hi, d_lo)
                    sp.dma_start(DRAW[:, n % FRING, :], down_w(i)[f * P:(f + 1) * P, half * HALF:(half + 1) * HALF]).then_inc(*d_loaded[n % FRING].up(16))

                for i in range(passes):
                    for f in range(FU):
                        if f + 2 < FU:
                            load_g(i * FU + f + 2)
                        load_d(i * 2 * FU + f)
                    for f in range(FU):
                        load_d(i * 2 * FU + FU + f)
                        if f in (2, 5) and i + 1 < passes:
                            load_g((i + 1) * FU + (f == 5))

            @block.tensor
            def _(pe):
                def gate_up(g):
                    f, r = g % FU, g % FRING
                    pe.wait_ge(*g_hi.at(g + 1))
                    pe.wait_ge(*g_lo.at(g + 1))
                    if f >= 2:
                        pe.wait_ge(*prod_done.at(g - 1))
                    elif g >= FU:
                        pe.wait_ge(*acc_done.at((g // FU) * 2 * TT))
                    for u in range(2):
                        out = self.bank(2 * (f % 2) + u)
                        for k in range(DT):
                            w = [GSPL[:, r, s, (u * DT + k) * P:(u * DT + k + 1) * P] for s in range(2)]
                            nc.tensor.matmul(out, w[0], XR[:, 0, k, :], start=k == 0, stop=False)
                            nc.tensor.matmul(out, w[0], XR[:, 1, k, :], start=False, stop=False)
                            mm = nc.tensor.matmul(out, w[1], XR[:, 0, k, :], start=False, stop=k == DT - 1)
                    mm.then_inc(*g_mm.up())

                def down(n):
                    i, r = divmod(n, 2 * FU)
                    half, f = divmod(r, FU)
                    g = i * FU + f
                    pe.wait_ge(*d_hi.at(n + 1))
                    pe.wait_ge(*d_lo.at(n + 1))
                    if half == 0:
                        pe.wait_ge(*hid_lo.at(g + 1))
                        if f == 0 and i > 0:
                            pe.wait_ge(*acc_done.at(i * 2 * TT - TT))
                    for t in range(TT):
                        x = [HID[:, s, f, t * P:(t + 1) * P] for s in range(2)]
                        w = [DSPL[:, n % FRING, s, :] for s in range(2)]
                        out = self.bank(4 - 4 * half + t)
                        nc.tensor.matmul(out, x[0], w[0], start=f == 0, stop=False)
                        nc.tensor.matmul(out, x[0], w[1], start=False, stop=False)
                        mm = nc.tensor.matmul(out, x[1], w[0], start=False, stop=f == FU - 1)
                    mm.then_inc(*d_mm.up())

                for i in range(passes):
                    for f in range(FU):
                        gate_up(i * FU + f)
                        if f:
                            down(i * 2 * FU + f - 1)
                    for f in range(FU - 1, 2 * FU):
                        down(i * 2 * FU + f)

            @block.scalar
            def _(act):
                def split_g(g):
                    r = g % FRING
                    act.wait_ge(*g_loaded[r].at(32 * (g // FRING + (r > 1))))
                    g_waits(act, g, g_mm)
                    nc.scalar.activation(GSPL[:, r, 0, :], GRAW[:, r, :], ACT.Copy).then_inc(*g_hi.up())

                def split_d(n):
                    r = n % FRING
                    act.wait_ge(*d_loaded[r].at(16 * (n // FRING + 1)))
                    g_waits(act, n, d_mm)
                    nc.scalar.activation(DSPL[:, r, 0, :], DRAW[:, r, :], ACT.Copy).then_inc(*d_hi.up())

                split_g(0)
                split_g(1)
                for i in range(passes):
                    for f in range(FU):
                        g = i * FU + f
                        if f + 2 < FU:
                            split_g(g + 2)
                        split_d(i * 2 * FU + f)
                        act.wait_ge(*g_mm.at(g + 1))
                        if g >= 2:
                            act.wait_ge(*hid_lo.at(g - 1))
                        nc.scalar.activation(TMP[:, f % 2, :], self.bank(2 * (f % 2)), ACT.Silu).then_inc(*silu_done.up())
                        act.wait_ge(*prod_done.at(g + 1))
                        if i > 0:
                            act.wait_ge(*d_mm.at(i * 2 * FU))
                        nc.scalar.activation(HID[:, 0, f, :], TMP[:, f % 2, :], ACT.Copy).then_inc(*hid_hi.up())
                    for f in range(FU):
                        split_d(i * 2 * FU + FU + f)
                    if i + 1 < passes:
                        split_g((i + 1) * FU)
                        split_g((i + 1) * FU + 1)

            @block.vector
            def _(dve):
                def split_g(g):
                    r = g % FRING
                    dve.wait_ge(*g_hi.at(g + 1))
                    nc.vector.tensor_tensor(GSPL[:, r, 1, :], GRAW[:, r, :], GSPL[:, r, 0, :].bitcast(F32), ALU.subtract).then_inc(*g_lo.up())

                def split_d(n):
                    r = n % FRING
                    dve.wait_ge(*d_hi.at(n + 1))
                    nc.vector.tensor_tensor(DSPL[:, r, 1, :], DRAW[:, r, :], DSPL[:, r, 0, :].bitcast(F32), ALU.subtract).then_inc(*d_lo.up())

                def add(i, half):
                    dve.wait_ge(*d_mm.at(i * 2 * FU + (half + 1) * FU))
                    for t in range(TT):
                        y = H[:, t, half * HALF:(half + 1) * HALF]
                        nc.vector.tensor_tensor(y, y, self.bank(4 - 4 * half + t), ALU.add).then_inc(*acc_done.up())

                split_g(0)
                split_g(1)
                for i in range(passes):
                    for f in range(FU):
                        g = i * FU + f
                        if f + 2 < FU:
                            split_g(g + 2)
                        split_d(i * 2 * FU + f)
                        dve.wait_ge(*silu_done.at(g + 1))
                        nc.vector.tensor_tensor(TMP[:, f % 2, :], TMP[:, f % 2, :], self.bank(2 * (f % 2) + 1), ALU.mult).then_inc(*prod_done.up())
                        dve.wait_ge(*hid_hi.at(g + 1))
                        nc.vector.tensor_tensor(HID[:, 1, f, :], TMP[:, f % 2, :], HID[:, 0, f, :].bitcast(F32), ALU.subtract).then_inc(*hid_lo.up())
                    if i > 0:
                        dve.wait_ge(*acc_done.at(i * 2 * TT))
                    for f in range(FU):
                        split_d(i * 2 * FU + FU + f)
                        if f == 1:
                            add(i, 0)
                    if i + 1 < passes:
                        split_g((i + 1) * FU)
                        split_g((i + 1) * FU + 1)
                    add(i, 1)
        self.close()

    def area(self, off, *dims):
        n = int(np.prod(dims))
        a = self.A[:, off:off + n]
        if len(dims) == 2:
            a = a.rearrange("p (a b) -> p a b", b=dims[1])
        elif len(dims) == 3:
            a = a.rearrange("p (a b c) -> p a b c", b=dims[1], c=dims[2])
        return a

    def ft(self, i, n=1):
        return self.A[:, FT0 + i * SEQ:FT0 + (i + n) * SEQ]

    def tok(self, col, n=GROUP):
        return self.area(TOK0, TT, TOKW)[:, :, col:col + n]

    def stage_load(self, ahead):
        nc, ap = self.nc, self.ap
        loaded = self.sig("inputs_loaded")
        with nc.Block() as block:
            @block.sync
            def _(sp):
                sp.dma_start(self.H, ap["x"][0].rearrange("(t p) d -> p t d", p=P)).then_inc(*loaded.up(16))
                sp.dma_start(self.CF[:, :], ap["const_f"]).then_inc(*loaded.up(16))
                sp.dma_start(self.PAR[:, 0:2 * NPAR], ap["par"]).then_inc(*loaded.up(16))
                sp.dma_start(self.MASK, ap["const_i"]).then_inc(*loaded.up(16))
                sp.dma_start(self.B[:, NCI * P + 1024:NCI * P + 1536], ap["const_g"]).then_inc(*loaded.up(16))
                ahead(sp)
                sp.wait_ge(*loaded.at(80))

            @block.scalar
            def _(act):
                for n in ("gate_up_hi_ready", "down_hi_ready", "silu_done", "hidden_hi_ready", "scatter_matrix_ready", "tokens_hi_ready", "outputs_hi_ready"):
                    act.sem_inc(*self.sig("moe_" + n).up(8))

            @block.vector
            def _(dve):
                for n in ("gate_up_lo_ready", "down_lo_ready", "hidden_product_done", "hidden_lo_ready", "sum_done", "pick_ready", "part_sums_ready", "tokens_lo_ready", "outputs_lo_ready"):
                    dve.sem_inc(*self.sig("moe_" + n).up(8))

            @block.tensor
            def _(pe):
                for n in ("gate_up_products", "down_products", "pick_turned", "gathered", "scattered"):
                    pe.sem_inc(*self.sig("moe_" + n).up(8))
        self.close()

    def stage_to_feature(self, src, dst, scale=None, src_factor=None, split=None, ahead=None):
        nc, PS = self.nc, self.PS
        turned, moved, parts, read = self.sig("turned_to_feature"), self.sig("feature_tile_copied"), self.sig("feature_tile_split"), self.sig("source_scaled")
        ident = self.cf("ident")
        with nc.Block() as block:
            @block.sync
            def _(sp):
                if ahead is not None:
                    ahead(sp)

            @block.tensor
            def _(pe):
                for k in range(DT):
                    for t in range(TT):
                        mm = nc.tensor.transpose(PS[:, k * HALF + t * P:k * HALF + (t + 1) * P], src[:, t, k * P:(k + 1) * P], ident)
                    mm.then_inc(*turned.up())

            @block.scalar
            def _(act):
                for k in range(DT):
                    act.wait_ge(*turned.at(k + 1))
                    if split is not None:
                        nc.scalar.activation(split[:, 0, k, :], self.bank(k), ACT.Copy, scale=1.0 if scale is None else scale(k)).then_inc(*parts.up())
                    elif k % 2 == 0:
                        nc.scalar.activation(dst[:, k, :], self.bank(k), ACT.Copy, scale=1.0 if scale is None else scale(k)).then_inc(*moved.up())

            @block.vector
            def _(dve):
                for k in range(DT):
                    if split is not None:
                        dve.wait_ge(*parts.at(k + 1))
                        nc.vector.scalar_tensor_tensor(split[:, 1, k, :], self.bank(k), 1.0 if scale is None else scale(k), split[:, 0, k, :].bitcast(F32),
                                                       ALU.mult, ALU.subtract).then_inc(*moved.up())
                    elif k % 2 == 1:
                        dve.wait_ge(*turned.at(k + 1))
                        if scale is None:
                            nc.vector.tensor_copy(dst[:, k, :], self.bank(k)).then_inc(*moved.up())
                        else:
                            nc.vector.tensor_scalar(dst[:, k, :], self.bank(k), scale(k), None, ALU.mult).then_inc(*moved.up())
                if src_factor == 0.0:
                    nc.vector.memset(src, 0.0).then_inc(*read.up())
                elif src_factor is not None:
                    nc.vector.tensor_scalar(src, src, src_factor, None, ALU.mult).then_inc(*read.up())
        self.close()

    def load_piece(self, sp, w, pieces, raw_at, p):
        width, at = sum(n for _, n in pieces[p]), 0
        raw = self.area(raw_at, PRAW, DT * PW)[:, p % PRAW, 0:DT * width].rearrange("p (k c) -> p k c", k=DT)
        for c, n in pieces[p]:
            sp.dma_start(raw[:, :, at:at + n], w[:, c:c + n].rearrange("(k p) c -> p k c", p=P)).then_inc(*self.sig(f"w_piece_loaded{p % PRAW}").up(16))
            at += n

    def first_pieces(self, w, pieces, raw_at):
        return lambda sp: [self.load_piece(sp, w, pieces, raw_at, p) for p in range(PRAW)]

    def stage_stream(self, w, pieces, units, raw_at, copy_out, parts=1, engines=2, row=None):
        nc, XR, WSPL = self.nc, self.XR, self.WSPL
        loaded = [self.sig(f"w_piece_loaded{r}") for r in range(PRAW)]
        hi, lo, used, done, row_loaded = (self.sig(n) for n in ("w_piece_hi_ready", "w_piece_lo_ready", "w_piece_used", "projection_products", "gain_rows_loaded"))
        copied = [self.sig("projection_copied_act"), self.sig("projection_copied_dve")]
        raw = self.area(raw_at, PRAW, DT * PW)
        width = [sum(n for _, n in p) for p in pieces]
        flat = [(p, u, t) for p, us in enumerate(units) for u in us for t in (range(TT) if u[0] == "T" else [0])]
        turn = lambda j: j % 2 if engines == 2 else 1
        nth = lambda j: j // 2 + 1 if engines == 2 else j + 1
        dmas = lambda p: 16 * sum(len(x) for x in pieces[p % PRAW + PRAW:p + 1:PRAW])

        with nc.Block() as block:
            @block.sync
            def _(sp):
                for p in range(PRAW, len(pieces)):
                    sp.wait_ge(*hi.at(p - PRAW + 1))
                    sp.wait_ge(*lo.at(p - PRAW + 1))
                    self.load_piece(sp, w, pieces, raw_at, p)
                    if p == PRAW and row is not None:
                        sp.dma_start(self.area(FT0 - D, D), row.partition_broadcast(P)).then_inc(*row_loaded.up(16))
                if row is not None:
                    sp.wait_ge(*row_loaded.at(16))

            @block.tensor
            def _(pe):
                for j, (p, u, t) in enumerate(flat):
                    kind, _, c, n = u
                    if j == 0 or flat[j - 1][0] != p:
                        pe.wait_ge(*hi.at(p + 1))
                        pe.wait_ge(*lo.at(p + 1))
                    if j >= 8:
                        pe.wait_ge(*copied[turn(j)].at(nth(j - 8)))
                    ws = [WSPL[p % PSPL][:, s, 0:DT * width[p]].rearrange("p (k c) -> p k c", k=DT)[:, :, c:c + n] for s in range(2)]
                    for part in range(parts):
                        per = DT // parts
                        for k in range(part * per, (part + 1) * per):
                            first, last = k == part * per, k == (part + 1) * per - 1
                            if kind == "F":
                                out = self.bank(j % 8)[0:n, :]
                                trio = [(ws[0][:, k, :], XR[:, 0, k, :]), (ws[0][:, k, :], XR[:, 1, k, :]), (ws[1][:, k, :], XR[:, 0, k, :])]
                            else:
                                out = self.bank(j % 8)[:, part * n:(part + 1) * n]
                                xs = [XR[:, s, k, t * P:(t + 1) * P] for s in range(2)]
                                trio = [(xs[0], ws[0][:, k, :]), (xs[0], ws[1][:, k, :]), (xs[1], ws[0][:, k, :])]
                            if kind == "F" and n < P:
                                trio = [(a.bitcast(F32), b.bitcast(F32)) for a, b in trio]
                            for i, (a, b) in enumerate(trio):
                                mm = nc.tensor.matmul(out, a, b, start=first and i == 0, stop=last and i == 2)
                    mm.then_inc(*done.up())
                    if j + 1 == len(flat) or flat[j + 1][0] != p:
                        pe.wait_ge(*done.at(j + 1))
                        pe.sem_inc(*used.up())

            @block.scalar
            def _(act):
                j = 0
                for p in range(len(pieces) + 1):
                    if p < len(pieces):
                        act.wait_ge(*loaded[p % PRAW].at(dmas(p)))
                        if p >= PSPL:
                            act.wait_ge(*used.at(p - PSPL + 1))
                        nc.scalar.activation(WSPL[p % PSPL][:, 0, 0:DT * width[p]], raw[:, p % PRAW, 0:DT * width[p]], ACT.Copy).then_inc(*hi.up())
                    while j < len(flat) and flat[j][0] < p:
                        if turn(j) == 0:
                            act.wait_ge(*done.at(j + 1))
                            copy_out(0, flat[j][1], flat[j][2], j % 8).then_inc(*copied[0].up())
                        j += 1

            @block.vector
            def _(dve):
                j = 0
                for p in range(len(pieces) + 1):
                    if p < len(pieces):
                        dve.wait_ge(*hi.at(p + 1))
                        nc.vector.tensor_tensor(WSPL[p % PSPL][:, 1, 0:DT * width[p]], raw[:, p % PRAW, 0:DT * width[p]],
                                                WSPL[p % PSPL][:, 0, 0:DT * width[p]].bitcast(F32), ALU.subtract).then_inc(*lo.up())
                    while j < len(flat) and flat[j][0] < p:
                        if turn(j) == 1:
                            dve.wait_ge(*done.at(j + 1))
                            copy_out(1, flat[j][1], flat[j][2], j % 8).then_inc(*copied[1].up())
                        j += 1
        self.close()

    def project(self, w, pieces, units, row, ft, tok):
        nc = self.nc

        def copy_out(engine, u, t, b):
            kind, where, _, n = u
            out, src = (tok(where, n)[:, t, :], self.bank(b, n)) if kind == "T" else (ft(where)[0:n, :], self.bank(b)[0:n, :])
            return nc.vector.tensor_copy(out, src) if engine else nc.scalar.activation(out, src, ACT.Copy)
        self.stage_stream(w, pieces, units, HT0, copy_out, row=row)

    def stage_hgrn_gates(self, l, k):
        nc, SM = self.nc, self.SM
        sig_done, f_done, lb_ready, act_done = self.sig("hgrn_sigmoid_done"), self.sig("hgrn_f_done"), self.sig("hgrn_lb_step"), self.sig("hgrn_log_done")
        step = self.sig("dve_steps")
        q, f = self.ft(HQ, 2), self.ft(HF, 2)
        lb, om = SM[:, 64:66], SM[:, 66:68]
        a0, a1 = PAR["lb0"][0] + l * NPAR, PAR["lb1"][0] + l * NPAR
        with nc.Block() as block:
            @block.scalar
            def _(act):
                nc.scalar.activation(f, f, ACT.Sigmoid).then_inc(*sig_done.up())
                if l > 0:
                    act.wait_ge(*lb_ready.at(1))
                    nc.scalar.activation(lb, om, ACT.Sigmoid).then_inc(*sig_done.up())
                nc.scalar.activation(q, q, ACT.Silu).then_inc(*act_done.up())
                act.wait_ge(*f_done.at(2))
                nc.scalar.activation(f, f, ACT.Ln).then_inc(*act_done.up())

            @block.vector
            def _(dve):
                s = Steps(dve, step)
                if l > 0:
                    nc.vector.tensor_tensor(om, self.PAR[:, a1:a1 + 2], self.PAR[:, a0:a0 + 2], ALU.subtract).then_inc(*lb_ready.up())
                    dve.wait_ge(*sig_done.at(2))
                    s.link(nc.vector.tensor_scalar(om, lb, -1.0, 1.0, ALU.mult, ALU.add))
                    for i in range(2):
                        fi = f[:, i * SEQ:(i + 1) * SEQ]
                        s(nc.vector.tensor_scalar(fi, fi, om[:, i:i + 1], lb[:, i:i + 1], ALU.mult, ALU.add))
                    s.wait()
                else:
                    dve.wait_ge(*sig_done.at(1))
                nc.vector.tensor_scalar(k, f, -1.0, 1.0, ALU.mult, ALU.add).then_inc(*f_done.up(2))
        self.close()

    def stage_gla_gates(self, l, g, x):
        nc, ap = self.nc, self.ap
        loaded, mm_done, x_ready, log_done, step = (self.sig(n) for n in (
            "gla_w2_loaded", "gla_gate_product", "gla_gate_biased", "gla_softplus_done", "dve_steps"))
        w2 = self.A[0:16, 0:P]
        q = self.ft(GQ)
        astep = self.sig("act_steps")
        with nc.Block() as block:
            @block.sync
            def _(sp):
                sp.dma_start(w2, ap["gla_gate_w2"][l]).then_inc(*loaded.up(16))

            @block.tensor
            def _(pe):
                pe.wait_ge(*loaded.at(16))
                nc.tensor.matmul(self.bank(0), w2, self.ft(GLR)[0:16, :], start=True, stop=True).then_inc(*mm_done.up())

            @block.vector
            def _(dve):
                s = Steps(dve, step)
                dve.wait_ge(*mm_done.at(1))
                nc.vector.tensor_scalar(x, self.bank(0), self.par(l, "gate_b"), None, ALU.add).then_inc(*x_ready.up())
                dve.wait_ge(*x_ready.at(1))
                s(nc.vector.tensor_scalar(q, q, 32.0 ** -0.5, None, ALU.mult))
                s.link(nc.vector.tensor_scalar(self.bank(1), x, 0.0, None, ALU.min))
                dve.wait_ge(*log_done.at(1))
                s.link(nc.vector.tensor_tensor(g, self.bank(1), g, ALU.subtract))
                s.link(nc.vector.tensor_scalar(g, g, 1.0 / 16.0, None, ALU.mult))

            @block.scalar
            def _(act):
                s = Steps(act, astep)
                act.wait_ge(*x_ready.at(1))
                s.link(nc.scalar.activation(g, x, ACT.Abs))
                s.link(nc.scalar.activation(g, g, ACT.Exp, scale=-1.0))
                nc.scalar.activation(g, g, ACT.Ln, bias=1.0).then_inc(*log_done.up())
        self.close()

    def stage_decay_scores(self, q, k, g, T, kd, S, Qc, KD, DEC, base):
        nc, PS = self.nc, self.PS
        W = T * SEQ
        cum, rst = self.area(base, W), self.area(base + 1024, W)
        E = [self.area(base + 2048 + 1024 * i, W) for i in range(2)]
        hpt = P // kd
        Q = [self.area(o, hpt, W) for o in (base + 4096, 18432)]
        K = [self.area(base + 6144 + 1024 * i, W) for i in range(2)]
        step, astep, diff, exps, qk, mms, taken, cleared, bare, sums = (self.sig(n) for n in (
            "dve_steps", "act_steps", "decay_difference", "decay_factor", "decayed_qk_ready", "score_products", "scores_taken", "scores_cleared",
            "bare_queries_ready", "decay_sums"))
        chunks = cum.rearrange("p (n s) -> p n s", s=P)
        LAST = LEVELS + 1
        with nc.Block() as block:
            @block.gpsimd
            def _(pool):
                nc.gpsimd.memset(Q[0], 0.0).then_inc(*cleared.up())
                pool.wait_ge(*sums.at(1))
                for l in range(LEVELS + 1):
                    if l >= 2:
                        pool.wait_ge(*qk.at(l - 1))
                    h, at = (1 << l, (1 << l) - 1) if l < LEVELS else (P // 2, P - 1)
                    v = "p (n s) -> p n s"
                    c = cum.rearrange(v, s=2 * h)
                    nc.gpsimd.tensor_tensor(E[l % 2].rearrange(v, s=2 * h), c, c[:, :, at:at + 1].broadcast_to([P, W // (2 * h), 2 * h]),
                                            ALU.subtract).then_inc(*diff.up())
                    if l < 2:
                        nc.gpsimd.memset((Q[1], S)[l], 0.0).then_inc(*cleared.up())

            @block.vector
            def _(dve):
                s = Steps(dve, step)
                s.link(nc.vector.memset(rst, 1.0))
                s.link(nc.vector.memset(rst.rearrange("p (n s) -> p n s", s=P)[:, :, 0:1], 0.0))
                nc.vector.tensor_tensor_scan(cum, rst, g, 0.0, ALU.mult, ALU.add).then_inc(*sums.up())

                def take(l):
                    dve.wait_ge(*mms.at(l + 1))
                    if l >= 1:
                        dve.wait_ge(*taken.at(l))
                    else:
                        dve.wait_ge(*cleared.at(3))
                    m = self.MASK[:, (LVT + l) * P:(LVT + l + 1) * P] if l < LEVELS else self.MASK[:, DIAG * P:(DIAG + 1) * P]
                    nc.vector.copy_predicated(S.rearrange("p (n i) -> p n i", i=P), m.unsqueeze(1).broadcast_to([P, 16, P]),
                                              PS[:, (l % 2) * 2048:(l % 2) * 2048 + 2048].rearrange("p (n i) -> p n i", i=P)).then_inc(*taken.up())

                for l in range(LEVELS):
                    dve.wait_ge(*exps.at(l + 1))
                    if l >= 2:
                        dve.wait_ge(*mms.at(l - 1))
                    else:
                        dve.wait_ge(*cleared.at(l + 1))
                    for i in range(hpt):
                        r = slice(i * kd, (i + 1) * kd)
                        s(nc.vector.tensor_tensor(Q[l % 2][r, i, :], q[r, :], E[l % 2][r, :], ALU.mult))
                    nc.vector.tensor_tensor(K[l % 2], k, E[l % 2], ALU.mult).then_inc(*qk.up())
                    if l >= 1:
                        take(l - 1)
                take(LEVELS - 1)
                dve.wait_ge(*exps.at(LEVELS + 1))
                s(nc.vector.tensor_tensor(KD, k, E[LEVELS % 2], ALU.mult))
                dve.wait_ge(*exps.at(LEVELS + 2))
                s(nc.vector.tensor_tensor(Qc, q, rst, ALU.mult))
                take(LEVELS)

            @block.scalar
            def _(act):
                s = Steps(act, astep)
                for l in range(LEVELS + 1):
                    act.wait_ge(*diff.at(l + 1))
                    s.link(nc.scalar.activation(E[l % 2], E[l % 2], ACT.Abs))
                    nc.scalar.activation(E[l % 2], E[l % 2], ACT.Exp, scale=-1.0).then_inc(*exps.up())
                act.wait_ge(*mms.at(LEVELS - 1))
                for i in range(hpt):
                    r = slice(i * kd, (i + 1) * kd)
                    nc.scalar.activation(Q[LEVELS % 2][r, i, :], q[r, :], ACT.Copy).then_inc(*bare.up())
                nc.scalar.activation(DEC.rearrange("p (n s) -> p n s", s=1), chunks[:, :, P - 1:P], ACT.Exp).then_inc(*astep.up())
                nc.scalar.activation(rst, cum, ACT.Exp).then_inc(*exps.up())

            @block.tensor
            def _(pe):
                for l in range(LEVELS + 1):
                    b = K[l % 2] if l < LEVELS else k
                    if l < LEVELS:
                        pe.wait_ge(*qk.at(l + 1))
                    else:
                        pe.wait_ge(*bare.at(hpt))
                    if l >= 2:
                        pe.wait_ge(*taken.at(l - 1))
                    for c in range(TT):
                        for h in range(NHEAD):
                            col = (h // hpt) * SEQ + c * P
                            o = (l % 2) * 2048 + (h * TT + c) * P
                            mm = nc.tensor.matmul(PS[:, o:o + P], b[:, col:col + P], Q[l % 2][:, h % hpt, col:col + P], start=True, stop=True)
                    mm.then_inc(*mms.up())
        self.close()

    def stage_state(self, S, Qc, KD, DEC, V, T, kd, O, KT, Z):
        nc, PS = self.nc, self.PS
        turned, kt_ready, out_mm, z_mm, z_ready, o_ready, step = (self.sig(n) for n in (
            "key_turned", "key_token_major_ready", "chunk_output_products", "state_products", "state_ready", "chunk_output_ready", "dve_steps"))
        hpt = P // kd
        N = hpt * HD
        s_v = S.rearrange("p (n i) -> p n i", i=P)
        with nc.Block() as block:
            @block.tensor
            def _(pe):
                for c in range(TT - 1):
                    for j in range(T):
                        mm = nc.tensor.transpose(PS[:, c * HALF + j * P:c * HALF + (j + 1) * P], KD[:, j * SEQ + c * P:j * SEQ + (c + 1) * P], self.cf("ident"))
                mm.then_inc(*turned.up())
                for c in range(TT):
                    for h in range(NHEAD):
                        mm = nc.tensor.matmul(self.bank(4 + c)[:, h * HD:(h + 1) * HD], s_v[:, h * TT + c, :], V[:, c, h * HD:(h + 1) * HD], start=True, stop=c == 0)
                        if c > 0:
                            if h == 0:
                                pe.wait_ge(*z_ready.at(c))
                            j = h // hpt
                            mm = nc.tensor.matmul(self.bank(4 + c)[:, h * HD:(h + 1) * HD], Qc[:, j * SEQ + c * P:j * SEQ + (c + 1) * P],
                                                  Z[:, c - 1, h * HD:(h + 1) * HD], start=False, stop=True)
                    mm.then_inc(*out_mm.up())
                    if c == 0:
                        pe.wait_ge(*kt_ready.at(1))
                    if c < TT - 1:
                        for j in range(T):
                            mm = nc.tensor.matmul(self.bank(c)[:, j * N:(j + 1) * N], KT[:, c, j * P:(j + 1) * P], V[:, c, j * N:(j + 1) * N], start=True, stop=True)
                        mm.then_inc(*z_mm.up())

            @block.vector
            def _(dve):
                s = Steps(dve, step)
                dve.wait_ge(*turned.at(1))
                nc.vector.tensor_copy(KT[:, 0:TT - 1, :], PS[:, 0:(TT - 1) * HALF].rearrange("p (c n) -> p c n", n=HALF)[:, :, 0:T * P]).then_inc(*kt_ready.up())
                for c in range(TT - 1):
                    dve.wait_ge(*z_mm.at(c + 1))
                    z = Z[:, c, :].rearrange("p (j n) -> p j n", n=N)
                    own = (self.HSUM if kd == HD else self.GMASK).unsqueeze(1).broadcast_to([P, T, N])
                    if c == 0:
                        nc.vector.tensor_tensor(z, self.bank(0, GROUP).rearrange("p (j n) -> p j n", n=N), own, ALU.mult).then_inc(*z_ready.up())
                    else:
                        dve.wait_ge(*z_ready.at(c))
                        for j in range(T):
                            a = slice(j * N, (j + 1) * N)
                            s(nc.vector.scalar_tensor_tensor(Z[:, c, a], Z[:, c - 1, a], DEC[:, j * TT + c:j * TT + c + 1], self.bank(c)[:, a], ALU.mult, ALU.add))
                        s.wait()
                        nc.vector.tensor_tensor(z, z, own, ALU.mult).then_inc(*z_ready.up())

            @block.scalar
            def _(act):
                for c in range(TT):
                    act.wait_ge(*out_mm.at(c + 1))
                    nc.scalar.activation(O[:, c, :], self.bank(4 + c, GROUP), ACT.Copy).then_inc(*o_ready.up())
        self.close()

    def stage_head_norm(self, O, SQ, gate, out, eps, center=False, gain=None, bias=None, bonus=None, silu_gate=True):
        nc, SM = self.nc, self.SM
        step, var_ready, root_ready, gate_ready = self.sig("dve_steps"), self.sig("head_variance_ready"), self.sig("head_root_ready"), self.sig("head_gate_ready")
        N = TT * NHEAD
        mean, var = SM[:, 64:64 + N], SM[:, 80:80 + N]
        fh = "p t (h e) -> p (t h) e"
        o3, sq3, v3 = O.rearrange("p t n -> p (t n)").rearrange("p (n e) -> p n e", e=HD), SQ.rearrange("p t n -> p (t n)").rearrange("p (n e) -> p n e", e=HD), None
        bc = lambda x: x.unsqueeze(2).broadcast_to([P, N, HD])
        rowbc = lambda x: x.unsqueeze(1).broadcast_to([P, TT, GROUP])
        with nc.Block() as block:
            @block.vector
            def _(dve):
                s = Steps(dve, step)
                if center:
                    s.link(nc.vector.tensor_reduce(mean, o3, AX.X, ALU.add))
                    s.link(nc.vector.tensor_scalar(mean, mean, 1.0 / HD, None, ALU.mult))
                    s.link(nc.vector.tensor_tensor(o3, o3, bc(mean), ALU.subtract))
                s.link(nc.vector.tensor_tensor(SQ, O, O, ALU.mult))
                s.link(nc.vector.tensor_reduce(var, sq3, AX.X, ALU.add))
                nc.vector.tensor_scalar(var, var, 1.0 / HD, eps, ALU.mult, ALU.add).then_inc(*var_ready.up())
                dve.wait_ge(*root_ready.at(1))
                s.link(nc.vector.reciprocal(var, var))
                s.link(nc.vector.tensor_tensor(o3, o3, bc(var), ALU.mult))
                if gain is not None:
                    s.link(nc.vector.tensor_tensor(O, O, rowbc(gain), ALU.mult))
                if bias is not None:
                    s.link(nc.vector.tensor_tensor(O, O, rowbc(bias), ALU.add))
                if bonus is not None:
                    s.link(nc.vector.tensor_tensor(sq3, bonus[0].rearrange("p t n -> p (t n)").rearrange("p (n e) -> p n e", e=HD), bc(bonus[1]), ALU.mult))
                    s.link(nc.vector.tensor_tensor(O, O, SQ, ALU.add))
                if silu_gate:
                    dve.wait_ge(*gate_ready.at(1))
                s.link(nc.vector.tensor_tensor(out, O, gate, ALU.mult))

            @block.scalar
            def _(act):
                if silu_gate:
                    nc.scalar.activation(gate, gate, ACT.Silu).then_inc(*gate_ready.up())
                act.wait_ge(*var_ready.at(1))
                nc.scalar.activation(var, var, ACT.Sqrt).then_inc(*root_ready.up())
        self.close()

    def stage_retention_scores(self, S, Qc, KD, DEC, base):
        nc, ap, PS = self.nc, self.ap, self.PS
        loaded, step, asteps, swapped, rotated, mms, angles, trig = (self.sig(n) for n in (
            "retention_tables_loaded", "dve_steps", "act_steps", "rotary_swapped", "rotary_ready", "score_products", "angles_ready", "sines_ready"))
        q, k = self.ft(RQ, 2), self.ft(RKK, 2)
        pos = self.area(base, SEQ).bitcast(I32)
        ang, n1, sn, cs = (self.area(base + SEQ * i, SEQ) for i in (1, 2, 3, 4))
        tab = self.area(base + SEQ * 5, NRET)
        tmp = self.area(base + SEQ * 5 + 1088, 2 * SEQ)
        MAGIC = 12582912.0
        C1, C2 = 6.28125, 0.0019350051879882812
        C3 = float(2.0 * np.pi - C1 - C2)
        LIM = 3.1415925
        t3 = lambda x: x.rearrange("p (a t) -> p a t", t=SEQ)
        bc = lambda x: x.unsqueeze(1).broadcast_to([P, 2, SEQ])
        with nc.Block() as block:
            @block.sync
            def _(sp):
                sp.dma_start(pos, ap["positions"][0].partition_broadcast(P)).then_inc(*loaded.up(16))
                sp.dma_start(tab, ap["ret_c"]).then_inc(*loaded.up(16))

            @block.tensor
            def _(pe):
                for i, x in enumerate((q, k)):
                    for j in range(2):
                        mm = nc.tensor.matmul(self.bank(2 * i + j), self.SWAP, x[:, j * SEQ:(j + 1) * SEQ], start=True, stop=True)
                mm.then_inc(*swapped.up())
                pe.wait_ge(*rotated.at(1))
                for c in range(TT):
                    for h in range(NHEAD):
                        r, col = (h % 2) * HD, (h // 2) * SEQ + c * P
                        mm = nc.tensor.matmul(self.bank(4 + h)[:, c * P:(c + 1) * P], k[r:r + HD, col:col + P], q[r:r + HD, col:col + P], start=True, stop=True)
                mm.then_inc(*mms.up())

            @block.scalar
            def _(act):
                for i, x in enumerate((sn, cs)):
                    act.wait_ge(*angles.at(i + 1))
                    nc.scalar.activation(x, x, ACT.Sin).then_inc(*trig.up())

            @block.vector
            def _(dve):
                s = Steps(dve, step)
                dve.wait_ge(*loaded.at(32))
                s.link(nc.vector.tensor_copy(ang, pos))
                s.link(nc.vector.tensor_scalar(ang, ang, self.cf("invf"), None, ALU.mult))
                for i, (x, turn) in enumerate(((sn, 0.0), (cs, 0.25))):
                    s.link(nc.vector.tensor_scalar(n1, ang, 1.0 / (2.0 * np.pi), turn, ALU.mult, ALU.add))
                    s.link(nc.vector.tensor_scalar(n1, n1, MAGIC, None, ALU.add))
                    s.link(nc.vector.tensor_scalar(n1, n1, MAGIC, None, ALU.subtract))
                    s.link(nc.vector.scalar_tensor_tensor(x, n1, -C1, ang, ALU.mult, ALU.add))
                    s.link(nc.vector.scalar_tensor_tensor(x, n1, -C2, x, ALU.mult, ALU.add))
                    s.link(nc.vector.scalar_tensor_tensor(x, n1, -C3, x, ALU.mult, ALU.add))
                    s.link(nc.vector.tensor_scalar(x, x, turn * 2.0 * np.pi, None, ALU.add))
                    nc.vector.tensor_scalar(x, x, LIM, -LIM, ALU.min, ALU.max).then_inc(*angles.up())
                dve.wait_ge(*trig.at(2))
                dve.wait_ge(*swapped.at(1))
                for i, x in enumerate((q, k)):
                    s.link(nc.vector.tensor_tensor(t3(tmp), t3(PS[:, 2 * i * HALF:(2 * i + 2) * HALF]), bc(sn), ALU.mult))
                    s.link(nc.vector.tensor_tensor(t3(x), t3(x), bc(cs), ALU.mult))
                    if i == 0:
                        s.link(nc.vector.tensor_tensor(x, x, tmp, ALU.add))
                s.link(nc.vector.tensor_tensor(k, k, tmp, ALU.add))
                nc.vector.tensor_scalar(k, k, HD ** -0.5, None, ALU.mult).then_inc(*rotated.up())
                dve.wait_ge(*rotated.at(1))
                for j in range(2):
                    c3 = lambda x: x[:, j * SEQ:(j + 1) * SEQ].rearrange("p (c t) -> p c t", t=P)
                    tbl = lambda o: tab[:, o + j * P:o + (j + 1) * P].unsqueeze(1).broadcast_to([P, TT, P])
                    s(nc.vector.tensor_tensor(c3(Qc), c3(q), tbl(RET_Q), ALU.mult))
                    s(nc.vector.tensor_tensor(c3(KD), c3(k), tbl(RET_K), ALU.mult))
                    s(nc.vector.tensor_copy(DEC[:, j * TT:(j + 1) * TT], tab[:, RET_C + j:RET_C + j + 1].broadcast_to([P, TT])))
                dve.wait_ge(*mms.at(1))
                h3 = lambda x: x.rearrange("p (h c i) -> p h c i", c=TT, i=P)
                s(nc.vector.tensor_tensor(h3(S), h3(PS[:, 4 * HALF:8 * HALF]),
                                          tab[:, RET_D:RET_D + HALF].rearrange("p (h i) -> p h i", i=P).unsqueeze(2).broadcast_to([P, NHEAD, TT, P]), ALU.mult))
        self.close()

    RW_A, RW_B, RW_R, RW_K = 0, 1024, 2048, 3072
    RW_AT, RW_BT, RW_KT, RW_VT = 4096, 5120, 6144, 7168
    RW_M, RW_MAK, RW_MRB, RW_MRK = 8192, 10240, 12288, 14336
    RW_T, RW_U, RW_X, RW_PT = 16384, 18432, FT0, FT0 + 2048
    RW_SMALL = FT0 + 3072
    RW_Z = 20480
    RW_C, RW_LR, RW_KK, RW_G, RW_T1, RW_T2 = (TOK0 + 1024 * i for i in range(6))
    RW_O, RW_U0 = FT0 + 16 * SEQ, FT0 + 18 * SEQ

    def stage_rwkv_gates(self, l):
        nc, ap, PS = self.nc, self.ap, self.PS
        loaded, step, astep, shifted, lowrank, mms, gates, v_mm, v_cp, kk_sq, kk_sum, kk_root, root, cum_ready, exps = (self.sig(n) for n in (
            "rwkv_weights_loaded", "dve_steps", "act_steps", "rwkv_shifted", "rwkv_low_rank_ready", "rwkv_gate_products", "rwkv_gates_ready",
            "rwkv_value_products", "rwkv_value_step", "rwkv_kk_squares", "rwkv_kk_sums", "rwkv_kk_clamped", "rwkv_kk_norm", "decay_sums", "rwkv_decay_factors"))
        X = self.ft(RR, 9).rearrange("p (n t) -> p n t", t=SEQ)
        Dd = self.area(8192, 9, SEQ)
        r, k, v = self.ft(RR, 2), self.ft(RK, 2), self.ft(RV, 2)
        wa, g0, g1 = self.ft(RWA), self.ft(RG), self.ft(RG + 1)[0:32, :]
        w2a2 = self.area(self.RW_T, 256)
        g2a, g2b = self.area(self.RW_T + 256, 256), self.area(self.RW_T + 512, 256)
        v1 = self.area(self.RW_T + 768, 2, 32)
        v2 = self.area(self.RW_T + 832, 256)[0:32, :]
        t32 = self.area(self.RW_T + 1088, SEQ)[0:32, :]
        rst = self.area(self.RW_U, 1024)
        c, a, kk, gt, t1, t2 = (self.area(o, 1024) for o in (self.RW_C, self.RW_LR, self.RW_KK, self.RW_G, self.RW_T1, self.RW_T2))
        At, Bt, Rt, Kt = (self.area(o, 1024) for o in (self.RW_A, self.RW_B, self.RW_R, self.RW_K))
        DEC, MID = self.area(self.RW_SMALL, 8), self.area(self.RW_SMALL + 8, 8)
        two = lambda x: [x[:, j * SEQ:(j + 1) * SEQ] for j in range(2)]
        chunk = lambda x: x.rearrange("p (n s) -> p n s", s=P)
        with nc.Block() as block:
            @block.sync
            def _(sp):
                sp.dma_start(w2a2[0:64, :], ap["rwkv_w2"][l]).then_inc(*loaded.up(16))
                sp.dma_start(w2a2[64:128, :], ap["rwkv_a2"][l]).then_inc(*loaded.up(16))
                sp.dma_start(g2a, ap["rwkv_g2"][l][0:P, :]).then_inc(*loaded.up(16))
                sp.dma_start(g2b[0:32, :], ap["rwkv_g2"][l][P:160, :]).then_inc(*loaded.up(16))
                if l > 0:
                    sp.dma_start(v1, ap["rwkv_v1"][l - 1].rearrange("(a p) n -> p a n", p=P)).then_inc(*loaded.up(16))
                    sp.dma_start(v2, ap["rwkv_v2"][l - 1]).then_inc(*loaded.up(16))

            @block.vector
            def _(dve):
                s = Steps(dve, step)
                s(nc.vector.tensor_tensor(Dd[:, 0:8, 1:SEQ], X[:, 0:8, 0:SEQ - 1], X[:, 0:8, 1:SEQ], ALU.subtract))
                s(nc.vector.tensor_tensor(Dd[0:32, 8, 1:SEQ], X[0:32, 8, 0:SEQ - 1], X[0:32, 8, 1:SEQ], ALU.subtract))
                s(nc.vector.tensor_scalar(Dd[:, 0:8, 0:1], X[:, 0:8, 0:1], -1.0, None, ALU.mult))
                s.link(nc.vector.tensor_scalar(Dd[0:32, 8, 0:1], X[0:32, 8, 0:1], -1.0, None, ALU.mult))
                for j in range(9):
                    n = 32 if j == 8 else P
                    nc.vector.scalar_tensor_tensor(X[0:n, j, :], Dd[0:n, j, :], self.par(l, "mu", j)[0:n, :], X[0:n, j, :], ALU.mult, ALU.add).then_inc(*shifted.up())
                dve.wait_ge(*shifted.at(9))
                for j in range(2):
                    s(nc.vector.tensor_scalar(two(kk)[j], two(k)[j], self.par(l, "k_k", j), None, ALU.mult))
                s.wait()
                nc.vector.tensor_tensor(t1, kk, kk, ALU.mult).then_inc(*kk_sq.up())
                s.link(nc.vector.memset(rst, 1.0))
                s.link(nc.vector.memset(chunk(rst)[:, :, 0:1], 0.0))
                dve.wait_ge(*gates.at(4))
                s.link(nc.vector.tensor_scalar(t2, t2, -EXP_NEG_HALF, None, ALU.mult))
                s.link(nc.vector.tensor_tensor_scan(c, rst, t2, 0.0, ALU.mult, ALU.add))
                s.link(nc.vector.tensor_copy(MID, chunk(c)[:, :, P // 2 - 1:P // 2].rearrange("p n s -> p (n s)")))
                s.link(nc.vector.tensor_tensor(chunk(c), chunk(c), MID.unsqueeze(2).broadcast_to([P, 8, P]), ALU.subtract))
                nc.vector.tensor_tensor(t2, c, t2, ALU.subtract).then_inc(*cum_ready.up())
                s.link(nc.vector.tensor_copy(DEC, chunk(c)[:, :, P - 1:P].rearrange("p n s -> p (n s)")))
                for j in range(2):
                    s(nc.vector.tensor_tensor(DEC[:, j * TT:j * TT + 3], DEC[:, j * TT:j * TT + 3], MID[:, j * TT + 1:j * TT + 4], ALU.add))
                s.wait()
                nc.vector.tensor_copy(DEC, DEC).then_inc(*cum_ready.up())
                if l == 0:
                    s(nc.vector.tensor_copy(self.VF, v))
                else:
                    dve.wait_ge(*v_mm.at(1))
                    nc.vector.tensor_copy(t32, self.bank(0)[0:32, :]).then_inc(*v_cp.up())
                    s.link(nc.vector.tensor_tensor(self.VF, self.VF, v, ALU.subtract))
                    dve.wait_ge(*v_cp.at(3))
                    s.link(nc.vector.tensor_tensor(self.VF, self.VF, At, ALU.mult))
                    s.link(nc.vector.tensor_tensor(v, v, self.VF, ALU.add))
                dve.wait_ge(*kk_sum.at(1))
                nc.vector.tensor_scalar(t1, PS[:, 6 * HALF:8 * HALF], 1e-24, None, ALU.max).then_inc(*kk_root.up())
                dve.wait_ge(*root.at(1))
                s.link(nc.vector.reciprocal(t1, t1))
                s.link(nc.vector.tensor_tensor(kk, kk, t1, ALU.mult))
                for j in range(2):
                    s(nc.vector.tensor_scalar(two(t1)[j], two(a)[j], 1.0, self.par(l, "k_a", j), ALU.subtract, ALU.mult))
                s.wait()
                s.link(nc.vector.scalar_tensor_tensor(k, t1, 1.0, k, ALU.add, ALU.mult))
                dve.wait_ge(*exps.at(3))
                s.link(nc.vector.scalar_tensor_tensor(At, kk, -1.0, t2, ALU.mult, ALU.mult))
                s.link(nc.vector.tensor_tensor(Rt, r, Rt, ALU.mult))
                s.link(nc.vector.tensor_tensor(Kt, k, Bt, ALU.mult))
                s.link(nc.vector.tensor_tensor(kk, kk, a, ALU.mult))
                s.link(nc.vector.tensor_tensor(Bt, kk, Bt, ALU.mult))
                for j in range(2):
                    s(nc.vector.scalar_tensor_tensor(two(r)[j], two(r)[j], self.par(l, "r_k", j), two(k)[j], ALU.mult, ALU.mult))

            @block.scalar
            def _(act):
                s = Steps(act, astep)
                act.wait_ge(*shifted.at(9))
                nc.scalar.activation(wa[0:64, :], wa[0:64, :], ACT.Tanh).then_inc(*lowrank.up())
                nc.scalar.activation(g0, g0, ACT.Sigmoid).then_inc(*lowrank.up())
                nc.scalar.activation(g1, g1, ACT.Sigmoid).then_inc(*lowrank.up())
                act.wait_ge(*mms.at(1))
                for j in range(2):
                    nc.scalar.activation(two(t2)[j], self.bank(j), ACT.Sigmoid, bias=self.par(l, "w0", j)).then_inc(*gates.up())
                for j in range(2):
                    nc.scalar.activation(two(a)[j], self.bank(2 + j), ACT.Sigmoid, bias=self.par(l, "a0", j)).then_inc(*gates.up())
                s(nc.scalar.activation(gt, PS[:, 4 * HALF:6 * HALF], ACT.Copy))
                if l > 0:
                    act.wait_ge(*v_mm.at(2))
                    for j in range(2):
                        nc.scalar.activation(two(At)[j], self.bank(2 + j), ACT.Sigmoid, bias=self.par(l, "v0", j)).then_inc(*v_cp.up())
                act.wait_ge(*kk_root.at(1))
                nc.scalar.activation(t1, t1, ACT.Sqrt).then_inc(*root.up())
                act.wait_ge(*cum_ready.at(2))
                nc.scalar.activation(Rt, c, ACT.Exp).then_inc(*exps.up())
                nc.scalar.activation(Bt, c, ACT.Exp, scale=-1.0).then_inc(*exps.up())
                s(nc.scalar.activation(DEC, DEC, ACT.Exp))
                nc.scalar.activation(t2, t2, ACT.Exp).then_inc(*exps.up())

            @block.tensor
            def _(pe):
                pe.wait_ge(*loaded.at(64 if l == 0 else 96))
                pe.wait_ge(*lowrank.at(3))
                for j in range(2):
                    nc.tensor.matmul(self.bank(j), w2a2[0:64, j * P:(j + 1) * P], wa[0:64, :], start=True, stop=True)
                    nc.tensor.matmul(self.bank(2 + j), w2a2[64:128, j * P:(j + 1) * P], wa[64:128, :], start=True, stop=True)
                for t in range(TT):
                    o = PS[:, 4 * HALF + t * GROUP:4 * HALF + (t + 1) * GROUP]
                    nc.tensor.matmul(o, g0[:, t * P:(t + 1) * P], g2a, start=True, stop=False)
                    mm = nc.tensor.matmul(o, g1[:, t * P:(t + 1) * P], g2b[0:32, :], start=False, stop=True)
                mm.then_inc(*mms.up())
                pe.wait_ge(*kk_sq.at(1))
                for j in range(2):
                    mm = nc.tensor.matmul(self.bank(6 + j), self.HSUM, two(t1)[j], start=True, stop=True)
                mm.then_inc(*kk_sum.up())
                if l > 0:
                    pe.wait_ge(*gates.at(4))
                    for j in range(2):
                        mm = nc.tensor.matmul(self.bank(0)[0:32, :], v1[:, j, :], two(v)[j], start=j == 0, stop=j == 1)
                    mm.then_inc(*v_mm.up())
                    pe.wait_ge(*v_cp.at(1))
                    for j in range(2):
                        mm = nc.tensor.matmul(self.bank(2 + j), v2[:, j * P:(j + 1) * P], t32, start=True, stop=True)
                    mm.then_inc(*v_mm.up())
        self.close()

    def stage_rwkv_scores(self, l):
        nc, PS = self.nc, self.PS
        heads_ready, mms, taken, turned, copied, step, cleared = (self.sig(n) for n in (
            "rwkv_heads_apart", "score_products", "scores_taken", "rwkv_turned", "rwkv_token_major_ready", "dve_steps", "scores_cleared"))
        At, Bt, Rt, Kt = (self.area(o, 1024) for o in (self.RW_A, self.RW_B, self.RW_R, self.RW_K))
        v, r = self.ft(RV, 2), self.ft(RR, 2)
        Am, Rm = self.area(self.RW_T1, 2, 1024), self.area(self.RW_C, 2, 1024)
        pairs = [(Bt, Am, self.RW_M, STRICT), (Kt, Am, self.RW_MAK, STRICT), (Bt, Rm, self.RW_MRB, INCL), (Kt, Rm, self.RW_MRK, INCL)]
        turns = [(At, self.RW_AT), (Bt, self.RW_BT), (Kt, self.RW_KT), (v, self.RW_VT)]
        n3 = lambda x: x.rearrange("p (n i) -> p n i", i=P)
        bonus = self.area(self.RW_SMALL + 16, 16)
        with nc.Block() as block:
            @block.gpsimd
            def _(pool):
                for i, o in enumerate((self.RW_M, self.RW_MAK, self.RW_MRB, self.RW_MRK)):
                    nc.gpsimd.memset(self.area(o, 2048), 0.0).then_inc(*cleared.up())

            @block.tensor
            def _(pe):
                def scores(i):
                    a, b, _, _ = pairs[i]
                    for c in range(TT):
                        for h in range(NHEAD):
                            col = (h // 2) * SEQ + c * P
                            o = (h * TT + c) * P
                            mm = nc.tensor.matmul(PS[:, o:o + P], a[:, col:col + P], b[:, h % 2, col:col + P], start=True, stop=True)
                    mm.then_inc(*mms.up())

                def turn(i):
                    for c in range(TT):
                        for j in range(2):
                            o = 2048 + i % 2 * 1024 + c * GROUP + j * P
                            mm = nc.tensor.transpose(PS[:, o:o + P], turns[i][0][:, j * SEQ + c * P:j * SEQ + (c + 1) * P], self.cf("ident"))
                    mm.then_inc(*turned.up())

                turn(0)
                turn(1)
                for i in range(4):
                    pe.wait_ge(*heads_ready.at(2 + 2 * (i // 2)))
                    if i >= 1:
                        pe.wait_ge(*taken.at(i))
                    scores(i)
                    if i < 2:
                        pe.wait_ge(*copied.at(i + 1))
                        turn(i + 2)
                pe.wait_ge(*copied.at(3))
                for c in range(TT):
                    for j in range(2):
                        mm = nc.tensor.matmul(PS[:, 2048 + c * NHEAD:2048 + (c + 1) * NHEAD], r[:, j * SEQ + c * P:j * SEQ + (c + 1) * P],
                                              self.cf("headcol")[:, j * 4:j * 4 + 4], start=j == 0, stop=j == 1)
                mm.then_inc(*turned.up())

            @block.vector
            def _(dve):
                for x, src in ((Am, At), (Rm, Rt)):
                    for i in range(2):
                        own, other = slice(i * HD, (i + 1) * HD), slice((1 - i) * HD, (2 - i) * HD)
                        nc.vector.memset(x[other, i, :], 0.0).then_inc(*step.up())
                        nc.vector.tensor_copy(x[own, i, :], src[own, :]).then_inc(*heads_ready.up())
                for i, (_, _, o, m) in enumerate(pairs):
                    dve.wait_ge(*cleared.at(i + 1))
                    dve.wait_ge(*mms.at(i + 1))
                    nc.vector.copy_predicated(n3(self.area(o, 2048)), self.MASK[:, m * P:(m + 1) * P].unsqueeze(1).broadcast_to([P, 16, P]),
                                              n3(PS[:, 0:2048])).then_inc(*taken.up())
                U = n3(self.area(self.RW_U, 2048))
                s = Steps(dve, step)
                s.link(nc.vector.tensor_copy(U, self.cf("ident").unsqueeze(1).broadcast_to([P, 16, P])))
                s(nc.vector.copy_predicated(U, self.MASK[:, LVT * P:(LVT + 1) * P].unsqueeze(1).broadcast_to([P, 16, P]), n3(self.area(self.RW_M, 2048))))

            @block.scalar
            def _(act):
                for i, (_, o) in enumerate(turns):
                    act.wait_ge(*turned.at(i + 1))
                    nc.scalar.activation(self.area(o, 1024), PS[:, 2048 + i % 2 * 1024:3072 + i % 2 * 1024], ACT.Copy).then_inc(*copied.up())
                act.wait_ge(*turned.at(5))
                nc.scalar.activation(bonus, PS[:, 2048:2064], ACT.Copy).then_inc(*copied.up())
        self.close()

    def stage_rwkv_solve(self):
        nc, PS = self.nc, self.PS
        x_mm, x_ready, t_mm, u_mm, t_ready, u_ready = (self.sig(n) for n in (
            "solve_nt_products", "solve_nt_ready", "solve_tnt_products", "solve_u_products", "solve_t_ready", "solve_u_ready"))
        M, T, U, X = (self.area(o, NHEAD, TT, P) for o in (self.RW_M, self.RW_T, self.RW_U, self.RW_X))
        b3 = lambda b: self.bank(b).rearrange("p (c i) -> p c i", i=P)
        with nc.Block() as block:
            @block.tensor
            def _(pe):
                for h in range(NHEAD):
                    for c in range(TT):
                        mm = nc.tensor.transpose(self.bank(4 + h)[:, c * P:(c + 1) * P], U[:, h, c, :], self.cf("ident"))
                    mm.then_inc(*t_mm.up())
                for l in range(1, LEVELS):
                    for h in range(NHEAD):
                        pe.wait_ge(*t_ready.at((l - 1) * NHEAD + h + 1))
                        if l > 1:
                            pe.wait_ge(*u_ready.at((l - 2) * NHEAD + h + 1))
                        for c in range(TT):
                            mm = nc.tensor.matmul(self.bank(h)[:, c * P:(c + 1) * P], M[:, h, c, :], T[:, h, c, :], start=True, stop=True)
                        mm.then_inc(*x_mm.up())
                    for h in range(NHEAD):
                        pe.wait_ge(*x_ready.at((l - 1) * NHEAD + h + 1))
                        if l < LEVELS - 1:
                            for c in range(TT):
                                mm = nc.tensor.matmul(self.bank(4 + h)[:, c * P:(c + 1) * P], U[:, h, c, :], X[:, h, c, :], start=True, stop=True)
                            mm.then_inc(*t_mm.up())
                        for c in range(TT):
                            mm = nc.tensor.matmul(self.bank(h)[:, c * P:(c + 1) * P], X[:, h, c, :], U[:, h, c, :], start=True, stop=True)
                        mm.then_inc(*u_mm.up())

            @block.scalar
            def _(act):
                for l in range(1, LEVELS):
                    for h in range(NHEAD):
                        act.wait_ge(*x_mm.at((l - 1) * NHEAD + h + 1))
                        nc.scalar.activation(X[:, h, :, :], b3(h), ACT.Copy).then_inc(*x_ready.up())

            @block.vector
            def _(dve):
                mask = lambda m: self.MASK[:, m * P:(m + 1) * P].unsqueeze(1).broadcast_to([P, TT, P])
                for h in range(NHEAD):
                    dve.wait_ge(*t_mm.at(h + 1))
                    nc.vector.tensor_copy(T[:, h, :, :], b3(4 + h)).then_inc(*t_ready.up())
                for l in range(1, LEVELS):
                    for h in range(NHEAD):
                        dve.wait_ge(*u_mm.at((l - 1) * NHEAD + h + 1))
                        if l < LEVELS - 1:
                            dve.wait_ge(*t_ready.at((l - 1) * NHEAD + h + 1))
                            nc.vector.copy_predicated(T[:, h, :, :], mask(LV + l), b3(4 + h)).then_inc(*t_ready.up())
                        nc.vector.copy_predicated(U[:, h, :, :], mask(LVT + l), b3(h)).then_inc(*u_ready.up())
        self.close()

    def stage_rwkv_scan(self):
        nc, PS = self.nc, self.PS
        pre_mm, y_ready, p_ready, u0_mm, u0_ready, sa_mm, sa_ready, z_mm, z_ready, o_mm, o_ready, step = (self.sig(n) for n in (
            "rwkv_precomputed", "rwkv_y_ready", "rwkv_p_ready", "rwkv_u0_products", "rwkv_u0_ready", "rwkv_sa_products", "rwkv_sa_ready",
            "state_products", "state_ready", "chunk_output_products", "chunk_output_ready", "dve_steps"))
        U = self.area(self.RW_U, NHEAD, TT, P)
        MAK, MRB, MRK = (self.area(o, NHEAD, TT, P) for o in (self.RW_MAK, self.RW_MRB, self.RW_MRK))
        AT, BT, KT, VT, Y, U0, O = (self.area(o, TT, GROUP) for o in (self.RW_AT, self.RW_BT, self.RW_KT, self.RW_VT, self.RW_T1, self.RW_U0, self.RW_O))
        PT, Rt = self.area(self.RW_PT, 1024), self.area(self.RW_R, 1024)
        DEC = self.area(self.RW_SMALL, 8)
        Z = self.area(self.RW_Z, 3, GROUP)
        hs = lambda h: slice(h * HD, (h + 1) * HD)
        rows = lambda h: slice((h % 2) * HD, (h % 2) * HD + HD)
        js = lambda j: slice(j * P, (j + 1) * P)
        cols = lambda j, c: slice(j * SEQ + c * P, j * SEQ + (c + 1) * P)
        with nc.Block() as block:
            @block.tensor
            def _(pe):
                for c in range(TT):
                    for h in range(NHEAD):
                        nc.tensor.matmul(PS[:, c * GROUP + h * HD:c * GROUP + (h + 1) * HD], MAK[:, h, c, :], VT[:, c, hs(h)], start=True, stop=True)
                for c in range(TT):
                    for h in range(NHEAD):
                        o = 1024 + (h // 2) * SEQ + c * P
                        mm = nc.tensor.matmul(PS[rows(h), o:o + P], AT[:, c, hs(h)], U[:, h, c, :], start=True, stop=True)
                mm.then_inc(*pre_mm.up())
                pe.wait_ge(*y_ready.at(1))
                for c in range(TT):
                    for h in range(NHEAD):
                        o = 2048 + c * GROUP + h * HD
                        mm = nc.tensor.matmul(PS[:, o:o + HD], U[:, h, c, :], Y[:, c, hs(h)], start=True, stop=True)
                mm.then_inc(*u0_mm.up())
                pe.wait_ge(*p_ready.at(1))
                pe.wait_ge(*u0_ready.at(1))
                for c in range(TT):
                    if c > 0:
                        pe.wait_ge(*z_ready.at(c))
                        for j in range(2):
                            mm = nc.tensor.matmul(self.bank(6)[:, js(j)], PT[:, cols(j, c)], Z[:, c - 1, js(j)], start=True, stop=True)
                        mm.then_inc(*sa_mm.up())
                        pe.wait_ge(*sa_ready.at(c))
                    if c < TT - 1:
                        for j in range(2):
                            nc.tensor.matmul(self.bank(7)[:, js(j)], BT[:, c, js(j)], U0[:, c, js(j)], start=True, stop=False)
                            mm = nc.tensor.matmul(self.bank(7)[:, js(j)], KT[:, c, js(j)], VT[:, c, js(j)], start=False, stop=True)
                        mm.then_inc(*z_mm.up())
                    for h in range(NHEAD):
                        o = self.bank(c)[:, hs(h)]
                        nc.tensor.matmul(o, MRB[:, h, c, :], U0[:, c, hs(h)], start=True, stop=False)
                        mm = nc.tensor.matmul(o, MRK[:, h, c, :], VT[:, c, hs(h)], start=False, stop=c == 0)
                        if c > 0:
                            mm = nc.tensor.matmul(o, Rt[:, cols(h // 2, c)], Z[:, c - 1, hs(h)], start=False, stop=True)
                    mm.then_inc(*o_mm.up())

            @block.vector
            def _(dve):
                dve.wait_ge(*pre_mm.at(1))
                nc.vector.tensor_copy(Y.rearrange("p c n -> p (c n)"), PS[:, 0:1024]).then_inc(*y_ready.up())
                dve.wait_ge(*u0_mm.at(1))
                nc.vector.tensor_copy(U0.rearrange("p c n -> p (c n)"), PS[:, 2048:3072]).then_inc(*u0_ready.up())
                dve.wait_ge(*u0_ready.at(1))
                s = Steps(dve, step)
                for c in range(TT - 1):
                    if c > 0:
                        dve.wait_ge(*sa_mm.at(c))
                        nc.vector.tensor_tensor(U0[:, c, :], U0[:, c, :], self.bank(6, GROUP), ALU.add).then_inc(*sa_ready.up())
                    dve.wait_ge(*z_mm.at(c + 1))
                    if c == 0:
                        s.link(nc.vector.tensor_copy(Z[:, 0, :], self.bank(7, GROUP)))
                    else:
                        s.link(nc.vector.tensor_tensor(Z[:, c, :], Z[:, c - 1, :], self.bank(7, GROUP), ALU.add))
                    for j in range(2):
                        ins = nc.vector.scalar_tensor_tensor(Z[:, c, js(j)], Z[:, c, js(j)], DEC[:, j * TT + c:j * TT + c + 1], self.HSUM, ALU.mult, ALU.mult)
                        if j == 0:
                            s(ins)
                        else:
                            ins.then_inc(*z_ready.up())
                    dve.wait_ge(*z_ready.at(c + 1))
                    s.wait()
                dve.wait_ge(*sa_mm.at(TT - 1))
                nc.vector.tensor_tensor(U0[:, TT - 1, :], U0[:, TT - 1, :], self.bank(6, GROUP), ALU.add).then_inc(*sa_ready.up())

            @block.scalar
            def _(act):
                act.wait_ge(*pre_mm.at(1))
                nc.scalar.activation(PT, PS[:, 1024:2048], ACT.Copy).then_inc(*p_ready.up())
                for c in range(TT):
                    act.wait_ge(*o_mm.at(c + 1))
                    nc.scalar.activation(O[:, c, :], self.bank(c, GROUP), ACT.Copy).then_inc(*o_ready.up())
        self.close()

    def out_project(self, w):
        def copy_out(engine, u, t, b):
            y = self.H[:, t, u[1]:u[1] + u[3]]
            return self.nc.vector.scalar_tensor_tensor(y, y, ALPHA, self.bank(b, u[3]), ALU.mult, ALU.add)
        self.stage_stream(w, OUT_PIECES, OUT_UNITS, FT0, copy_out, engines=1)

    def stage_layer_norm(self, row_g, row_b, out=None):
        nc, H = self.nc, self.H
        G, Bb = self.area(0, D), self.area(D, D)
        st, mv, rs = self.area(2 * D, TT, 12), self.area(2 * D + 48, TT, 2), self.area(2 * D + 64, TT)
        loaded, var_ready, root_ready, step, normed = (self.sig(n) for n in ("gain_rows_loaded", "variance_ready", "root_ready", "dve_steps", "rows_normed"))
        with nc.Block() as block:
            @block.sync
            def _(sp):
                sp.dma_start(G, row_g.partition_broadcast(P)).then_inc(*loaded.up(16))
                sp.dma_start(Bb, row_b.partition_broadcast(P)).then_inc(*loaded.up(16))

            @block.vector
            def _(dve):
                s = Steps(dve, step)
                for t in range(TT):
                    for i in range(2):
                        s(nc.vector.bn_stats(st[:, t, 6 * i:6 * i + 6], H[:, t, i * HALF:(i + 1) * HALF]))
                s.wait()
                for t in range(TT):
                    s(nc.vector.bn_aggr(mv[:, t, :], st[:, t, :]))
                s.wait()
                nc.vector.tensor_scalar(rs, mv[:, :, 1:2].rearrange("p t n -> p (t n)"), LN_EPS, None, ALU.add).then_inc(*var_ready.up())
                dve.wait_ge(*loaded.at(32))
                for t in range(TT):
                    s(nc.vector.scalar_tensor_tensor(H[:, t, :], H[:, t, :], mv[:, t, 0:1], G, ALU.subtract, ALU.mult))
                dve.wait_ge(*root_ready.at(1))
                s.link(nc.vector.reciprocal(rs, rs))
                for t in range(TT):
                    s(nc.vector.scalar_tensor_tensor(H[:, t, :], H[:, t, :], rs[:, t:t + 1], Bb, ALU.mult, ALU.add))

            @block.scalar
            def _(act):
                act.wait_ge(*var_ready.at(1))
                nc.scalar.activation(rs, rs, ACT.Sqrt).then_inc(*root_ready.up())
        self.close()

    def stage_router(self, router):
        nc, SM = self.nc, self.SM
        rw = self.area(0, DT, N_EXPERTS)
        lg, pr, top, idx, idf = self.area(64, TT, 8), self.area(96, TT, 8), self.area(128, TT, 8), self.area(160, TT, 8), self.area(192, TT, 8)
        hot, hot2, mx, sm = self.area(224, TT, 8), self.area(256, TT, 8), self.area(288, TT, 1), self.area(292, TT, 1)
        gates = SM[:, 0:32].rearrange("p (t e) -> p t e", e=8)
        loaded, mms, centred, exped, step = (self.sig(n) for n in ("router_loaded", "router_products", "router_centred", "router_exped", "dve_steps"))
        bc = lambda x: x.broadcast_to([P, TT, 8])
        with nc.Block() as block:
            @block.sync
            def _(sp):
                sp.dma_start(rw, router.rearrange("(k p) e -> p k e", p=P)).then_inc(*loaded.up(16))

            @block.tensor
            def _(pe):
                pe.wait_ge(*loaded.at(16))
                for t in range(TT):
                    for k in range(DT):
                        mm = nc.tensor.matmul(self.PS[:, t * 8:(t + 1) * 8], self.HT[:, k, t * P:(t + 1) * P], rw[:, k, :], start=k == 0, stop=k == DT - 1)
                mm.then_inc(*mms.up())

            @block.vector
            def _(dve):
                s = Steps(dve, step)
                dve.wait_ge(*mms.at(1))
                s.link(nc.vector.tensor_copy(lg, self.PS[:, 0:32].rearrange("p (t e) -> p t e", e=8)))
                s.link(nc.vector.tensor_reduce(mx, lg, AX.X, ALU.max))
                nc.vector.tensor_tensor(lg, lg, bc(mx), ALU.subtract).then_inc(*centred.up())
                dve.wait_ge(*exped.at(1))
                s.link(nc.vector.tensor_reduce(sm, pr, AX.X, ALU.add))
                s.link(nc.vector.reciprocal(sm, sm))
                s.link(nc.vector.tensor_tensor(pr, pr, bc(sm), ALU.mult))
                for t in range(TT):
                    s(nc.vector.max(top[:, t, :], pr[:, t, :]))
                s.wait()
                for t in range(TT):
                    s(nc.vector.max_index(idx[:, t, :].bitcast(U32), top[:, t, :], pr[:, t, :]))
                s.wait()
                s.link(nc.vector.tensor_copy(idf, idx.bitcast(U32)))
                s.link(nc.vector.tensor_tensor(sm, top[:, :, 0:1], top[:, :, 1:2], ALU.add))
                s.link(nc.vector.reciprocal(sm, sm))
                iota = self.cf("iota8").unsqueeze(1).broadcast_to([P, TT, 8])
                for i, h in enumerate((hot, hot2)):
                    s.link(nc.vector.tensor_tensor(h, iota, bc(idf[:, :, i:i + 1]), ALU.is_equal))
                    s.link(nc.vector.tensor_tensor(h, h, bc(top[:, :, i:i + 1]), ALU.mult))
                s.link(nc.vector.tensor_tensor(hot, hot, hot2, ALU.add))
                s.link(nc.vector.tensor_tensor(gates, hot, bc(sm), ALU.mult))

            @block.scalar
            def _(act):
                act.wait_ge(*centred.at(1))
                nc.scalar.activation(pr, lg, ACT.Exp).then_inc(*exped.up())
        self.close()

    def block_one(self):
        ap = self.ap
        Y = self.HT.rearrange("p k t -> p (k t)").rearrange("p (t d) -> p t d", d=D)
        S = self.area(8192, 2048)
        Qc, KD, KT = self.area(10240, 1024), self.area(11264, 1024), self.area(12288, 1024)
        DEC, Z, O, kf = self.area(13312, 8), self.area(13320, 3, GROUP), self.area(14336, TT, GROUP), self.area(15360, 1024)
        SQ, g1, x1 = self.area(16384, TT, GROUP), self.area(17408, SEQ), self.area(17920, SEQ)
        ygrp = lambda m: Y[:, :, m * GROUP:(m + 1) * GROUP]
        row = lambda i: self.area(FT0 - 1024 + i * GROUP, GROUP)
        pieces_in = lambda l: self.first_pieces(ap["w_in"][l], IN_PIECES, HT0)
        self.stage_load(pieces_in(0))
        self.stage_to_feature(self.H, None, split=self.XR)
        for l in range(2):
            rows = ap["rows"]
            self.project(ap["w_in"][l], IN_PIECES, IN_UNITS, rows[l * 5 + 4], self.ft, self.tok)
            self.stage_hgrn_gates(l, kf)
            self.stage_decay_scores(self.ft(HQ, 2), kf, self.ft(HF, 2), 2, HD, S, Qc, KD, DEC, 0)
            self.stage_state(S, Qc, KD, DEC, self.tok(0), 2, HD, O, KT.rearrange("p (c n) -> p c n", n=GROUP), Z)
            self.stage_head_norm(O, SQ, self.tok(256), ygrp(0), RMS_EPS, gain=row(0))
            self.stage_gla_gates(l, g1, x1)
            self.stage_decay_scores(self.ft(GQ), self.ft(GK), g1, 1, 32, S, Qc[:, 0:SEQ], KD[:, 0:SEQ], DEC[:, 0:4], 0)
            self.stage_state(S, Qc, KD, DEC, self.tok(512), 1, 32, O, KT[:, 0:SEQ].rearrange("p (c n) -> p c n", n=P), Z)
            self.stage_head_norm(O, SQ, self.tok(768), ygrp(1), RMS_EPS, gain=row(1))
            self.stage_retention_scores(S, Qc, KD, DEC, 0)
            self.stage_state(S, Qc, KD, DEC, self.tok(1024), 2, HD, O, KT.rearrange("p (c n) -> p c n", n=GROUP), Z)
            self.stage_head_norm(O, SQ, self.tok(1280), ygrp(3), LN_EPS, center=True)
            self.stage_rwkv_gates(l)
            self.stage_rwkv_scores(l)
            self.stage_rwkv_solve()
            self.stage_rwkv_scan()
            self.stage_head_norm(self.area(self.RW_O, TT, GROUP), self.area(self.RW_T2, TT, GROUP), self.area(self.RW_G, TT, GROUP), ygrp(2), LNX_EPS,
                                 center=True, gain=row(2), bias=row(3), silu_gate=False,
                                 bonus=(self.area(self.RW_VT, TT, GROUP), self.area(self.RW_SMALL + 16, 16)))
            self.stage_to_feature(Y, None, split=self.XR, ahead=self.first_pieces(ap["w_out"][l], OUT_PIECES, FT0))
            self.out_project(ap["w_out"][l])
            self.stage_layer_norm(rows[l * 5], rows[l * 5 + 1])
            if l == 0:
                split = lambda w: w.rearrange("d (e f) -> e d f", f=FPASS)
                gw, uw = split(ap["ffn_w_gate"][0]), split(ap["ffn_w_up"][0])
                dw = ap["ffn_w_down"][0].rearrange("(e f) d -> e f d", f=FPASS)
                self.stage_to_feature(self.H, None, src_factor=ALPHA, split=self.XR, ahead=self.first_units(gw[0], uw[0]))
                self.stage_ffn(2, lambda i: gw[i], lambda i: uw[i], lambda i: dw[i])
            else:
                self.stage_to_feature(self.H, self.HT)
                self.stage_router(ap["moe_router"][0])
                gwm, uwm, dwm = ap["moe_w_gate"][0], ap["moe_w_up"][0], ap["moe_w_down"][0]
                self.stage_slots(ahead=self.first_units(gwm[0], uwm[0], "moe", FRING))
                self.stage_moe(lambda i, ahead=0: gwm[ahead:][i], lambda i, ahead=0: uwm[ahead:][i], lambda i: dwm[i])
            self.stage_layer_norm(rows[l * 5 + 2], rows[l * 5 + 3])
            if l == 0:
                self.stage_to_feature(self.H, None, split=self.XR, ahead=pieces_in(1))

    def stage_slots(self, ahead):
        nc, H, HR, SM = self.nc, self.H, self.HR, self.SM
        sel, selc, tri, ones = self.area(SLOT_TMP, TT, 8), self.area(SLOT_TMP + 32, TT, 8), self.area(SLOT_TMP + 64, P), self.area(SLOT_TMP + 192, P)
        tot, mx, nb = self.area(SLOT_TMP + 320, 8), self.area(SLOT_TMP + 328, 1), self.area(SLOT_TMP + 329, 1)
        gates = SM[:, 0:32].rearrange("p (t e) -> p t e", e=8)
        SVW = self.SVW
        step, rounded, ready, mms, iota_in = (self.sig(n) for n in ("dve_steps", "tokens_rounded", "slot_inputs_ready", "slot_products", "slot_iota_loaded"))
        FAR = -4096.0
        with nc.Block() as block:
            @block.sync
            def _(sp):
                sp.dma_start(self.IOTA, self.ap["slot_iota"].partition_broadcast(P)).then_inc(*iota_in.up(16))
                ahead(sp)
                sp.wait_ge(*iota_in.at(16))

            @block.scalar
            def _(act):
                nc.scalar.activation(HR[:, 0], H, ACT.Copy).then_inc(*rounded.up())

            @block.vector
            def _(dve):
                s = Steps(dve, step)
                s.link(nc.vector.tensor_scalar(sel, gates, 0.0, None, ALU.is_gt))
                s(nc.vector.tensor_copy(tri, self.MASK[:, STRICT * P:(STRICT + 1) * P]))
                s(nc.vector.memset(ones, 1.0))
                s.link(nc.vector.memset(selc[:, 0, :], 0.0))
                for t in range(1, TT):
                    s.link(nc.vector.tensor_tensor(selc[:, t, :], selc[:, t - 1, :], sel[:, t - 1, :], ALU.add))
                nc.vector.tensor_tensor(tot, selc[:, TT - 1, :], sel[:, TT - 1, :], ALU.add).then_inc(*ready.up())
                dve.wait_ge(*rounded.at(1))
                s.link(nc.vector.tensor_tensor(HR[:, 1], H, HR[:, 0].bitcast(F32), ALU.subtract))
                s.link(nc.vector.tensor_scalar(H, H, ALPHA, None, ALU.mult))
                dve.wait_ge(*mms.at(1))
                s.link(nc.vector.tensor_reduce(mx, self.bank(1, 8), AX.X, ALU.max))
                s.link(nc.vector.memset(nb, 1.0))
                for b in range(1, NBLK):
                    s.link(nc.vector.scalar_tensor_tensor(nb, mx, float(b * CAP), nb, ALU.is_gt, ALU.add))
                s(nc.vector.tensor_copy(self.NBI, nb))
                s(nc.vector.memset(SVW, FAR))
                s.link(nc.vector.tensor_scalar(selc, self.bank(0, 32).rearrange("p (t e) -> p t e", e=8), -FAR, None, ALU.add))
                s.link(nc.vector.tensor_tensor(selc, selc, sel, ALU.mult))
                for b in range(NBLK):
                    s(nc.vector.tensor_scalar(SVW[:, :, b * 8:(b + 1) * 8], selc, FAR - b * CAP, None, ALU.add))

            @block.tensor
            def _(pe):
                pe.wait_ge(*ready.at(1))
                flat = lambda x: x.rearrange("p t e -> p (t e)")
                nc.tensor.matmul(self.bank(0, 32), tri, flat(sel), start=True, stop=False)
                nc.tensor.matmul(self.bank(0, 32), ones, flat(selc), start=False, stop=True)
                nc.tensor.matmul(self.bank(1, 8), ones, tot, start=True, stop=True).then_inc(*mms.up())
        self.close()

    def stage_moe(self, gate_w, up_w, down_w):
        nc, H, HR, HID, TMP, XE, PSEL, PT, YE = self.nc, self.H, self.HR, self.HIDS, self.TMP, self.XE, self.PSEL, self.PT, self.YE
        GSPL, DSPL, GRAW, DRAW, SM = self.GSPL, self.DSPL, self.GRAW, self.DRAW, self.SM
        N, E, DU = CAP, N_EXPERTS, 2 * FU
        gates = SM[:, 0:32].rearrange("p (t e) -> p t e", e=8)
        g_loaded = [self.sig(f"moe_gate_up_loaded{r}") for r in range(FRING)]
        d_loaded = [self.sig(f"moe_down_loaded{r}") for r in range(FRING)]
        g_mm, d_mm, halves = self.sig("moe_gate_up_products"), self.sig("moe_down_products"), self.sig("moe_part_sums_ready")
        (g_hi, g_lo, d_hi, d_lo, silu_done, prod_done, hid_hi, hid_lo, acc_done, pick_ready, pick_turned, pt_ready, gathered,
         x_hi, x_lo, y_hi, y_lo, scattered) = (self.sig("moe_" + n) for n in (
            "gate_up_hi_ready", "gate_up_lo_ready", "down_hi_ready", "down_lo_ready", "silu_done", "hidden_product_done", "hidden_hi_ready", "hidden_lo_ready",
            "sum_done", "pick_ready", "pick_turned", "scatter_matrix_ready", "gathered", "tokens_hi_ready", "tokens_lo_ready", "outputs_hi_ready", "outputs_lo_ready",
            "scattered"))
        uses = lambda L, r: len(range(r, L, FRING))
        TILES = (0, N - P)
        SBANK = (4, 5, 2, 3, 4, 5, 6, 7)
        XB = [(k // 3, (k % 3) * N) for k in range(DT)]

        def before(f, L):
            return f - FRING + 1 if f >= FRING else max(u for u in range(L) if u % FRING == f % FRING) - L + 1

        def wait(eng, w, c, L, k):
            eng.wait_ge(c.sem, c.base + w * L + k)

        def passes(eng, body):
            nb = eng.value_load(self.NBI[0:1, 0:1], min_val=1, max_val=NBLK)
            with eng.Fori(0, nb) as b:
                with eng.Fori(0, E) as e:
                    body(b * E + e, e)

        with nc.Block() as block:
            @block.sync
            def _(sp):
                def load_g(w, e, f, k=0, ahead=0):
                    for c in (g_hi, g_lo):
                        wait(sp, w, c, FU, before(f, FU) + k)
                    r = f % FRING
                    for u, wt in enumerate((gate_w, up_w)):
                        sp.dma_start(GRAW[:, r, u * D:(u + 1) * D].rearrange("p (k f) -> p k f", k=DT),
                                     wt(e, ahead)[:, f * P:(f + 1) * P].rearrange("(k p) f -> p k f", p=P)).then_inc(g_loaded[r].sem, 16)

                def load_d(w, e, n):
                    half, f = divmod(n, FU)
                    for c in (d_hi, d_lo):
                        wait(sp, w, c, DU, before(n, DU))
                    sp.dma_start(DRAW[:, n % FRING, :], down_w(e)[f * P:(f + 1) * P, half * HALF:(half + 1) * HALF]).then_inc(d_loaded[n % FRING].sem, 16)

                def body(w, e, after, ahead):
                    for f in range(FU):
                        load_d(w, e, f)
                        if f + 3 < FU:
                            load_g(w, e, f + 3)
                    for f in range(FU):
                        load_d(w, e, FU + f)
                        if f in (2, 5, 8):
                            load_g(w, after, f // 3, FU, ahead)

                nb = sp.value_load(self.NBI[0:1, 0:1], min_val=1, max_val=NBLK)
                with sp.Fori(0, nb) as b:
                    with sp.Fori(0, E - 1) as e:
                        body(b * E + e, e, e, 1)
                    with sp.Fori(E - 1, E) as e:
                        body(b * E + e, e, 0, 0)

            @block.tensor
            def _(pe):
                def gather():
                    for k, (b, o) in enumerate(XB):
                        for t in range(TT):
                            for s in range(2):
                                mm = nc.tensor.matmul(self.bank(b)[:, o:o + N], HR[:, s, t, k * P:(k + 1) * P], PSEL[:, t, :],
                                                      start=t + s == 0, stop=t == TT - 1 and s == 1)
                    mm.then_inc(gathered.sem, 1)

                def gate_up(w, f, k=0):
                    wait(pe, w, g_hi, FU, f + 1 + k * FU)
                    wait(pe, w, g_lo, FU, f + 1 + k * FU)
                    if f >= 2:
                        wait(pe, w, halves, FU, f - 1)
                    else:
                        wait(pe, w, x_lo, 1, 1 + k)
                        wait(pe, w, acc_done, 2 * TT, -TT + k * 2 * TT)
                    r = f % FRING
                    for u in range(2):
                        out = self.bank(2 * (f % 2) + u, 2 * N)
                        for k8 in range(DT):
                            wt = [GSPL[:, r, s, (u * DT + k8) * P:(u * DT + k8 + 1) * P] for s in range(2)]
                            hi = lambda start, stop: nc.tensor.matmul(out, wt[0], XE[:, k8, :, :].rearrange("p s n -> p (s n)"), start=start, stop=stop)
                            lo = lambda: nc.tensor.matmul(out[:, N:2 * N], wt[1], XE[:, k8, 0, :], start=False, stop=False)
                            if k8 < DT - 1:
                                hi(k8 == 0, False)
                                lo()
                            else:
                                lo()
                                mm = hi(False, True)
                    mm.then_inc(g_mm.sem, 1)

                def down(w, n):
                    half, f = divmod(n, FU)
                    wait(pe, w, d_hi, DU, n + 1)
                    wait(pe, w, d_lo, DU, n + 1)
                    if half == 0:
                        wait(pe, w, hid_lo, FU, f + 1)
                    if f == 0:
                        wait(pe, w, acc_done, 2 * TT, 0)
                        wait(pe, w, pt_ready, 2, 2)
                    for j, s0 in enumerate(TILES):
                        x = [HID[:, s, f, s0:s0 + P] for s in range(2)]
                        wt = [DSPL[:, n % FRING, s, :] for s in range(2)]
                        out = self.bank(4 + 2 * half + j)
                        nc.tensor.matmul(out, x[0], wt[0], start=f == 0, stop=False)
                        nc.tensor.matmul(out, x[0], wt[1], start=False, stop=False)
                        mm = nc.tensor.matmul(out, x[1], wt[0], start=False, stop=f == FU - 1)
                    mm.then_inc(d_mm.sem, 1)

                def turn_pick(w):
                    wait(pe, w, acc_done, 2 * TT, 0)
                    for j, s0 in enumerate(TILES):
                        for t in range(TT):
                            mm = nc.tensor.transpose(self.bank(6 + j)[:, t * P:(t + 1) * P], PSEL[:, t, s0:s0 + P].bitcast(F32), self.cf("ident"))
                        mm.then_inc(pick_turned.sem, 1)

                def scatter(w, half):
                    wait(pe, w, y_lo, 2, half + 1)
                    for t in range(TT):
                        n = half * TT + t
                        if n in (4, 5):
                            wait(pe, w, acc_done, 2 * TT, n - 3)
                        if n in (2, 3):
                            wait(pe, w, x_lo, 1, 2)
                        for j in range(2):
                            for s in range(2):
                                mm = nc.tensor.matmul(self.bank(SBANK[n]), PT[:, j, t * P:(t + 1) * P], YE[:, s, j, half * HALF:(half + 1) * HALF],
                                                      start=j + s == 0, stop=j + s == 2)
                        mm.then_inc(scattered.sem, 1)

                def body(w, e):
                    for f in range(1, FU):
                        gate_up(w, f)
                        if f == 2:
                            turn_pick(w)
                        if f >= 2:
                            down(w, f - 2)
                    down(w, FU - 2)
                    down(w, FU - 1)
                    wait(pe, w, pick_ready, 1, 2)
                    wait(pe, w, halves, FU, FU)
                    gather()
                    for f in range(FU):
                        down(w, FU + f)
                        if f == 6:
                            scatter(w, 0)
                    gate_up(w, 0, 1)
                    scatter(w, 1)

                pe.wait_ge(pick_ready.sem, pick_ready.base + 1)
                gather()
                gate_up(0, 0)
                passes(pe, body)

            @block.scalar
            def _(act):
                def split_g(w, f, k=0):
                    r = f % FRING
                    act.wait_ge(g_loaded[r].sem, g_loaded[r].base + 32 * (w * uses(FU, r) + f // FRING) + 32 * k * uses(FU, r))
                    wait(act, w, g_mm, FU, before(f, FU) + k * FU)
                    nc.scalar.activation(GSPL[:, r, 0, :], GRAW[:, r, :], ACT.Copy).then_inc(g_hi.sem, 1)

                def split_d(w, n):
                    r = n % FRING
                    act.wait_ge(d_loaded[r].sem, d_loaded[r].base + 16 * (w * uses(DU, r) + n // FRING + 1))
                    wait(act, w, d_mm, DU, before(n, DU))
                    nc.scalar.activation(DSPL[:, r, 0, :], DRAW[:, r, :], ACT.Copy).then_inc(d_hi.sem, 1)

                def tokens_hi(count):
                    act.wait_ge(gathered.sem, count)
                    for b in range(3):
                        n = min(3, DT - 3 * b)
                        ins = nc.scalar.activation(XE[:, 3 * b:3 * b + n, 0, :], self.bank(b, n * N).rearrange("p (k n) -> p k n", n=N), ACT.Copy)
                    ins.then_inc(x_hi.sem, 1)

                def outputs_hi(w, half):
                    wait(act, w, d_mm, DU, (half + 1) * FU)
                    wait(act, w, scattered, 2 * TT, 0)
                    nc.scalar.activation(YE[:, 0, :, half * HALF:(half + 1) * HALF], self.PS[:, (4 + 2 * half) * HALF:(6 + 2 * half) * HALF].rearrange("p (j n) -> p j n", n=HALF),
                                         ACT.Copy).then_inc(y_hi.sem, 1)

                def body(w, e):
                    split_d(w, 0)
                    for f in range(FU):
                        wait(act, w, halves, FU, f + 1)
                        nc.scalar.activation(TMP[:, f % 2, 0:N], TMP[:, f % 2, 0:N], ACT.Silu).then_inc(silu_done.sem, 1)
                        wait(act, w, prod_done, FU, f + 1)
                        wait(act, w, d_mm, DU, 0)
                        nc.scalar.activation(HID[:, 0, f, :], TMP[:, f % 2, 0:N], ACT.Copy).then_inc(hid_hi.sem, 1)
                        if f == 2:
                            wait(act, w, pick_turned, 2, 2)
                            nc.scalar.activation(PT[:, 0, :], self.bank(6), ACT.Copy).then_inc(pt_ready.sem, 1)
                            nc.scalar.activation(PT[:, 1, :], self.bank(7), ACT.Copy, scale=self.cf("tail")).then_inc(pt_ready.sem, 1)
                        if f + 3 < FU:
                            split_g(w, f + 3)
                        split_d(w, f + 1)
                    split_d(w, FU + 1)
                    outputs_hi(w, 0)
                    tokens_hi(gathered.base + w + 2)
                    for f in range(2, FU):
                        split_d(w, FU + f)
                        if f in (4, 6, 8):
                            split_g(w, f // 2 - 2, 1)
                    outputs_hi(w, 1)

                tokens_hi(gathered.base + 1)
                for f in range(FRING):
                    split_g(0, f)
                passes(act, body)

            @block.vector
            def _(dve):
                def split_g(w, f, k=0):
                    r = f % FRING
                    wait(dve, w, g_hi, FU, f + 1 + k * FU)
                    nc.vector.tensor_tensor(GSPL[:, r, 1, :], GRAW[:, r, :], GSPL[:, r, 0, :].bitcast(F32), ALU.subtract).then_inc(g_lo.sem, 1)

                def split_d(w, n):
                    r = n % FRING
                    wait(dve, w, d_hi, DU, n + 1)
                    nc.vector.tensor_tensor(DSPL[:, r, 1, :], DRAW[:, r, :], DSPL[:, r, 0, :].bitcast(F32), ALU.subtract).then_inc(d_lo.sem, 1)

                def tokens_lo(count):
                    dve.wait_ge(x_hi.sem, count)
                    for b in range(3):
                        n = min(3, DT - 3 * b)
                        ins = nc.vector.tensor_tensor(XE[:, 3 * b:3 * b + n, 1, :], self.bank(b, n * N).rearrange("p (k n) -> p k n", n=N),
                                                      XE[:, 3 * b:3 * b + n, 0, :].bitcast(F32), ALU.subtract)
                    ins.then_inc(x_lo.sem, 1)

                def outputs_lo(w, half):
                    wait(dve, w, y_hi, 2, half + 1)
                    cols = slice(half * HALF, (half + 1) * HALF)
                    nc.vector.tensor_tensor(YE[:, 1, :, cols], self.PS[:, (4 + 2 * half) * HALF:(6 + 2 * half) * HALF].rearrange("p (j n) -> p j n", n=HALF),
                                            YE[:, 0, :, cols].bitcast(F32), ALU.subtract).then_inc(y_lo.sem, 1)

                def pick(at):
                    for t in range(TT):
                        ins = nc.vector.tensor_scalar(PSEL[:, t, :], self.IOTA, self.SVW[:, t, bass.ds(at, 1)], None, ALU.is_equal)
                    ins.then_inc(pick_ready.sem, 1)

                def add(w, e, n):
                    half, t = divmod(n, TT)
                    y = H[:, t, half * HALF:(half + 1) * HALF]
                    wait(dve, w, scattered, 2 * TT, n + 1)
                    wait(dve, w, acc_done, 2 * TT, n)
                    nc.vector.scalar_tensor_tensor(y, self.bank(SBANK[n]), gates[:, t, bass.ds(e, 1)], y, ALU.mult, ALU.add).then_inc(acc_done.sem, 1)

                def body(w, e):
                    for f in range(FU):
                        if 0 < f < FU - 1:
                            split_g(w, f + 1)
                        split_d(w, f)
                        wait(dve, w, g_mm, FU, f + 1)
                        wait(dve, w, hid_lo, FU, f - 1)
                        nc.vector.tensor_reduce(TMP[:, f % 2, 0:2 * N].rearrange("p (u n) -> p u n", u=2),
                                                self.PS[:, 2 * (f % 2) * HALF:(2 * (f % 2) + 2) * HALF].rearrange("p (u c) -> p u c", u=2)[:, :, 0:2 * N]
                                                .rearrange("p u (s n) -> p u n s", s=2), AX.X, ALU.add).then_inc(halves.sem, 1)
                        wait(dve, w, silu_done, FU, f + 1)
                        nc.vector.tensor_tensor(TMP[:, f % 2, 0:N], TMP[:, f % 2, 0:N], TMP[:, f % 2, N:2 * N], ALU.mult).then_inc(prod_done.sem, 1)
                        wait(dve, w, hid_hi, FU, f + 1)
                        nc.vector.tensor_tensor(HID[:, 1, f, :], TMP[:, f % 2, 0:N], HID[:, 0, f, :].bitcast(F32), ALU.subtract).then_inc(hid_lo.sem, 1)
                        if f == 3:
                            wait(dve, w, pick_turned, 2, 2)
                            pick(w + 1)
                    split_d(w, FU)
                    split_d(w, FU + 1)
                    outputs_lo(w, 0)
                    tokens_lo(x_hi.base + w + 2)
                    for f in range(2, FU):
                        split_d(w, FU + f)
                        if f in (5, 7):
                            split_g(w, f // 7, 1)
                        if f >= FU - 2:
                            add(w, e, 2 * (f - FU + 2))
                            add(w, e, 2 * (f - FU + 2) + 1)
                    outputs_lo(w, 1)
                    for n in range(TT, 2 * TT):
                        add(w, e, n)

                pick(0)
                tokens_lo(x_hi.base + 1)
                split_g(0, 0)
                split_g(0, 1)
                passes(dve, body)
        self.close()

    def stage_begin_two(self):
        nc, ap = self.nc, self.ap
        loaded, copied = self.sig("inputs_loaded"), self.sig("residual_added")
        with nc.Block() as block:
            @block.sync
            def _(sp):
                sp.dma_start(self.PAR[:, 0:64], ap["par2"]).then_inc(*loaded.up(16))
                sp.wait_ge(*loaded.at(16))

            @block.vector
            def _(dve):
                nc.vector.tensor_copy(self.X2, self.H).then_inc(*copied.up())
        self.close()

    def root_mean_square(self, dve, s, x, junk, ss, n, eps, var_ready, root_ready, factor=1.0):
        nc = self.nc
        s.link(nc.vector.tensor_tensor(junk, x, x, ALU.mult))
        s.link(nc.vector.tensor_reduce(ss, junk, AX.X, ALU.add))
        nc.vector.tensor_scalar(ss, ss, 1.0 / n, eps, ALU.mult, ALU.add).then_inc(*var_ready.up())
        dve.wait_ge(*root_ready.at(1))
        s.link(nc.vector.reciprocal(ss, ss))
        if factor != 1.0:
            s.link(nc.vector.tensor_scalar(ss, ss, factor, None, ALU.mult))

    def norm_factor(self, dve, s, ss, sums, var_ready, root_ready, nth, factor=1.0):
        nc = self.nc
        dve.wait_ge(*sums.at(nth * TT))
        nc.vector.tensor_scalar(ss, ss, 1.0 / D, RMS_EPS, ALU.mult, ALU.add).then_inc(*var_ready.up())
        dve.wait_ge(*root_ready.at(nth))
        if factor != 1.0:
            s.link(nc.vector.reciprocal(ss, ss))
            s(nc.vector.tensor_scalar(ss, ss, factor, None, ALU.mult))
        else:
            s(nc.vector.reciprocal(ss, ss))
        s.wait()

    def stage_pre_norm(self):
        nc, H, X2 = self.nc, self.H, self.X2
        ss = self.SM[:, 64:68]
        step, sums, var_ready, root_ready, factor_ready, normed = (self.sig(n) for n in (
            "dve_steps", "squares_summed", "variance_ready", "root_ready", "norm_factor_ready", "rows_normed"))
        with nc.Block() as block:
            @block.scalar
            def _(act):
                for t in range(TT):
                    nc.scalar.activation(H[:, t, :], X2[:, t, :], ACT.Square, accum_out=ss[:, t:t + 1]).then_inc(*sums.up())
                act.wait_ge(*var_ready.at(1))
                nc.scalar.activation(ss, ss, ACT.Sqrt).then_inc(*root_ready.up())
                act.wait_ge(*factor_ready.at(1))
                for t in (1, 3):
                    nc.scalar.activation(H[:, t, :], X2[:, t, :], ACT.Copy, scale=ss[:, t:t + 1]).then_inc(*normed.up())

            @block.vector
            def _(dve):
                s = Steps(dve, step)
                self.norm_factor(dve, s, ss, sums, var_ready, root_ready, 1)
                dve.sem_inc(*factor_ready.up())
                for t in (0, 2):
                    s(nc.vector.tensor_scalar(H[:, t, :], X2[:, t, :], ss[:, t:t + 1], None, ALU.mult))
        self.close()

    def stage_post_norm(self, row, factor, last=False):
        nc, H, X2, out = self.nc, self.H, self.X2, self.ap["out"]
        ss, ss2, G, junk = self.SM[:, 64:68], self.SM[:, 68:72], self.area(0, D), self.area(4096, TT, D)
        step, sums, var_ready, root_ready, factor_ready, added, scaled, normed, loaded, stored = (self.sig(n) for n in (
            "dve_steps", "squares_summed", "variance_ready", "root_ready", "norm_factor_ready", "residual_added", "rows_scaled", "rows_normed", "gain_rows_loaded",
            "output_stored"))
        with nc.Block() as block:
            @block.sync
            def _(sp):
                sp.dma_start(G, row.partition_broadcast(P)).then_inc(*loaded.up(16))
                if last:
                    for t in range(TT):
                        sp.wait_ge(*added.at(t + 1))
                        sp.dma_start(out[0, t * P:(t + 1) * P, :], X2[:, t, :]).then_inc(*stored.up(16))
                    sp.wait_ge(*stored.at(16 * TT))

            @block.scalar
            def _(act):
                for t in range(TT):
                    nc.scalar.activation(junk[:, t, :], H[:, t, :], ACT.Square, accum_out=ss[:, t:t + 1]).then_inc(*sums.up())
                act.wait_ge(*var_ready.at(1))
                nc.scalar.activation(ss, ss, ACT.Sqrt).then_inc(*root_ready.up())
                if not last:
                    act.wait_ge(*sums.at(TT))
                    for t in range(TT):
                        act.wait_ge(*added.at(t + 1))
                        nc.scalar.activation(junk[:, t, :], X2[:, t, :], ACT.Square, accum_out=ss2[:, t:t + 1]).then_inc(*sums.up())
                    act.wait_ge(*var_ready.at(2))
                    nc.scalar.activation(ss2, ss2, ACT.Sqrt).then_inc(*root_ready.up())
                    act.wait_ge(*factor_ready.at(1))
                    for t in (1, 3):
                        nc.scalar.activation(H[:, t, :], X2[:, t, :], ACT.Copy, scale=ss2[:, t:t + 1]).then_inc(*normed.up())

            @block.vector
            def _(dve):
                s = Steps(dve, step)
                self.norm_factor(dve, s, ss, sums, var_ready, root_ready, 1, factor)
                dve.wait_ge(*loaded.at(16))
                for t in range(TT + 1):
                    if t < TT:
                        nc.vector.scalar_tensor_tensor(H[:, t, :], H[:, t, :], ss[:, t:t + 1], G, ALU.mult, ALU.mult).then_inc(*scaled.up())
                    if t > 0:
                        dve.wait_ge(*scaled.at(t))
                        nc.vector.tensor_tensor(X2[:, t - 1, :], X2[:, t - 1, :], H[:, t - 1, :], ALU.add).then_inc(*added.up())
                if not last:
                    dve.wait_ge(*added.at(TT))
                    self.norm_factor(dve, s, ss2, sums, var_ready, root_ready, 2)
                    dve.sem_inc(*factor_ready.up())
                    for t in (0, 2):
                        s(nc.vector.tensor_scalar(H[:, t, :], X2[:, t, :], ss2[:, t:t + 1], None, ALU.mult))
        self.close()

    def stage_lru(self, YT, rl):
        nc, ap, PS = self.nc, self.ap, self.PS
        x, gate = (self.ft(i, 4).rearrange("p (j t) -> p j t", t=SEQ) for i in (L2X, L2G))
        xc, r, ig, th, u, h = (self.area(o, 4, SEQ) for o in (0, 2048, 4096, 6144, 8192, 12288))
        Wr, Wi = self.area(10240, 4, P), self.area(10752, 4, P)
        ls, l1, ones = self.area(11264, 4), self.area(11268, 4), self.area(11272, 1)
        zeroed, loaded, step, astep, conv_ready, mms, gates, lam_ready, logits, th_ready, var_ready, root_ready, gelu_ready, sq_ready, sum_mm = (self.sig(n) for n in (
            "lru_weights_zeroed", "mixer_tables_loaded", "dve_steps", "act_steps", "lru_conv_ready", "lru_gate_products", "lru_gates_ready",
            "lru_lambda_ready", "lru_log_a_ready", "lru_tanh_ready", "lru_square_ready", "root_ready", "lru_gelu_ready", "lru_squares_ready", "lru_square_sums"))
        col = lambda base, j: self.PAR[:, base + j:base + j + 1]
        with nc.Block() as block:
            @block.gpsimd
            def _(pool):
                for w in (Wr, Wi):
                    nc.gpsimd.memset(w, 0.0).then_inc(*zeroed.up())

            @block.sync
            def _(sp):
                sp.wait_ge(*zeroed.at(2))
                for w, name in ((Wr, "w_rg_2"), (Wi, "w_ig_2")):
                    src = ap[name][0].rearrange("(j b) i o -> b i j o", b=2)
                    for b in range(2):
                        a = slice(b * HD, (b + 1) * HD)
                        sp.dma_start(w[a, :, a], src[b]).then_inc(*loaded.up(16))

            @block.vector
            def _(dve):
                s = Steps(dve, step)
                for j in range(4):
                    s(nc.vector.tensor_scalar(xc[:, j, :], x[:, j, :], col(CONV_W + 12, j), col(CONV_B, j), ALU.mult, ALU.add))
                for d in range(1, 4):
                    s.wait()
                    for j in range(4):
                        ins = nc.vector.scalar_tensor_tensor(xc[:, j, d:SEQ], x[:, j, 0:SEQ - d], col(CONV_W + 4 * (3 - d), j), xc[:, j, d:SEQ], ALU.mult, ALU.add)
                        if d == 3:
                            ins.then_inc(*conv_ready.up())
                        else:
                            s(ins)
                lam = self.PAR[:, LAM:LAM + 4]
                s.link(nc.vector.tensor_scalar(l1, lam, 0.0, None, ALU.min))
                dve.wait_ge(*lam_ready.at(1))
                s.link(nc.vector.tensor_tensor(ls, l1, ls, ALU.subtract))
                s.link(nc.vector.tensor_scalar(ls, ls, -4.0, None, ALU.mult))
                s.link(nc.vector.memset(ones, 1.0))
                for j in range(4):
                    dve.wait_ge(*gates.at(2 * j + 1))
                    nc.vector.tensor_scalar(th[:, j, :], r[:, j, :], ls[:, j:j + 1], None, ALU.mult).then_inc(*logits.up())
                dve.wait_ge(*gates.at(8))
                s.link(nc.vector.tensor_tensor(u, ig, xc, ALU.mult))
                dve.wait_ge(*th_ready.at(4))
                s.link(nc.vector.tensor_scalar(r, th, 1.0, None, ALU.add))
                s.link(nc.vector.reciprocal(r, r))
                s.link(nc.vector.tensor_tensor(th, th, r, ALU.mult))
                s.link(nc.vector.tensor_scalar(th, th, 2.0, None, ALU.mult))
                s.link(nc.vector.tensor_scalar(r, th, -1.0, 1.0, ALU.mult, ALU.add))
                nc.vector.scalar_tensor_tensor(th, r, 1.0, th, ALU.add, ALU.mult).then_inc(*var_ready.up())
                dve.wait_ge(*root_ready.at(1))
                s.link(nc.vector.tensor_tensor(u, u, th, ALU.mult))
                for j in range(4):
                    s(nc.vector.tensor_tensor_scan(h[:, j, :], r[:, j, :], u[:, j, :], 0.0, ALU.mult, ALU.add))
                s.wait()
                dve.wait_ge(*gelu_ready.at(1))
                s.link(nc.vector.tensor_tensor(h, h, gate, ALU.mult))
                nc.vector.tensor_tensor(th, h, h, ALU.mult).then_inc(*sq_ready.up())
                for j in range(4):
                    s(nc.vector.tensor_scalar(YT[:, j, :], h[:, j, :], col(G_OUT, j), None, ALU.mult))
                dve.wait_ge(*sum_mm.at(1))
                nc.vector.tensor_scalar(rl, PS[:, 0:TT], 1.0 / 512, RMS_EPS, ALU.mult, ALU.add).then_inc(*var_ready.up())
                dve.wait_ge(*root_ready.at(2))
                s(nc.vector.reciprocal(rl, rl))

            @block.scalar
            def _(act):
                s = Steps(act, astep)
                s.link(nc.scalar.activation(ls, self.PAR[:, LAM:LAM + 4], ACT.Abs))
                s.link(nc.scalar.activation(ls, ls, ACT.Exp, scale=-1.0))
                nc.scalar.activation(ls, ls, ACT.Ln, bias=1.0).then_inc(*lam_ready.up())
                for j in range(4):
                    act.wait_ge(*mms.at(j + 1))
                    nc.scalar.activation(r[:, j, :], self.bank(2 * j), ACT.Sigmoid, bias=col(B_RG, j)).then_inc(*gates.up())
                    nc.scalar.activation(ig[:, j, :], self.bank(2 * j + 1), ACT.Sigmoid, bias=col(B_IG, j)).then_inc(*gates.up())
                for j in range(4):
                    act.wait_ge(*logits.at(j + 1))
                    nc.scalar.activation(th[:, j, :], th[:, j, :], ACT.Tanh).then_inc(*th_ready.up())
                nc.scalar.activation(gate, gate, ACT.Gelu_apprx_tanh).then_inc(*gelu_ready.up())
                act.wait_ge(*var_ready.at(1))
                nc.scalar.activation(th, th, ACT.Sqrt).then_inc(*root_ready.up())
                act.wait_ge(*var_ready.at(2))
                nc.scalar.activation(rl, rl, ACT.Sqrt).then_inc(*root_ready.up())

            @block.tensor
            def _(pe):
                pe.wait_ge(*loaded.at(64))
                for j in range(4):
                    pe.wait_ge(*conv_ready.at(j + 1))
                    nc.tensor.matmul(self.bank(2 * j), Wr[:, j, :], xc[:, j, :], start=True, stop=True)
                    nc.tensor.matmul(self.bank(2 * j + 1), Wi[:, j, :], xc[:, j, :], start=True, stop=True).then_inc(*mms.up())
                pe.wait_ge(*sq_ready.at(1))
                for t in range(TT):
                    for j in range(4):
                        mm = nc.tensor.matmul(PS[:, t:t + 1], th[:, j, t * P:(t + 1) * P], ones, start=j == 0, stop=j == 3)
                mm.then_inc(*sum_mm.up())
        self.close()

    def stage_attention(self, YT, ra):
        nc, ap, PS = self.nc, self.ap, self.PS
        q, k = self.ft(L2Q, 4), self.ft(L2K, 2)
        V = self.area(TOK0, TT, P)
        HG, NU = QH // 2, 2 * TT
        S = [self.area(14336 + 1024 * i, HG, 256) for i in range(2)]
        PT = [self.area(16384 + 1024 * i, HG * 256) for i in range(2)]
        MA, snk = self.area(18432, 256), self.area(18688, QH)
        mx, dn = ([self.area(o + HG * i, HG) for i in range(2)] for o in (18696, 18704))
        O, SQ = self.area(18944, TT, 512), self.area(12288, TT, 512)
        loaded, step, mms, p_in, p_out, turned, pt_ready, o_mm, o_ready, var_ready, root_ready, y_mm, y_ready = (self.sig(n) for n in (
            "mixer_tables_loaded", "dve_steps", "score_products", "softmax_centred", "softmax_exped", "probabilities_turned", "probabilities_ready",
            "chunk_output_products", "chunk_output_ready", "variance_ready", "root_ready", "attention_turned", "attention_feature_ready"))
        slot = lambda h: 2 * (h % 2) + h // 2
        w0 = lambda u: P if u < 2 else 0
        sc = lambda u: PS[:, 1024 * (u % 3):1024 * (u % 3) + 1024]
        turned_at = 3 * 1024
        with nc.Block() as block:
            @block.sync
            def _(sp):
                sp.dma_start(MA, ap["window"]).then_inc(*loaded.up(16))
                sp.dma_start(snk, ap["rows"][13, 0:QH].partition_broadcast(P)).then_inc(*loaded.up(16))

            @block.tensor
            def _(pe):
                def scores(u):
                    n, g = divmod(u, 2)
                    if u >= 3:
                        pe.wait_ge(*o_ready.at(u - 2))
                    for h in range(HG):
                        rr, tile = slice((h % 2) * HD, (h % 2) * HD + HD), 2 * g + h // 2
                        mm = nc.tensor.matmul(sc(u)[:, slot(h) * 256 + w0(u):(slot(h) + 1) * 256], q[rr, tile * SEQ + n * P:tile * SEQ + (n + 1) * P],
                                              k[rr, g * SEQ + (n - 1) * P + w0(u):g * SEQ + (n + 1) * P], start=True, stop=True)
                    mm.then_inc(*mms.up())

                scores(0)
                scores(1)
                for u in range(NU):
                    n, g = divmod(u, 2)
                    pe.wait_ge(*p_out.at(2 * u + 1))
                    if u > 0:
                        pe.wait_ge(*pt_ready.at(u))
                    for h in range(HG):
                        for b in range(w0(u) // P, 2):
                            o = turned_at + (2 * h + b) * P
                            mm = nc.tensor.transpose(PS[:, o:o + P], S[u % 2][:, slot(h), b * P:(b + 1) * P], self.cf("ident"))
                    mm.then_inc(*turned.up())
                    if u + 2 < NU:
                        scores(u + 2)
                    pe.wait_ge(*pt_ready.at(u + 1))
                    for h in range(HG):
                        for b in range(w0(u) // P, 2):
                            mm = nc.tensor.matmul(sc(u)[:, slot(h) * HD:(slot(h) + 1) * HD], PT[u % 2][:, (2 * h + b) * P:(2 * h + b + 1) * P],
                                                  V[:, n - 1 + b, g * HD:(g + 1) * HD], start=b == w0(u) // P, stop=b == 1)
                    mm.then_inc(*o_mm.up())
                pe.wait_ge(*o_ready.at(NU))
                for j in range(4):
                    for t in range(TT):
                        mm = nc.tensor.transpose(PS[:, 2048 + j * HALF + t * P:2048 + j * HALF + (t + 1) * P], O[:, t, j * P:(j + 1) * P], self.cf("ident"))
                    mm.then_inc(*y_mm.up())

            @block.scalar
            def _(act):
                for u in range(NU):
                    act.wait_ge(*p_in.at(u + 1))
                    x = S[u % 2][:, :, w0(u):256]
                    nc.scalar.activation(x, x, ACT.Exp).then_inc(*p_out.up())
                    nc.scalar.activation(mx[u % 2], mx[u % 2], ACT.Exp).then_inc(*p_out.up())
                    act.wait_ge(*turned.at(u + 1))
                    if u >= 2:
                        act.wait_ge(*o_mm.at(u - 1))
                    v = lambda x: x.rearrange("p (h w) -> p h w", w=256)[:, :, w0(u):256]
                    nc.scalar.activation(v(PT[u % 2]), v(PS[:, turned_at:turned_at + 1024]), ACT.Copy).then_inc(*pt_ready.up())
                for j in range(4):
                    act.wait_ge(*y_mm.at(j + 1))
                    nc.scalar.activation(YT[:, 4 + j, :], self.bank(4 + j), ACT.Copy, scale=self.PAR[:, G_OUT + 4 + j:G_OUT + 5 + j]).then_inc(*y_ready.up())
                act.wait_ge(*var_ready.at(1))
                nc.scalar.activation(ra, ra, ACT.Sqrt).then_inc(*root_ready.up())

            @block.vector
            def _(dve):
                s = Steps(dve, step)
                dve.wait_ge(*loaded.at(32))
                v = lambda x: x.rearrange("p (r q) -> p r q", r=2)
                sv = lambda u: snk[:, u % 2 * HG:(u % 2 + 1) * HG].rearrange("p (q r) -> p r q", r=2)

                def centre(u):
                    x, m, w = S[u % 2][:, :, w0(u):256], mx[u % 2], 256 - w0(u)
                    dve.wait_ge(*mms.at(u + 1))
                    if u >= 2:
                        dve.wait_ge(*turned.at(u - 1))
                    s.link(nc.vector.scalar_tensor_tensor(x, sc(u).rearrange("p (h w) -> p h w", w=256)[:, :, w0(u):256], HD ** -0.5,
                                                          MA[:, w0(u):256].unsqueeze(1).broadcast_to([P, HG, w]), ALU.mult, ALU.add))
                    s.link(nc.vector.tensor_reduce(m, x, AX.X, ALU.max))
                    s.link(nc.vector.tensor_tensor(v(m), v(m), sv(u), ALU.max))
                    s.link(nc.vector.tensor_tensor(x, x, m.unsqueeze(2).broadcast_to([P, HG, w]), ALU.subtract))
                    nc.vector.tensor_tensor(v(m), sv(u), v(m), ALU.subtract).then_inc(*p_in.up())

                def normalise(u):
                    n, g = divmod(u, 2)
                    m, d = mx[u % 2], dn[u % 2]
                    dve.wait_ge(*p_out.at(2 * u + 2))
                    s.link(nc.vector.tensor_reduce(d, S[u % 2][:, :, w0(u):256], AX.X, ALU.add))
                    s.link(nc.vector.tensor_tensor(d, d, m, ALU.add))
                    s.link(nc.vector.reciprocal(d, d))
                    dve.wait_ge(*o_mm.at(u + 1))
                    o3 = O[:, n, g * HG * HD:(g + 1) * HG * HD].rearrange("p (q r e) -> p r q e", r=2, e=HD)
                    src = sc(u)[:, 0:HG * HD].rearrange("p (r q e) -> p r q e", r=2, e=HD)
                    for r in range(2):
                        ins = nc.vector.tensor_tensor(o3[:, r], src[:, r], v(d)[:, r].unsqueeze(2).broadcast_to([P, 2, HD]), ALU.mult)
                        if r == 0:
                            s(ins)
                    ins.then_inc(*o_ready.up())

                centre(0)
                for u in range(NU):
                    if u + 1 < NU:
                        centre(u + 1)
                    normalise(u)
                dve.wait_ge(*o_ready.at(NU))
                self.root_mean_square(dve, s, O, SQ, ra.unsqueeze(2), 512, RMS_EPS, var_ready, root_ready)
        self.close()

    def out_two(self, w, rl, ra):
        nc = self.nc

        def copy_out(engine, u, t, b):
            y, n = self.H[:, t, u[1]:u[1] + u[3]], u[3]
            step = self.sig("dve_steps")
            nc.vector.tensor_scalar(y, self.bank(b, n), rl[:, t:t + 1], None, ALU.mult).then_inc(*step.up())
            nc.vector.wait_ge(*step.at(step.sent))
            return nc.vector.scalar_tensor_tensor(y, self.bank(b)[:, n:2 * n], ra[:, t:t + 1], y, ALU.mult, ALU.add)
        self.stage_stream(w, OUT_PIECES, OUT_UNITS, FT0, copy_out, parts=2, engines=1)

    def stage_split(self, x, ahead):
        nc, XR = self.nc, self.XR
        rounded, rest = self.sig("x_rounded"), self.sig("x_rest_ready")
        with nc.Block() as block:
            @block.sync
            def _(sp):
                ahead(sp)

            @block.scalar
            def _(act):
                for k in range(DT):
                    nc.scalar.activation(XR[:, 0, k, :], x[:, k, :], ACT.Copy).then_inc(*rounded.up())

            @block.vector
            def _(dve):
                for k in range(DT):
                    dve.wait_ge(*rounded.at(k + 1))
                    nc.vector.tensor_tensor(XR[:, 1, k, :], x[:, k, :], XR[:, 0, k, :].bitcast(F32), ALU.subtract).then_inc(*rest.up())
        self.close()

    def block_two(self):
        ap, H, HT = self.ap, self.H, self.HT
        self.X2 = self.B[:, 0:TT * D].rearrange("p (t d) -> p t d", d=D)
        col = lambda base: (lambda k: self.PAR[:, base + k:base + k + 1])
        rows = ap["rows"]
        YT = self.area(TOK0 + 512, DT, SEQ)
        rl, ra = self.SM[:, 72:76], self.SM[:, 76:80]

        def feed_forward(pre, w_gu, w_down, row):
            gu = w_gu.rearrange("d (u e f) -> u e d f", u=2, f=FPASS)
            dw = w_down.rearrange("(e f) d -> e f d", f=FPASS)
            self.stage_to_feature(H, None, scale=col(pre), src_factor=0.0, split=self.XR, ahead=self.first_units(gu[0][0], gu[1][0]))
            self.stage_ffn(2, lambda i: gu[0][i], lambda i: gu[1][i], lambda i: dw[i])
            self.stage_post_norm(rows[row], 0.5, last=row == 12)

        self.stage_begin_two()
        self.stage_pre_norm()
        feed_forward(PRE1, ap["ffn1_w_gu_2"][0], ap["ffn1_w_down_2"][0], 10)
        self.stage_to_feature(H, None, scale=col(PRE_MIX), split=self.XR, ahead=self.first_pieces(ap["w_in_2"][0], IN2_PIECES, HT0))
        self.project(ap["w_in_2"][0], IN2_PIECES, IN2_UNITS, None, self.ft, lambda c, n: self.area(TOK0, TT, P)[:, :, c:c + n])
        self.stage_lru(YT, rl)
        self.stage_attention(YT, ra)
        self.stage_split(YT, ahead=self.first_pieces(ap["w_o_2"][0], OUT_PIECES, FT0))
        self.out_two(ap["w_o_2"][0], rl, ra)
        self.stage_post_norm(rows[11], 1.0)
        feed_forward(PRE2, ap["ffn2_w_gu_2"][0], ap["ffn2_w_down_2"][0], 12)


def shape_constants():
    ar = np.arange(P)
    j, i = ar[:, None], ar[None, :]
    cf = np.zeros((P, NCF), np.float32)
    put = lambda name, v: cf.__setitem__((slice(None), slice(CF[name][0], CF[name][0] + CF[name][1])), v)
    put("ident", np.eye(P))
    for t in range(2):
        for h in range(NHEAD):
            cf[:, CF["headcol"][0] + 4 * t + h] = (ar // HD + 2 * t) == h
    cf[:, CF["invf"][0]] = np.float32(10000.0) ** (-(ar % 32).astype(np.float32) / np.float32(32))
    put("iota8", np.broadcast_to(np.arange(8), (P, 8)))
    put("tail", (ar >= 2 * P - CAP)[:, None])
    ci = np.zeros((P, NCI, P), np.int32)
    for l in range(LEVELS):
        s = 1 << l
        m = (j // (2 * s) == i // (2 * s)) & (j % (2 * s) < s) & (i % (2 * s) >= s)
        ci[:, LVT + l], ci[:, LV + l] = m, m.T
    ci[:, DIAG], ci[:, INCL], ci[:, STRICT] = i == j, j <= i, j < i
    cg = np.zeros((P, 512), np.float32)
    for m in range(P):
        if m % HD < 32:
            cg[m + 32, m] = -1.0
        else:
            cg[m - 32, m] = 1.0
    cg[:, P:2 * P] = (j // HD) == (i // HD)
    cg[:, 2 * P:] = (j // 32) == (np.arange(256)[None, :] // HD)
    rc = np.zeros((P, NRET), np.float64)
    lg = np.log(1.0 - 2.0 ** (-5.0 - np.arange(NHEAD)))
    for h in range(NHEAD):
        rc[:, RET_D + h * P:RET_D + (h + 1) * P] = np.where(j <= i, np.exp(np.minimum((i - j), P) * lg[h] * (j <= i)), 0.0)
    for t in range(2):
        g = lg[ar // HD + 2 * t][:, None]
        rc[:, RET_Q + t * P:RET_Q + (t + 1) * P] = np.exp((i + 1) * g)
        rc[:, RET_K + t * P:RET_K + (t + 1) * P] = np.exp((P - 1 - i) * g)
        rc[:, RET_C + t:RET_C + t + 1] = np.exp(P * g)
    kj, qi = np.arange(256)[None, :], j
    window = np.where((qi + P - kj >= 0) & (qi + P - kj < P), 0.0, -1e30).astype(np.float32)
    return {"window": window, "slot_iota": np.arange(CAP, dtype=np.float32), "const_f": cf, "const_i": ci.reshape(P, NCI * P), "const_g": cg, "ret_c": rc.astype(np.float32)}


def columns(v, n):
    v = np.asarray(v, np.float32).reshape(-1)
    out = np.zeros(n * P, np.float32)
    out[:v.size] = v
    return out.reshape(n, P).T


def packed(inputs):
    g = lambda n: np.asarray(inputs[n])
    par = []
    for l in range(2):
        src = {"lb0": g("hgrn_lb_logits")[0], "lb1": g("hgrn_lb_logits")[1], "gate_b": g("gla_gate_b")[l], "mu": g("rwkv_mu")[l],
               "w0": g("rwkv_w0")[l], "a0": g("rwkv_a0")[l], "k_k": g("rwkv_k_k")[l], "k_a": g("rwkv_k_a")[l],
               "r_k": g("rwkv_r_k")[l], "v0": g("rwkv_v0")[0]}
        par += [columns(src[n], PAR[n][1]) for n in PAR]
    rows = []
    for l in range(2):
        rows += [g("ln1_g")[l], g("ln1_b")[l], g("ln2_g")[l], g("ln2_b")[l],
                 np.concatenate([np.tile(g("hgrn_norm_g")[l], NHEAD), np.tile(g("gla_norm_g")[l], NHEAD), g("rwkv_lnx_g")[l], g("rwkv_lnx_b")[l]])]
    rows += [g("ffn1_post_g_2")[0], g("mix_post_g_2")[0], g("ffn2_post_g_2")[0], np.tile(g("sinks_2")[0], P)]
    par2 = [columns(g(n)[0], 8) for n in ("ffn1_pre_g_2", "mix_pre_g_2", "ffn2_pre_g_2")]
    par2.append(columns(np.concatenate([g("g_lru_out_2")[0], g("g_attn_out_2")[0]]), 8))
    par2 += [columns(g("conv_w_2")[0, i], 4) for i in range(4)]
    par2 += [columns(g(n)[0], 4) for n in ("conv_b_2", "b_rg_2", "b_ig_2", "lru_lambda_2")]
    return {"par": np.concatenate(par, 1), "rows": np.stack(rows), "par2": np.concatenate(par2, 1)}


BIG = ["x", "positions", "w_in", "w_out", "gla_gate_w2", "rwkv_w2", "rwkv_a2", "rwkv_g2", "rwkv_v1", "rwkv_v2",
       "ffn_w_gate", "ffn_w_up", "ffn_w_down", "moe_router", "moe_w_gate", "moe_w_up", "moe_w_down",
       "ffn1_w_gu_2", "ffn1_w_down_2", "w_in_2", "w_rg_2", "w_ig_2", "w_o_2", "ffn2_w_gu_2", "ffn2_w_down_2"]


def laid_out(inputs):
    arrays = {n: np.ascontiguousarray(inputs[n]) for n in BIG}
    arrays.update({n: np.ascontiguousarray(a) for n, a in {**shape_constants(), **packed(inputs)}.items()})
    return arrays


def build(nc, ap):
    k = Kernel(nc, ap)
    k.block_one()
    k.block_two()


def kernel(**inputs):
    import concourse.bacc as bacc
    from concourse.bass_utils import run_bass_kernel_spmd

    nc = bacc.Bacc("TRN2", target_bir_lowering=False, num_devices=1)
    arrays, ap = {}, {}
    for name, a in laid_out(inputs).items():
        arrays[f"in_{name}"] = a
        ap[name] = nc.dram_tensor(f"in_{name}", a.shape, mybir.dt.from_np(a.dtype), kind="ExternalInput").ap()
    ap["out"] = nc.dram_tensor("out_0", (1, SEQ, D), F32, kind="ExternalOutput").ap()
    build(nc, ap)
    r = run_bass_kernel_spmd(nc, [arrays], core_ids=[0])
    return r.results[0]["out_0"]
```
